# Optimizing a Trainium2 kernel written in Bass

```python
import jax, jax.numpy as jnp
from jax import lax
import numpy as np
import math

D_MODEL = 1024
BATCH = 1
SEQ = 512
DEPTH = 1

NSA_HEADS = 8
NSA_KV_HEADS = 2
NSA_HEAD_DIM = 64
NSA_GROUP = NSA_HEADS // NSA_KV_HEADS
NSA_WIDTH = NSA_HEADS * NSA_HEAD_DIM
CMP_BLOCK = 32
CMP_STRIDE = 16
SLC_BLOCK = 64
SLC_TOPK = 16
WINDOW = 512
Q_BLOCK = 128
FORCE_SCORE = 1e4
NEG_INF = -1e30
RWKV_HEADS = 8
RWKV_HEAD_DIM = 64
RWKV_WIDTH = RWKV_HEADS * RWKV_HEAD_DIM
DECAY_RANK = 64
ICLR_RANK = 64
VRES_RANK = 32
GATE_RANK = 128
LNX_EPS = 1e-5 * RWKV_HEAD_DIM
D_FF = 2816
CONV_WIDTH = 3
EPS = 1e-6
NSA_Q_COLS = NSA_WIDTH
NSA_KV_COLS = NSA_KV_HEADS * NSA_HEAD_DIM
NSA_GATE_COLS = NSA_HEADS * 3
RWKV_SPLITS = (RWKV_WIDTH, RWKV_WIDTH, RWKV_WIDTH, DECAY_RANK, ICLR_RANK, GATE_RANK)
RWKV_COLS = sum(RWKV_SPLITS)
MERGE_COLS = 2 * D_MODEL
IN_SPLITS = (NSA_Q_COLS, NSA_KV_COLS, NSA_KV_COLS, NSA_KV_COLS, NSA_KV_COLS, NSA_KV_COLS, NSA_KV_COLS, NSA_GATE_COLS, RWKV_COLS, MERGE_COLS)
IN_COLS = sum(IN_SPLITS)


def _split(z, sizes):
    return jnp.split(z, np.cumsum(sizes)[:-1].tolist(), axis=-1)

def _rms_norm(x, g):
    x32 = x.astype(jnp.float32)
    y = x32 * lax.rsqrt(jnp.mean(x32 * x32, axis=-1, keepdims=True) + EPS)
    return (y * g.astype(jnp.float32)).astype(x.dtype)

def _masked_softmax(s, mask):
    p = jax.nn.softmax(jnp.where(mask, s.astype(jnp.float32), NEG_INF), axis=-1) * mask
    return p.astype(s.dtype)

def _nsa(q, kc, vc, ks, vs, kw, vw, gate_logits, qk_gain, cmp_pe, cmp_w1, cmp_w2):
    B, S, _ = q.shape
    dt = q.dtype
    G, HG, Dh = NSA_KV_HEADS, NSA_GROUP, NSA_HEAD_DIM
    scale = Dh ** -0.5
    qh = _rms_norm(q.reshape(B, S, G, HG, Dh), qk_gain[0]).transpose(0, 2, 3, 1, 4)

    nc = (S - CMP_BLOCK) // CMP_STRIDE + 1
    tok = np.arange(nc)[:, None] * CMP_STRIDE + np.arange(CMP_BLOCK)[None, :]

    def compress(z, pe, w1, w2):
        blocks = z.reshape(B, S, G, Dh)[:, tok] + pe[None, None, :, None, :]
        hid = jax.nn.silu(jnp.einsum('bnlgd,lde->bnge', blocks, w1))
        return jnp.einsum('bnge,ef->bgnf', hid, w2)

    k_cmp = _rms_norm(compress(kc, cmp_pe[0], cmp_w1[0], cmp_w2[0]), qk_gain[1])
    v_cmp = compress(vc, cmp_pe[1], cmp_w1[1], cmp_w2[1])
    cmp_end = jnp.arange(nc) * CMP_STRIDE + CMP_BLOCK - 1

    ns = S // SLC_BLOCK
    n_sel = min(SLC_TOPK, ns)
    k_slc = _rms_norm(ks.reshape(B, S, G, Dh), qk_gain[2]).transpose(0, 2, 1, 3).reshape(B, G, ns, SLC_BLOCK, Dh)
    v_slc = vs.reshape(B, S, G, Dh).transpose(0, 2, 1, 3).reshape(B, G, ns, SLC_BLOCK, Dh)
    n_idx = jnp.arange(nc)[:, None]
    s_idx = jnp.arange(ns)
    overlap = ((n_idx * CMP_STRIDE < (s_idx[None, :] + 1) * SLC_BLOCK)
               & (n_idx * CMP_STRIDE + CMP_BLOCK > s_idx[None, :] * SLC_BLOCK)).astype(jnp.float32)

    pad = ((0, 0), (0, 0), (WINDOW, 0), (0, 0))
    k_win = jnp.pad(_rms_norm(kw.reshape(B, S, G, Dh), qk_gain[3]).transpose(0, 2, 1, 3), pad)
    v_win = jnp.pad(vw.reshape(B, S, G, Dh).transpose(0, 2, 1, 3), pad)

    gates = jax.nn.sigmoid(gate_logits.astype(jnp.float32)).astype(dt)
    gates = gates.reshape(B, S, G, HG, 3).transpose(0, 2, 3, 1, 4)
    bi = jnp.arange(B)[:, None, None, None]
    gi = jnp.arange(G)[None, :, None, None]

    def block(c):
        t0 = c * Q_BLOCK
        t = t0 + jnp.arange(Q_BLOCK)
        qb = lax.dynamic_slice_in_dim(qh, t0, Q_BLOCK, axis=3)
        gb = lax.dynamic_slice_in_dim(gates, t0, Q_BLOCK, axis=3)
        s = jnp.einsum('bghtd,bgnd->bghtn', qb, k_cmp) * scale
        p_cmp = _masked_softmax(s, cmp_end[None, :] <= t[:, None])
        o_cmp = jnp.einsum('bghtn,bgnd->bghtd', p_cmp, v_cmp)
        imp = jnp.einsum('bghtn,ns->bgts', p_cmp.astype(jnp.float32), overlap)
        cur = t // SLC_BLOCK
        forced = (s_idx[None, :] == 0) | (s_idx[None, :] == cur[:, None]) | (s_idx[None, :] == cur[:, None] - 1)
        imp = jnp.where(forced, FORCE_SCORE, imp)
        imp = jnp.where(s_idx[None, :] > cur[:, None], -1.0, imp)
        _, sel = lax.top_k(imp, n_sel)
        k_sel = k_slc[bi, gi, sel].reshape(B, G, Q_BLOCK, n_sel * SLC_BLOCK, Dh)
        v_sel = v_slc[bi, gi, sel].reshape(B, G, Q_BLOCK, n_sel * SLC_BLOCK, Dh)
        pos = (sel[..., None] * SLC_BLOCK + jnp.arange(SLC_BLOCK)).reshape(B, G, Q_BLOCK, n_sel * SLC_BLOCK)
        s = jnp.einsum('bghtd,bgtkd->bghtk', qb, k_sel) * scale
        p_slc = _masked_softmax(s, pos[:, :, None] <= t[:, None])
        o_slc = jnp.einsum('bghtk,bgtkd->bghtd', p_slc, v_sel)
        k_w = lax.dynamic_slice_in_dim(k_win, t0, WINDOW + Q_BLOCK, axis=2)
        v_w = lax.dynamic_slice_in_dim(v_win, t0, WINDOW + Q_BLOCK, axis=2)
        kpos = t0 - WINDOW + jnp.arange(WINDOW + Q_BLOCK)
        dist = t[:, None] - kpos[None, :]
        s = jnp.einsum('bghtd,bgkd->bghtk', qb, k_w) * scale
        p_win = _masked_softmax(s, (kpos[None, :] >= 0) & (dist >= 0) & (dist < WINDOW))
        o_win = jnp.einsum('bghtk,bgkd->bghtd', p_win, v_w)
        return gb[..., 0:1] * o_cmp + gb[..., 1:2] * o_slc + gb[..., 2:3] * o_win

    o = lax.map(block, jnp.arange(S // Q_BLOCK))
    return o.transpose(1, 0, 4, 2, 3, 5).reshape(B, S, NSA_WIDTH)

def _wkv7_scan(r, w, k, v, a, b):
    B, S, H, N = r.shape

    def step(state, inp):
        r_t, w_t, k_t, v_t, a_t, b_t = inp
        sa = jnp.einsum('bhvk,bhk->bhv', state, a_t)
        state = state * w_t[:, :, None, :] + sa[..., None] * b_t[:, :, None, :] + v_t[..., None] * k_t[:, :, None, :]
        return state, jnp.einsum('bhvk,bhk->bhv', state, r_t)

    xs = (jnp.swapaxes(r, 0, 1), jnp.swapaxes(w, 0, 1), jnp.swapaxes(k, 0, 1),
          jnp.swapaxes(v, 0, 1), jnp.swapaxes(a, 0, 1), jnp.swapaxes(b, 0, 1))
    _, y = lax.scan(step, jnp.zeros((B, H, N, N), jnp.float32), xs)
    return jnp.swapaxes(y, 0, 1)

def _rwkv7(z, v_first, vres, mu, w0, w_up, a0, a_up, g_up, k_k, k_a, r_k, ln_w, ln_b):
    B, S, _ = z.shape
    dt = z.dtype
    f32 = jnp.float32
    H, N = RWKV_HEADS, RWKV_HEAD_DIM
    z_prev = jnp.pad(z[:, :-1], ((0, 0), (1, 0), (0, 0)))
    z = z + mu * (z_prev - z)
    r, k, v, wd, ad, gd = _split(z, RWKV_SPLITS)
    if vres is None:
        v_first = v
    else:
        v0, v1, v2 = vres
        v = v + (v_first - v) * jax.nn.sigmoid(v0 + (v @ v1) @ v2)
    w = -jax.nn.softplus(-(w0 + jnp.tanh(wd) @ w_up).astype(f32)) - 0.5
    decay = jnp.exp(-jnp.exp(w))
    a = jax.nn.sigmoid((a0 + ad @ a_up).astype(f32))
    g = jax.nn.sigmoid(gd) @ g_up

    def heads(t):
        return t.astype(f32).reshape(B, S, H, N)

    rh, vh, ah, wh = heads(r), heads(v), heads(a), heads(decay)
    kk = heads(k * k_k)
    kk = kk / jnp.maximum(jnp.sqrt(jnp.sum(kk * kk, axis=-1, keepdims=True)), 1e-12)
    kh = heads(k) * (1.0 + (ah - 1.0) * k_a.astype(f32).reshape(H, N))
    y = _wkv7_scan(rh, wh, kh, vh, -kk, kk * ah)
    mean = jnp.mean(y, axis=-1, keepdims=True)
    var = jnp.mean(jnp.square(y - mean), axis=-1, keepdims=True)
    y = (y - mean) * lax.rsqrt(var + LNX_EPS) * ln_w.astype(f32).reshape(H, N) + ln_b.astype(f32).reshape(H, N)
    y = y + jnp.sum(rh * kh * r_k.astype(f32), axis=-1, keepdims=True) * vh
    return y.reshape(B, S, RWKV_WIDTH).astype(dt) * g, v_first

def _conv_ffn(h, w_up, conv_w, w_down):
    u = h @ w_up
    u = lax.conv_general_dilated(u, conv_w[:, None, :], window_strides=(1,),
                                 padding=((CONV_WIDTH - 1, 0),),
                                 dimension_numbers=('NWC', 'WIO', 'NWC'),
                                 feature_group_count=u.shape[-1])
    a, b = jnp.split(u, 2, axis=-1)
    return (jax.nn.silu(a) * b) @ w_down

def first_inputs(seed: int = 0) -> dict:
    key = jax.random.key(seed)
    k = jax.random.split(key, 32)
    L, D, Dh = DEPTH, D_MODEL, NSA_HEAD_DIM
    f32 = jnp.float32

    def nrm(kk, shape, scale):
        return jax.random.normal(kk, shape, f32) * scale

    def gain(kk, shape):
        return 1.0 + 0.1 * jax.random.normal(kk, shape, f32)

    return {
        'x': nrm(k[0], (BATCH, SEQ, D), 1.0),
        'norm_mix': gain(k[1], (L, D)),
        'norm_ffn': gain(k[2], (L, D)),
        'w_in': nrm(k[3], (L, D, IN_COLS), D ** -0.5),
        'qk_gain': gain(k[4], (L, 4, Dh)),
        'cmp_pe': nrm(k[5], (L, 2, CMP_BLOCK, Dh), 0.1),
        'cmp_w1': nrm(k[6], (L, 2, CMP_BLOCK, Dh, Dh), (CMP_BLOCK * Dh) ** -0.5),
        'cmp_w2': nrm(k[7], (L, 2, Dh, Dh), Dh ** -0.5),
        'rwkv_mu': jax.random.uniform(k[8], (L, RWKV_COLS), f32),
        'rwkv_w0': jax.random.uniform(k[9], (L, RWKV_WIDTH), f32, -3.0, 2.0),
        'rwkv_w_up': nrm(k[10], (L, DECAY_RANK, RWKV_WIDTH), 0.1),
        'rwkv_a0': nrm(k[11], (L, RWKV_WIDTH), 0.5),
        'rwkv_a_up': nrm(k[12], (L, ICLR_RANK, RWKV_WIDTH), ICLR_RANK ** -0.5),
        'rwkv_g_up': nrm(k[13], (L, GATE_RANK, RWKV_WIDTH), GATE_RANK ** -0.5),
        'rwkv_k_k': 0.85 + 0.1 * jax.random.normal(k[14], (L, RWKV_WIDTH), f32),
        'rwkv_k_a': gain(k[15], (L, RWKV_WIDTH)),
        'rwkv_r_k': nrm(k[16], (L, RWKV_HEADS, RWKV_HEAD_DIM), 0.1),
        'rwkv_ln_w': gain(k[17], (L, RWKV_WIDTH)),
        'rwkv_ln_b': nrm(k[18], (L, RWKV_WIDTH), 0.02),
        'vres_v0': nrm(k[19], (L - 1, RWKV_WIDTH), 0.5),
        'vres_v1': nrm(k[20], (L - 1, RWKV_WIDTH, VRES_RANK), RWKV_WIDTH ** -0.5),
        'vres_v2': nrm(k[21], (L - 1, VRES_RANK, RWKV_WIDTH), VRES_RANK ** -0.5),
        'proj_nsa': nrm(k[22], (L, NSA_WIDTH, D), NSA_WIDTH ** -0.5),
        'proj_rwkv': nrm(k[23], (L, RWKV_WIDTH, D), RWKV_WIDTH ** -0.5),
        'w_out': nrm(k[24], (L, D, D), D ** -0.5),
        'ffn_up': nrm(k[25], (L, D, 2 * D_FF), D ** -0.5),
        'ffn_conv': nrm(k[26], (L, CONV_WIDTH, 2 * D_FF), CONV_WIDTH ** -0.5),
        'ffn_down': nrm(k[27], (L, D_FF, D), D_FF ** -0.5),
    }

def first_block(x, norm_mix, norm_ffn, w_in, qk_gain, cmp_pe, cmp_w1, cmp_w2, rwkv_mu, rwkv_w0,
              rwkv_w_up, rwkv_a0, rwkv_a_up, rwkv_g_up, rwkv_k_k, rwkv_k_a, rwkv_r_k, rwkv_ln_w,
              rwkv_ln_b, vres_v0, vres_v1, vres_v2, proj_nsa, proj_rwkv, w_out, ffn_up, ffn_conv,
              ffn_down):
    B, S, D = x.shape
    v_first = None
    for l in range(DEPTH):
        h = _rms_norm(x, norm_mix[l])
        u = h @ w_in[l]
        q, kc, vc, ks, vs, kw, vw, nsa_gl, rw, merge = _split(u, IN_SPLITS)
        o_nsa = _nsa(q, kc, vc, ks, vs, kw, vw, nsa_gl, qk_gain[l], cmp_pe[l], cmp_w1[l], cmp_w2[l])
        vres = None if l == 0 else (vres_v0[l - 1], vres_v1[l - 1], vres_v2[l - 1])
        o_rwkv, v_first = _rwkv7(rw, v_first, vres, rwkv_mu[l], rwkv_w0[l], rwkv_w_up[l], rwkv_a0[l],
                                 rwkv_a_up[l], rwkv_g_up[l], rwkv_k_k[l], rwkv_k_a[l], rwkv_r_k[l],
                                 rwkv_ln_w[l], rwkv_ln_b[l])
        gates = jax.nn.sigmoid(merge.astype(jnp.float32)).astype(x.dtype).reshape(B, S, 2, D)
        y = gates[:, :, 0] * (o_nsa @ proj_nsa[l]) + gates[:, :, 1] * (o_rwkv @ proj_rwkv[l])
        x = x + y @ w_out[l]
        x = x + _conv_ffn(_rms_norm(x, norm_ffn[l]), ffn_up[l], ffn_conv[l], ffn_down[l])
    return x


DEPTH_2 = 2

N_MIXERS = 4
N_MOD = 9
GRID_W = 64

POOL_WINDOWS = (2, 4, 8, 16)
N_POOL = len(POOL_WINDOWS)
POOL_GROUP = D_MODEL // N_POOL

DIFF_HEADS = 8
DIFF_HEAD_DIM = D_MODEL // DIFF_HEADS // 2
DIFF_V_DIM = 2 * DIFF_HEAD_DIM
ROPE_THETA = 500000.0
ROT_DIM = DIFF_HEAD_DIM // 4

GQA_HEADS = 8
GQA_KV_HEADS = 2
GQA_HEAD_DIM = D_MODEL // GQA_HEADS
GQA_GROUP = GQA_HEADS // GQA_KV_HEADS
GQA_Q_DIM = GQA_HEADS * GQA_HEAD_DIM
GQA_KV_DIM = GQA_KV_HEADS * GQA_HEAD_DIM
AXIAL_THETA = 10000.0
AXIAL_DIM = GQA_HEAD_DIM // 2


def rms_norm(x, g):
    xf = x.astype(jnp.float32)
    y = xf * lax.rsqrt(jnp.mean(xf * xf, axis=-1, keepdims=True) + EPS)
    return (y * g.astype(jnp.float32)).astype(x.dtype)

def modulate(h, shift, scale):
    return h * (1 + scale) + shift

def swiglu(h, w_gu, w_down):
    g, u = jnp.split(h @ w_gu, 2, axis=-1)
    return (jax.nn.silu(g) * u) @ w_down

def rope_tables(pos, dim, theta):
    inv = 1.0 / (theta ** (jnp.arange(0, dim, 2, dtype=jnp.float32) / dim))
    ang = pos.astype(jnp.float32)[:, None] * inv[None, :]
    return jnp.cos(ang), jnp.sin(ang)

def rope(x, cos, sin):
    half = x.shape[-1] // 2
    xf = x.astype(jnp.float32)
    x1, x2 = xf[..., :half], xf[..., half:]
    c = cos[None, :, None, :]
    s = sin[None, :, None, :]
    return jnp.concatenate([x1 * c - x2 * s, x2 * c + x1 * s], axis=-1).astype(x.dtype)

def sweep_query_blocks(fn, q):
    b, s = q.shape[:2]
    nblk = s // Q_BLOCK
    qb = jnp.moveaxis(q.reshape((b, nblk, Q_BLOCK) + q.shape[2:]), 1, 0)
    out = jnp.moveaxis(lax.map(fn, qb), 0, 1)
    return out.reshape((b, s) + out.shape[3:])

def pool_mixer(h, pool_w, pool_scale):
    b, s, d = h.shape
    cs = jnp.concatenate([jnp.zeros((b, 1, d), jnp.float32),
                          jnp.cumsum(h.astype(jnp.float32), axis=1)], axis=1)
    t = jnp.arange(s)
    diffs = []
    for g, win in enumerate(POOL_WINDOWS):
        lo = jnp.clip(t - win // 2, 0, s)
        hi = jnp.clip(t + win // 2, 0, s)
        csg = cs[..., g * POOL_GROUP:(g + 1) * POOL_GROUP]
        mean = (jnp.take(csg, hi, axis=1) - jnp.take(csg, lo, axis=1)) / (hi - lo).astype(jnp.float32)[None, :, None]
        diffs.append(mean.astype(h.dtype) - h[..., g * POOL_GROUP:(g + 1) * POOL_GROUP])
    dgrp = jnp.stack(diffs, axis=2)
    y = jnp.einsum('bsgc,gce->bsge', dgrp, pool_w).reshape(b, s, d)
    return y * pool_scale

def diff_attention(h, w_qkv, lam, subln_g, w_o, cos, sin, layer_idx):
    b, s, d = h.shape
    q, k, v = jnp.split(h @ w_qkv, 3, axis=-1)
    q = q.reshape(b, s, 2 * DIFF_HEADS, DIFF_HEAD_DIM)
    k = k.reshape(b, s, 2 * DIFF_HEADS, DIFF_HEAD_DIM)
    v = v.reshape(b, s, DIFF_HEADS, DIFF_V_DIM)
    q = jnp.concatenate([rope(q[..., :ROT_DIM], cos, sin), q[..., ROT_DIM:]], axis=-1)
    k = jnp.concatenate([rope(k[..., :ROT_DIM], cos, sin), k[..., ROT_DIM:]], axis=-1)
    q = (q * DIFF_HEAD_DIM ** -0.5).reshape(b, s, DIFF_HEADS, 2, DIFF_HEAD_DIM)
    k = k.reshape(b, s, DIFF_HEADS, 2, DIFF_HEAD_DIM)
    lam_init = 0.8 - 0.6 * math.exp(-0.3 * layer_idx)
    lf = lam.astype(jnp.float32)
    lam_full = jnp.exp(jnp.sum(lf[0] * lf[1])) - jnp.exp(jnp.sum(lf[2] * lf[3])) + lam_init

    def block(qb):
        sc = jnp.einsum('bqhcd,bkhcd->bhcqk', qb, k, preferred_element_type=jnp.float32)
        p = jax.nn.softmax(sc, axis=-1)
        a = p[:, :, 0] - lam_full * p[:, :, 1]
        return jnp.einsum('bhqk,bkhe->bqhe', a.astype(v.dtype), v)

    o = sweep_query_blocks(block, q)
    o = rms_norm(o, subln_g) * (1 - lam_init)
    return o.reshape(b, s, d) @ w_o

def gqa_axial_attention(h, w_qkv, q_norm_g, k_norm_g, w_o, cos_r, sin_r, cos_c, sin_c):
    b, s, d = h.shape
    qkv = h @ w_qkv
    q = qkv[..., :GQA_Q_DIM].reshape(b, s, GQA_HEADS, GQA_HEAD_DIM)
    k = qkv[..., GQA_Q_DIM:GQA_Q_DIM + GQA_KV_DIM].reshape(b, s, GQA_KV_HEADS, GQA_HEAD_DIM)
    v = qkv[..., GQA_Q_DIM + GQA_KV_DIM:].reshape(b, s, GQA_KV_HEADS, GQA_HEAD_DIM)
    q = rms_norm(q, q_norm_g)
    k = rms_norm(k, k_norm_g)

    def axial(t):
        return jnp.concatenate([rope(t[..., :AXIAL_DIM], cos_r, sin_r),
                                rope(t[..., AXIAL_DIM:], cos_c, sin_c)], axis=-1)

    q = (axial(q) * GQA_HEAD_DIM ** -0.5).reshape(b, s, GQA_KV_HEADS, GQA_GROUP, GQA_HEAD_DIM)
    k = axial(k)

    def block(qb):
        sc = jnp.einsum('bqgrd,bkgd->bgrqk', qb, k, preferred_element_type=jnp.float32)
        p = jax.nn.softmax(sc, axis=-1)
        return jnp.einsum('bgrqk,bkgd->bqgrd', p.astype(v.dtype), v)

    o = sweep_query_blocks(block, q)
    return o.reshape(b, s, d) @ w_o

def short_conv_mixer(h, w_in, w_conv, w_out):
    d = h.shape[-1]
    gb, gc, u = jnp.split(h @ w_in, 3, axis=-1)
    z = gc * u
    zc = lax.conv_general_dilated(z, w_conv[:, None, :], window_strides=(1,),
                                  padding=[((CONV_WIDTH - 1) // 2, (CONV_WIDTH - 1) // 2)],
                                  dimension_numbers=('NWC', 'WIO', 'NWC'),
                                  feature_group_count=d)
    return (gb * zc) @ w_out

def second_inputs(seed: int = 0) -> dict:
    key = jax.random.key(seed)
    ks = jax.random.split(key, 24)

    def nrm(k, shape, scale):
        return jax.random.normal(k, shape, jnp.float32) * scale

    D = D_MODEL
    return {
        "x": nrm(ks[0], (BATCH, SEQ, D), 1.0),
        "c": nrm(ks[1], (BATCH, D), 1.0),
        "mod_w": nrm(ks[2], (DEPTH_2, D, N_MOD * D), 0.5 * D ** -0.5),
        "mod_b": nrm(ks[3], (DEPTH_2, N_MOD * D), 0.02),
        "norm_g": 1.0 + nrm(ks[4], (DEPTH_2, 3, D), 0.1),
        "ffn_w_gu": nrm(ks[5], (DEPTH_2, 2, D, 2 * D_FF), D ** -0.5),
        "ffn_w_down": nrm(ks[6], (DEPTH_2, 2, D_FF, D), D_FF ** -0.5),
        "pool_w": nrm(ks[7], (N_POOL, POOL_GROUP, POOL_GROUP), POOL_GROUP ** -0.5),
        "pool_scale": 1.0 + nrm(ks[8], (D,), 0.1),
        "diff_w_qkv": nrm(ks[9], (D, 3 * D), D ** -0.5),
        "diff_lambda": nrm(ks[10], (4, DIFF_HEAD_DIM), 0.1),
        "diff_subln_g": 1.0 + nrm(ks[11], (DIFF_V_DIM,), 0.1),
        "diff_w_o": nrm(ks[12], (D, D), D ** -0.5),
        "gqa_w_qkv": nrm(ks[13], (D, GQA_Q_DIM + 2 * GQA_KV_DIM), D ** -0.5),
        "gqa_q_norm_g": 1.0 + nrm(ks[14], (GQA_HEAD_DIM,), 0.1),
        "gqa_k_norm_g": 1.0 + nrm(ks[15], (GQA_HEAD_DIM,), 0.1),
        "gqa_w_o": nrm(ks[16], (D, D), D ** -0.5),
        "conv_w_in": nrm(ks[17], (D, 3 * D), D ** -0.5),
        "conv_w": nrm(ks[18], (CONV_WIDTH, D), CONV_WIDTH ** -0.5),
        "conv_w_out": nrm(ks[19], (D, D), D ** -0.5),
        "final_g": 1.0 + nrm(ks[20], (D,), 0.1),
    }

def second_block(x, c, mod_w, mod_b, norm_g, ffn_w_gu, ffn_w_down, pool_w, pool_scale,
              diff_w_qkv, diff_lambda, diff_subln_g, diff_w_o,
              gqa_w_qkv, gqa_q_norm_g, gqa_k_norm_g, gqa_w_o,
              conv_w_in, conv_w, conv_w_out, final_g):
    s = x.shape[1]
    t = jnp.arange(s)
    cos1, sin1 = rope_tables(t, ROT_DIM, ROPE_THETA)
    rows = s // GRID_W
    row_pos = jnp.broadcast_to(jnp.arange(rows)[:, None], (rows, GRID_W)).reshape(-1)
    col_pos = jnp.broadcast_to(jnp.arange(GRID_W)[None, :], (rows, GRID_W)).reshape(-1)
    cos_r, sin_r = rope_tables(row_pos, AXIAL_DIM, AXIAL_THETA)
    cos_c, sin_c = rope_tables(col_pos, AXIAL_DIM, AXIAL_THETA)

    c_act = jax.nn.silu(c)
    for i in range(DEPTH_2):
        mod = (c_act @ mod_w[i] + mod_b[i])[:, None, :]
        sh0, sc0, g0, sh1, sc1, g1, sh2, sc2, g2 = jnp.split(mod, N_MOD, axis=-1)

        h = modulate(rms_norm(x, norm_g[i, 0]), sh0, sc0)
        x = x + 0.5 * g0 * swiglu(h, ffn_w_gu[i, 0], ffn_w_down[i, 0])

        h = modulate(rms_norm(x, norm_g[i, 1]), sh1, sc1)
        kind = i % N_MIXERS
        if kind == 0:
            y = pool_mixer(h, pool_w, pool_scale)
        elif kind == 1:
            y = diff_attention(h, diff_w_qkv, diff_lambda, diff_subln_g, diff_w_o, cos1, sin1, i)
        elif kind == 2:
            y = gqa_axial_attention(h, gqa_w_qkv, gqa_q_norm_g, gqa_k_norm_g, gqa_w_o,
                                    cos_r, sin_r, cos_c, sin_c)
        else:
            y = short_conv_mixer(h, conv_w_in, conv_w, conv_w_out)
        x = x + g1 * y

        h = modulate(rms_norm(x, norm_g[i, 2]), sh2, sc2)
        x = x + 0.5 * g2 * swiglu(h, ffn_w_gu[i, 1], ffn_w_down[i, 1])

    return rms_norm(x, final_g)


def setup_inputs(seed=0):
    out = dict(first_inputs(seed))
    for name, value in second_inputs(seed + 1).items():
        if name != "x":
            out[name + "_2"] = value
    return out


def reference(
    x, norm_mix, norm_ffn, w_in, qk_gain, cmp_pe, cmp_w1, cmp_w2, rwkv_mu, rwkv_w0, rwkv_w_up,
    rwkv_a0, rwkv_a_up, rwkv_g_up, rwkv_k_k, rwkv_k_a, rwkv_r_k, rwkv_ln_w, rwkv_ln_b, vres_v0,
    vres_v1, vres_v2, proj_nsa, proj_rwkv, w_out, ffn_up, ffn_conv, ffn_down, c_2, mod_w_2,
    mod_b_2, norm_g_2, ffn_w_gu_2, ffn_w_down_2, pool_w_2, pool_scale_2, diff_w_qkv_2,
    diff_lambda_2, diff_subln_g_2, diff_w_o_2, gqa_w_qkv_2, gqa_q_norm_g_2, gqa_k_norm_g_2,
    gqa_w_o_2, conv_w_in_2, conv_w_2, conv_w_out_2, final_g_2,
):
    x = first_block(
        x, norm_mix, norm_ffn, w_in, qk_gain, cmp_pe, cmp_w1, cmp_w2, rwkv_mu, rwkv_w0,
        rwkv_w_up, rwkv_a0, rwkv_a_up, rwkv_g_up, rwkv_k_k, rwkv_k_a, rwkv_r_k, rwkv_ln_w,
        rwkv_ln_b, vres_v0, vres_v1, vres_v2, proj_nsa, proj_rwkv, w_out, ffn_up, ffn_conv,
        ffn_down,
    )
    return second_block(
        x, c_2, mod_w_2, mod_b_2, norm_g_2, ffn_w_gu_2, ffn_w_down_2, pool_w_2, pool_scale_2,
        diff_w_qkv_2, diff_lambda_2, diff_subln_g_2, diff_w_o_2, gqa_w_qkv_2, gqa_q_norm_g_2,
        gqa_k_norm_g_2, gqa_w_o_2, conv_w_in_2, conv_w_2, conv_w_out_2, final_g_2,
    )


_drawn_inputs = setup_inputs


def setup_inputs(seed=0):
    import zlib

    import numpy as np

    out = dict(_drawn_inputs(seed))
    spreads = {}
    factors = {'qk_gain': 5.349,
     'cmp_pe': 4.624,
     'rwkv_k_k': 5.445,
     'rwkv_ln_b': 8.0,
     'diff_lambda_2': 3.183,
     'diff_subln_g_2': 3.251}
    for name, (base, spread) in spreads.items():
        noise = np.random.default_rng([zlib.crc32(name.encode()), seed]).standard_normal(out[name].shape)
        drawn = base * np.exp(spread * noise) if base else spread * noise
        out[name] = __import__('jax').numpy.asarray(drawn.astype(out[name].dtype))
    for name, factor in factors.items():
        out[name] = (out[name] * factor).astype(out[name].dtype)
    return out
```

```python
from contextlib import ExitStack

import numpy as np

import concourse.bass as bass
from concourse import mybir

F32 = mybir.dt.float32
F32R = mybir.dt.float32r
I32 = mybir.dt.int32
ALU = mybir.AluOpType
ACT = mybir.ActivationFunctionType
AX = mybir.AxisListType

P = 128
S = 512
TT = S // P
D = 1024
KD = D // P
FF = 2816
KF = FF // P
DOWN = [(0, 8), (8, 7), (15, 7)]
SLOT = KD * P
NSTAGE = 4
EPS = 1e-6
N_MOD_GROUPS = 36
MOD_GROUPS_LAYER = 18
HD = 64
DIFF_HEADS = 8
NEG = -1e30
DECAY = float(np.exp(-0.5))
NSA_HEADS, NSA_GROUPS = 8, 2
CMP_BLOCK, CMP_STRIDE = 32, 16
NC = (S - CMP_BLOCK) // CMP_STRIDE + 1
CHUNK = 64
NCH = S // CHUNK
PAIRS = 4
LNX_EPS = 1e-5 * HD
LAM_INIT = 0.8 - 0.6 * float(np.exp(-0.3))

VEC = {}
_at = 0
for _name, _n in [("norm_mix", 8), ("norm_ffn", 8), ("c", 8), ("final_g", 8), ("pool_scale", 8), ("subln", 1),
                  ("norm_g", 48), ("conv", 132), ("mod_b", 144), ("mu", 14), ("w0", 4), ("a0", 4), ("k_k", 4),
                  ("k_a", 4), ("r_k", 4), ("ln_w", 4), ("ln_b", 4), ("qk_gain", 4)]:
    VEC[_name] = (_at, _n)
    _at += _n
NVEC = _at

CST = {}
_at = 0
for _name, _n in [("ident", 128), ("ones", 128), ("pair", 128), ("perm", 128)]:
    CST[_name] = (_at, _at + _n)
    _at += _n
NCST = _at


def level_halves():
    return [("a", 0), ("b", 4)]


RW_PE = (["w", "a", "g", "kss", "krs", "bonus", "tokA", "tokB", "tokK", "tokV"]
         + [f"P1{n}" for n in range(4)] + [f"P2{n}" for n in range(4)] + ["X0a", "X0b"]
         + [f"{x}{lev}{h}" for lev in range(1, 6) for x in ("A", "Y", "X") for h in "ab" if (x, lev) != ("X", 5)]
         + ["MV", "U0", "WT"] + [x for c in range(NCH) for x in ((f"u{c}", f"s{c}") if c < NCH - 1 else (f"u{c}",))]
         + ["y", "mean", "vss", "vrs"])
RW_ACT = (["sw", "a", "g", "kkq", "kstd", "Ep", "En", "Em", "D", "tokA", "tokB", "tokK", "tokV", "X0a", "X0b"]
          + [f"{x}{lev}{h}" for lev in range(1, 6) for x in ("A", "X") for h in "ab" if (x, lev) != ("X", 5)]
          + ["MV", "U0", "y", "ysq", "vstd"])
RW_DVE = (["kk0", "cs", "rel", "relm", "dsum", "kmax", "krec", "krexp", "kkn", "a1", "kh", "A", "kka", "B", "K", "R",
           "rk", "bonus", "P10", "P11", "P12", "P13", "eye", "XT0", "P20", "P21", "P22", "P23"]
          + [f"Y{lev}{h}" for lev in range(1, 6) for h in "ab"] + ["WT"]
          + [x for c in range(NCH) for x in ((f"SD{c}", f"U{c}", f"S{c}") if c < NCH - 1 else (f"U{c}",))]
          + ["yc", "vrec", "vrexp", "yn", "yb", "o"])

NS_PE = (["vs", "vw", "gt"] + [f"ss{n}" for n in range(6)] + [f"rs{n}" for n in range(6)]
         + ["c0", "c1", "kc", "vc", "kcss", "kcrs"] + [f"cs{j}" for j in range(TT)])
NS_ACT = (["gl", "vs", "vw", "gt"] + [f"sq{n}" for n in range(6)] + ["std"] + [f"kd{n}" for n in range(8)]
          + ["cb0", "h0", "cb1", "h1", "kcsq", "kcstd"] + [f"kcd{n}" for n in range(4)] + [f"ce{j}" for j in range(TT)])
NS_DVE = (["pe", "q0", "q1", "q2", "q3", "kx", "vx", "ks", "vs", "kw", "vw", "gl", "gq", "rec"]
          + [f"{x}{n}" for n in range(6) for x in ("rexp", "n")] + ["kc", "vc", "kcrec", "kcrexp", "kcn"]
          + [f"{x}{j}" for j in range(TT) for x in ("add", "max", "sub", "sum", "rec", "coef", "mask", "p")])


def upto(steps, name, turn=0):
    return len(steps) * turn + steps.index(name) + 1


class Segment:

    def __init__(self, name, first, tile, shapes, tiles):
        self.name, self.first, self.tile, self.shapes, self.tiles = name, first, tile, shapes, tiles


def plan_stream(first_block, second_block):
    up, down = [(KD, P)] * (2 * KF), [(n, P) for _, n in DOWN] * KD
    order = []
    if first_block:
        order += [("mix_in", [(KD, P)] * 10 + [(KD, 24)] + [(KD, P)] * 14, 25),
                  ("merge", [(KD, P), (KD, P), (4, P), (4, P)] * 8, 32),
                  ("mix_out", [(KD, P)] * 8, 8), ("up0", up, 44), ("down0", down, 8)]
    if second_block:
        order += [("up1", up, 44), ("down1", down, 8), ("pool", [(2, P)] * 8, 8),
                  ("up2", up, 44), ("down2", down, 8), ("up3", up, 44), ("down3", down, 8),
                  ("qkv", [(KD, P)] * 24, 24), ("attn_out", [(KD, P)] * 8, 8),
                  ("up4", up, 44), ("down4", down, 8)]
    segments, unit, tile = {}, 0, 0
    for name, shapes, tiles in order:
        segments[name] = Segment(name, unit, tile, shapes, tiles)
        unit, tile = unit + len(shapes), tile + tiles
    return segments


def build(nc, A, out, first_block=True, second_block=True, dump=None):
    seg = plan_stream(first_block, second_block)
    units = [(s, n) for s in seg.values() for n in range(len(s.shapes))]

    with ExitStack() as ctx:
        def sb(name, shape, dt=F32, on=ctx):
            return on.enter_context(nc.sbuf_tensor(name, shape, dt))

        def sem(name):
            return ctx.enter_context(nc.semaphore(name))

        cst = sb("cst", [P, NCST])
        vec = sb("vec", [P, NVEC])
        eps = sb("eps", [P, 2])
        zero = sb("zero", [P, 1])
        xT = sb("xT", [P, KD, S])
        h_hi = sb("h_hi", [P, KD, S], F32R)
        h_lo = sb("h_lo", [P, KD, S], F32R)
        stage = sb("stage", [P, NSTAGE, SLOT])
        w_hi = sb("w_hi", [P, 2, SLOT], F32R)
        w_lo = sb("w_lo", [P, 2, SLOT], F32R)
        norm_t = sb("norm_t", [P, 2, S])
        sq = norm_t
        std = sb("std", [P, TT])
        rstd = sb("rstd", [P, TT])
        rdiag = sb("rdiag", [P, 2, TT, P])
        if second_block:
            modv = sb("modv", [P, 2, 72])
            c_act = sb("c_act", [P, KD])
            mod_w = sb("mod_w", [P, 2, 2, S])
            mod_acc = sb("mod_acc", [P, S])
            scales = sb("scales", [P, 2, 3, KD])
            gates = sb("gates", [P, 2, 3, KD])
            lam_in = sb("lam_in", [P, 4 * HD])
            lam_sum = sb("lam_sum", [P, 2])
            lam_exp = sb("lam_exp", [P, 2])
            neg_lam = sb("neg_lam", [P, 1])
            sub_gain = sb("sub_gain", [P, 1])
            nmax = sb("nmax", [P, 2, 2])
            esum = sb("esum", [P, 2, 2])
            coef = sb("coef", [P, 2, 2])
            ostd = sb("ostd", [P, DIFF_HEADS * TT])
            orstd = sb("orstd", [P, DIFF_HEADS * TT])

        ident, ones = cst[:, 0:128], cst[:, 128:256]
        pair_ones, perm = cst[:, 256:384], cst[:, 384:512]

        def v(name, n=0, count=1):
            return vec[:, VEC[name][0] + n:VEC[name][0] + n + count]

        psum = ctx.enter_context(nc.psum_tensor("psum", [P, 8, S], F32))

        tables = sem("tables")
        x_in = sem("x_in")
        filled = sem("filled")
        loaded = [sem(f"loaded{n}") for n in range(NSTAGE)]
        hi_done = sem("hi_done")
        lo_done = sem("lo_done")
        unit_done = sem("unit_done")
        x_ready = sem("x_ready")
        sq_done = sem("sq_done")
        ssq_done = sem("ssq_done")
        std_done = sem("std_done")
        rstd_done = sem("rstd_done")
        rdiag_done = sem("rdiag_done")
        rbc_done = sem("rbc_done")
        t_done = sem("t_done")
        hhi_done = sem("hhi_done")
        hlo_done = sem("hlo_done")
        silu_done = sem("silu_done")
        hid_done = sem("hid_done")
        hidhi_done = sem("hidhi_done")
        hidlo_done = sem("hidlo_done")
        tap_done = sem("tap_done")
        mod_in = [sem("mod_in0"), sem("mod_in1")]
        mod_mul = sem("mod_mul")
        mod_sum = sem("mod_sum")
        mod_out = sem("mod_out")
        mod_vec = sem("mod_vec")
        c_done = sem("c_done")
        lam_done = sem("lam_done")
        padded = sem("padded")
        win_done = sem("win_done")
        diff_done = sem("diff_done")
        diff_hi = sem("diff_hi")
        raw_done = sem("raw_done")
        post_done = sem("post_done")
        roped = sem("roped")
        vtok_done = sem("vtok_done")
        score_done = sem("score_done")
        max_done = sem("max_done")
        exp_done = sem("exp_done")
        comb_step = sem("comb_step")
        a_turned = sem("a_turned")
        pt_done = sem("pt_done")
        pv_done = sem("pv_done")
        o_done = sem("o_done")
        osq_done = sem("osq_done")
        ossq_done = sem("ossq_done")
        ostd_done = sem("ostd_done")
        orstd_done = sem("orstd_done")
        odiag_done = sem("odiag_done")
        obc_done = sem("obc_done")
        ot_done = sem("ot_done")
        ohi_done = sem("ohi_done")
        olo_done = sem("olo_done")
        xt_done = sem("xt_done")
        if first_block:
            ns_in, ns2_in, rw_in = sem("ns_in"), sem("ns2_in"), sem("rw_in")
            ns_pe, ns_act, ns_dve = sem("ns_pe"), sem("ns_act"), sem("ns_dve")
            rw_pe, rw_act, rw_dve = sem("rw_pe"), sem("rw_act"), sem("rw_dve")
            nscore_done, nmask_done, nmax_done, nexp_done = sem("nscore_done"), sem("nmask_done"), sem("nmax_done"), sem("nexp_done")
            nscale_step, nturned, npt_done, npv_done, no_done = (sem("nscale_step"), sem("nturned"), sem("npt_done"),
                                                                 sem("npv_done"), sem("no_done"))
            zraw_done, zdiff_done, zm_done, zact_done, zset = (sem("zraw_done"), sem("zdiff_done"), sem("zm_done"),
                                                              sem("zact_done"), sem("zset"))
            osplit_hi, osplit_lo = sem("osplit_hi"), sem("osplit_lo")
            sig_done, y_step, yhi_done, ylo_done = sem("sig_done"), sem("y_step"), sem("yhi_done"), sem("ylo_done")
        turned = sem("turned")
        out_copied = sem("out_copied")
        stored = sem("stored")

        def phase(*tensors):
            with ExitStack() as own:
                return [sb(n, shape, dt, own) for n, shape, dt in tensors]

        if first_block:
            mixer = ExitStack()
            o_nsa = sb("o_nsa", [P, 4, S], F32, mixer)

            def mixer_phase(*tensors):
                with ExitStack() as own:
                    return [sb(n, shape, dt, own) for n, shape, dt in tensors]

            (q_n, k_n, kd, kx, v_nt, gl, gate_t, Pn, PTn, PTc, Pc, kcd, cb, hid_c, kc_n, vc_t, raw_n, tri, cadd, cmul, w2_c,
             stat_n, rec_n, rexp_n, nmax_n, esum_n, coef_n, cmx, csum, gq, cpe) = mixer_phase(
                ("q_n", [P, 4, S], F32), ("k_n", [P, 2, S], F32), ("kd", [P, 2, 2, S], F32),
                ("kx", [P, 2, CMP_BLOCK, 32], F32), ("v_nt", [P, 2, TT, P], F32), ("gl", [24, S], F32),
                ("gate_t", [P, TT, 24], F32), ("Pn", [P, 2, 2, S], F32), ("PTn", [P, 2, 2, TT, S], F32),
                ("PTc", [NC, 2, S], F32), ("Pc", [P, TT, NSA_HEADS, 32], F32), ("kcd", [P, 2, 32], F32),
                ("cb", [P, 2], F32), ("hid_c", [P, 2, 32], F32), ("kc_n", [P, 32], F32), ("vc_t", [NC, P], F32),
                ("raw_n", [P, 2, S], F32), ("tri", [P, P], F32), ("cadd", [P, TT, NC], F32), ("cmul", [P, TT, NC], F32),
                ("w2_c", [P, 2, P], F32), ("stat_n", [P, 7, TT, 2], F32), ("rec_n", [P, 7, TT, 2], F32),
                ("rexp_n", [P, 2, TT, P], F32), ("nmax_n", [P, 2, 2], F32), ("esum_n", [P, 2, 2], F32),
                ("coef_n", [P, 2, 2], F32), ("cmx", [P, NSA_HEADS], F32), ("csum", [P, NSA_HEADS], F32),
                ("gq", [P, 1], F32), ("cpe", [P, 2, CMP_BLOCK], F32))
            w1_c = PTn[:].rearrange("p a b t s -> p (a b t s)").rearrange("p (k l n) -> p k l n", k=2, l=CMP_BLOCK)

            zm = sb("zm", [P, 14, S], F32, mixer)
            (low_up, g_up, keep, zraw, tA, tB, tC, tD, AR, Bt, Kt, tok, TR, MR, XT, X, Ap, Sh, SD, Dc, kst, krec,
             rmask, mask8) = mixer_phase(
                ("low_up", [P, S], F32), ("g_up", [P, S], F32), ("keep", [P, S], F32), ("zraw", [P, 2, S + 4], F32),
                ("tA", [P, S], F32), ("tB", [P, S], F32), ("tC", [P, S], F32), ("tD", [P, S], F32),
                ("AR", [P, TT, 2, P], F32), ("Bt", [P, S], F32), ("Kt", [P, S], F32), ("tok", [P, 4, TT, P], F32),
                ("TR", [P, 8, 2 * P], F32), ("MR", [P, 8, 2 * P], F32), ("XT", [P, 8, P], F32), ("X", [P, 8, P], F32),
                ("Ap", [P, 8, P], F32), ("Sh", [P, NCH, HD], F32), ("SD", [P, HD], F32), ("Dc", [P, NCH], F32),
                ("kst", [P, TT, 2], F32), ("krec", [P, TT, 2], F32), ("rmask", [P, S], F32),
                ("mask8", [P, 8 * P], mybir.dt.uint8))
            stri = mask8[:, 0:2 * P]
            lmask = mask8[:, 2 * P:].rearrange("p (l n) -> p l n", l=6)
            o_hi, o_lo, y_hi, y_lo = mixer_phase(
                ("o_hi", [P, KD, S], F32R), ("o_lo", [P, KD, S], F32R), ("y_hi", [P, KD, S], F32R),
                ("y_lo", [P, KD, S], F32R))
            sg = rdiag[:].rearrange("p a t n -> p a (t n)")
            y_t = norm_t[:, 0]
            mixer.close()

        x_tok, = phase(("x_tok", [P, TT, D], F32))
        hid_hi, hid_lo, s_buf, hid, taps = phase(
            ("hid_hi", [P, KF, S], F32R), ("hid_lo", [P, KF, S], F32R),
            ("s_buf", [P, 2, S], F32), ("hid", [P, 2, S], F32), ("taps", [P, 2, S], F32))
        hp, win, icnt, diff = phase(("hp", [P, 2, S + 16], F32), ("win", [P, 2, 4, S + 16], F32),
                                    ("icnt", [P, 4, S], F32), ("diff", [P, 2, S], F32))
        q_t, k_t, v_tok, rope, raw, E, PT, o_raw = phase(
            ("q_t", [P, KD, S], F32), ("k_t", [P, KD, S], F32), ("v_tok", [P, TT, D], F32), ("rope", [P, 2, S], F32),
            ("raw", [P, 2, S], F32), ("E", [P, 2, 2, S], F32), ("PT", [P, 2, TT, S], F32), ("o_raw", [P, DIFF_HEADS, S], F32))
        y_out, out_tok = phase(("y_out", [P, 2, S], F32), ("out_tok", [P, TT, D], F32))

        def repeat(eng, start, count, body):
            if count == 1:
                body(start)
            elif count > 1:
                with eng.Fori(start, start + count) as i:
                    body(i)

        def fixed(c, i):
            return (c + 4 * i, 0) if isinstance(i, int) else (c, i)

        def shape_of(c):
            s, n = units[c]
            return s.shapes[n]

        def slot(buf, c, kt, cols, ring):
            return buf[:, c % ring, 0:kt * cols].rearrange("p (k n) -> p k n", k=kt)

        def bank(c):
            return psum[:, c % 4, :]

        UP_RUNS = {
            0: [(0, 1, True), (1, 9, True), (10, 1, True)],
            1: [(0, 1, True), (1, 9, True), (10, 1, True)],
            2: [(0, 1, True), (1, 6, True), (7, 3, False), (10, 1, False)],
            3: [(0, 1, False), (1, 9, False), (10, 1, False)],
            4: [(0, 1, False), (1, 9, False), (10, 1, False)]}
        MIX_AT = {1: 0, 4: 1, 7: 2, 12: 3, 15: 4, 18: 5, 21: 6}
        MIX_SUM = {3: 0, 6: 1, 9: 2, 14: 3, 17: 4, 20: 5, 23: 6}
        MIX_FINISH = {10: 2, 24: 6}
        FRESH = (0, 3, 7, MOD_GROUPS_LAYER)
        MIX_GROUPS = 7
        MOD_FIRST = {0: MIX_GROUPS, 1: 18, 2: 29}
        if not first_block:
            UP_RUNS[1] = [(0, 1, False), (1, 9, False), (10, 1, False)]
            UP_RUNS[2] = UP_RUNS[1]
        PAIR = {f: KF * (f - (0 if first_block else 1)) for f in range(5)}
        NORM = {n: n - (0 if first_block else 2) for n in range(9)}
        ffns = ([0] if first_block else []) + ([1, 2, 3, 4] if second_block else [])
        last_norm = 8
        if not second_block:
            NORM[8] = 2

        def source(c, i=0):
            s, n = units[c]
            kt, cols = s.shapes[n]
            if s.name.startswith("up") or s.name.startswith("down"):
                w = A[s.name]
                if s.name.startswith("down"):
                    k0 = DOWN[n % 3][0] * P
                    return w[n // 3, :, k0:k0 + kt * P]
                return w[bass.ds(n + 4 * i, 1)].rearrange("a p n -> (a p) n")
            if s.name == "mix_in":
                return A["w_in24"] if cols == 24 else A["w_in"][n if n < 10 else n - 1]
            if s.name == "merge":
                w, at = [("w_merge", n // 4), ("w_merge", 8 + n // 4), ("proj_nsa", n // 4), ("proj_rwkv", n // 4)][n % 4]
                return A[w][at]
            return A[{"mix_out": "w_out", "pool": "pool_w", "qkv": "w_qkv", "attn_out": "w_o"}[s.name]][n]

        NU = len(units)

        block = ctx.enter_context(nc.Block())

        @block.sync
        def _(sp):
            sp.dma_start(x_tok[:], A["x"].rearrange("(t p) d -> p t d", p=P)).then_inc(x_in, 16)
            sp.dma_start(cst[:], A["cst"]).then_inc(tables, 16)
            sp.dma_start(vec[:], A["vec"]).then_inc(tables, 16)
            if second_block:
                sp.dma_start(lam_in[:], A["lam"].to_broadcast([P, 4 * HD])).then_inc(tables, 16)

            def load(c, i=0):
                c, i = fixed(c, i)
                kt, cols = shape_of(c)
                if not (isinstance(i, int) and c < NSTAGE):
                    sp.wait_ge(lo_done, c + 4 * i - NSTAGE + 1)
                sp.dma_start(stage[:, c % NSTAGE, 0:kt * cols], source(c, i)).then_inc(loaded[c % NSTAGE], 16)

            for s in seg.values():
                if s.name == "mix_in":
                    for n in range(NSTAGE):
                        load(s.first + n)
                    for dst, src in ((w1_c, "cmp_w1"), (w2_c[:], "cmp_w2"), (cpe[:], "cmp_pe"), (tri[:], "tri"),
                                     (cadd[:], "cadd"), (cmul[:], "cmul")):
                        if dst is w1_c:
                            sp.wait_ge(turned, KD)
                        sp.dma_start(dst, A[src]).then_inc(ns_in, 16)
                    for n in range(NSTAGE, 14):
                        load(s.first + n)
                    sp.wait_ge(no_done, NSA_HEADS)
                    for dst, src in ((low_up[:], "low_up"), (g_up[:], "g_up"), (rmask[:], "rmask"),
                                     (AR[:].rearrange("p t a n -> p (t a n)"), "masks")):
                        sp.dma_start(dst, A[src]).then_inc(rw_in, 16)
                    for n in range(14, 25):
                        load(s.first + n)
                elif s.name.startswith("up"):
                    repeat(sp, 0, KF // 2, lambda i: [load(s.first + j, i) for j in range(4)])
                else:
                    if s.name == "pool":
                        sp.wait_ge(unit_done, s.first)
                        sp.dma_start(icnt[:], A["icnt"].to_broadcast([P, 4, S])).then_inc(tables, 16)
                    if s.name == "qkv":
                        sp.wait_ge(unit_done, s.first)
                        sp.dma_start(rope[:], A["rope"]).then_inc(tables, 16)
                    for n in range(len(s.shapes)):
                        load(s.first + n)
            for tt in range(2):
                sp.wait_ge(out_copied, 8)
                sp.dma_start(out.rearrange("(t p) d -> p t d", p=P)[:, 2 * tt:2 * tt + 2, :],
                             out_tok[:, 2 * tt:2 * tt + 2, :]).then_inc(stored, 16)
            sp.wait_ge(stored, 32)

        @block.gpsimd
        def _(pool):
            pool.memset(eps[:, 0:1], EPS)
            pool.memset(eps[:, 1:2], LNX_EPS).then_inc(filled, 1)
            pool.memset(zero[:], 0.0).then_inc(filled, 1)

            def mod_load(g):
                for h in range(4):
                    if not (isinstance(g, int) and 4 * g + h < 2):
                        pool.wait_ge(mod_mul, 8 * g + 2 * h - 2)
                    pool.dma_start(mod_w[:, h % 2], A["mod_w"][bass.ds(4 * g + h, 1)].rearrange(
                        "a p (k n) -> (a p) k n", k=2)).then_inc(mod_in[h % 2], 16)

            if second_block:
                mod_load(0)
                repeat(pool, 1, N_MOD_GROUPS - 1, mod_load)

        @block.scalar
        def _(act):
            def hi(c, i=0):
                c, i = fixed(c, i)
                if c >= NU:
                    return
                kt, cols = shape_of(c)
                act.wait_ge(loaded[c % NSTAGE], 16 * (c // NSTAGE + 1 + i))
                if not (isinstance(i, int) and c < 2):
                    act.wait_ge(unit_done, c + 4 * i - 1)
                act.activation(w_hi[:, c % 2, 0:kt * cols], stage[:, c % NSTAGE, 0:kt * cols],
                               ACT.Copy).then_inc(hi_done, 1)

            def square(n_norm, k):
                at = KD * NORM[n_norm] + k
                act.wait_ge(x_ready, at + 1)
                if at >= 2:
                    act.wait_ge(ssq_done, at - 1)
                act.activation(sq[:, k % 2], xT[:, k], ACT.Square).then_inc(sq_done, 1)

            def root(n_norm):
                at = KD * NORM[n_norm]
                act.wait_ge(ssq_done, at + KD)
                act.activation(std[:], psum[:, 4, 0:TT], ACT.Sqrt, bias=eps[:, 0:1], scale=1.0 / D).then_inc(std_done, 1)

            def round_h(n_norm, shift):
                for k in range(KD):
                    at = KD * NORM[n_norm] + k
                    act.wait_ge(t_done, at + 1)
                    act.activation(h_hi[:, k], norm_t[:, k % 2], ACT.Identity, bias=shift(k)).then_inc(hhi_done, 1)

            def up(f):
                s, pairs = seg[f"up{f}"], PAIR[f]

                def body(i):
                    for q in range(2):
                        p = pairs + 2 * i + q
                        hi(s.first + 2 * q + 2, i)
                        if f == 0:
                            act.wait_ge(tap_done, 6 * (2 * i + q) + 3)
                            act.activation(s_buf[:, q], taps[:, 0], ACT.Silu).then_inc(silu_done, 1)
                        else:
                            act.wait_ge(unit_done, s.first + 4 * i + 2 * q + 1)
                            act.activation(s_buf[:, q], bank(s.tile + 2 * q), ACT.Silu).then_inc(silu_done, 1)
                        hi(s.first + 2 * q + 3, i)
                        act.wait_ge(hid_done, p + 1)
                        act.activation(hid_hi[:, bass.ds(2 * i + q, 1), :].rearrange("p a n -> p (a n)"), hid[:, q],
                                       ACT.Copy).then_inc(hidhi_done, 1)

                for start, count, _ in UP_RUNS[f]:
                    repeat(act, start, count, body)

            def down(f, n_norm):
                s = seg[f"down{f}"]
                for n in range(KD):
                    for j in range(3):
                        hi(s.first + 3 * n + j + 2)
                    square(n_norm, n)

            def mixed_out(name, n_norm):
                s = seg[name]
                for n in range(KD):
                    hi(s.first + n + 2)
                    square(n_norm, n)

            act.wait_ge(filled, 2)
            act.wait_ge(tables, 48 if second_block else 32)
            if second_block:
                act.activation(c_act[:], v("c", 0, KD), ACT.Silu).then_inc(c_done, 1)
                act.wait_ge(lam_done, 2)
                act.activation(lam_exp[:], lam_sum[:], ACT.Exp).then_inc(c_done, 1)
            hi(0)
            hi(1)
            for k in range(KD):
                square(0 if first_block else 2, k)

            def plain(name):
                return lambda k: v(name, k)

            if first_block:
                zero_shift = lambda k: zero[:, 0:1]
                root(0)
                round_h(0, zero_shift)
                s = seg["mix_in"]

                def ns(name, ins):
                    assert NS_ACT[ns_count[0]] == name, (name, NS_ACT[ns_count[0]])
                    ns_count[0] += 1
                    ins.then_inc(ns_act, 1)

                def after_ns(sem_, steps, name):
                    act.wait_ge(sem_, upto(steps, name))

                ns_count = [0]
                for n in range(11):
                    hi(s.first + n + 2)
                act.wait_ge(unit_done, s.first + 11)
                ns("gl", act.activation(gl[:], bank(s.tile + 10)[0:24, :], ACT.Sigmoid))
                for n, name in enumerate(("vs", "vw")):
                    after_ns(ns_pe, NS_PE, name)
                    ns(name, act.activation(v_nt[:, n], psum[:, 4 + n, :].rearrange("p (t n) -> p t n", t=TT), ACT.Copy))
                after_ns(ns_pe, NS_PE, "gt")
                ns("gt", act.activation(gate_t[:], psum[:, 6, 0:TT * 24].rearrange("p (t n) -> p t n", t=TT), ACT.Copy))
                for n in range(6):
                    src = q_n[:, n] if n < 4 else k_n[:, n - 4]
                    after_ns(ns_dve, NS_DVE, f"q{n}" if n < 4 else ("ks", "kw")[n - 4])
                    if n >= 2:
                        after_ns(ns_pe, NS_PE, f"ss{n - 2}")
                    ns(f"sq{n}", act.activation(raw_n[:, n % 2], src, ACT.Square))
                after_ns(ns_pe, NS_PE, "ss5")
                ns("std", act.activation(stat_n[:, 0:6].rearrange("p a t c -> p (a t c)"), psum[:, 7, 8:56], ACT.Sqrt,
                                         bias=eps[:, 0:1], scale=1.0 / HD))
                after_ns(ns_dve, NS_DVE, "n5")
                for kind in range(2):
                    for g in range(NSA_GROUPS):
                        for half in range(2):
                            src = k_n[HD * g:HD * g + HD, kind]
                            ns(f"kd{4 * kind + 2 * g + half}",
                               act.activation(kd[HD * half:HD * half + HD, kind, g], src, ACT.Copy))
                for c in range(2):
                    after_ns(ns_pe, NS_PE, f"c{c}")
                    ns(f"cb{c}", act.activation(cb[:, c:c + 1], psum[:, 4 + c, NC:NC + 1], ACT.Copy))
                    act.wait_ge(ns_act, upto(NS_ACT, f"cb{c}"))
                    ns(f"h{c}", act.activation(hid_c[:, c, 0:NC], psum[:, 4 + c, 0:NC], ACT.Silu, bias=cb[:, c:c + 1]))
                after_ns(ns_dve, NS_DVE, "kc")
                ns("kcsq", act.activation(raw_n[:, 0, 0:NC], kc_n[:, 0:NC], ACT.Square))
                after_ns(ns_pe, NS_PE, "kcss")
                ns("kcstd", act.activation(stat_n[0:NC, 6, 0, :], psum[0:NC, 4, 0:2], ACT.Sqrt, bias=eps[0:NC, 0:1],
                                           scale=1.0 / HD))
                after_ns(ns_dve, NS_DVE, "kcn")
                for g in range(NSA_GROUPS):
                    for half in range(2):
                        ns(f"kcd{2 * g + half}", act.activation(kcd[HD * half:HD * half + HD, g, 0:NC],
                                                                kc_n[HD * g:HD * g + HD, 0:NC], ACT.Copy))
                for j in range(TT):
                    after_ns(ns_dve, NS_DVE, f"sub{j}")
                    ns(f"ce{j}", act.activation(Pc[:, j, :, 0:NC], Pc[:, j, :, 0:NC], ACT.Exp))

                M = 4 * NSA_HEADS
                for m in range(M + 2):
                    if m < M:
                        h, j = m // 4, m % 4
                        act.wait_ge(nmax_done, m + 1)
                        if m >= 2:
                            act.wait_ge(nturned, m - 1)
                        for c in range(2):
                            act.activation(Pn[:, m % 2, c, 0:(j + 1) * P], psum[:, 2 * (m % 2) + c, 0:(j + 1) * P], ACT.Exp,
                                           bias=nmax_n[:, m % 2, c:c + 1],
                                           accum_out=esum_n[:, m % 2, c:c + 1]).then_inc(nexp_done, 1)
                    if m >= 2:
                        h, j = (m - 2) // 4, (m - 2) % 4
                        act.wait_ge(nturned, m - 1)
                        if h >= 2 and j == 0:
                            act.wait_ge(npv_done, h - 1)
                        for c in range(2):
                            act.activation(PTn[:, h % 2, c, 0:j + 1, j * P:(j + 1) * P],
                                           psum[:, 4 + c, 0:(j + 1) * P].rearrange("p (t n) -> p t n", n=P),
                                           ACT.Copy).then_inc(npt_done, 1)
                        act.activation(PTc[:, h % 2, j * P:(j + 1) * P], psum[0:NC, 7, 0:P], ACT.Copy).then_inc(npt_done, 1)

                act.wait_ge(zset, 2)
                for n in range(14):
                    act.wait_ge(unit_done, s.first + 11 + n + 1)
                    if n >= 2:
                        act.wait_ge(zm_done, n - 1)
                    act.activation(zraw[:, n % 2, 1:S + 1], bank(s.tile + 11 + n), ACT.Copy).then_inc(zraw_done, 1)
                    hi(s.first + 11 + n + 2)
                act.wait_ge(zm_done, 14)
                act.activation(zm[0:HD, 12], zm[0:HD, 12], ACT.Tanh).then_inc(zact_done, 1)
                act.activation(zm[:, 13], zm[:, 13], ACT.Sigmoid).then_inc(zact_done, 1)

                rw_count = [0]

                def rw(name, ins):
                    assert RW_ACT[rw_count[0] % len(RW_ACT)] == name, (name, RW_ACT[rw_count[0] % len(RW_ACT)])
                    rw_count[0] += 1
                    ins.then_inc(rw_act, 1)

                def heads(x):
                    return x.rearrange("p t n -> p (t n)")

                for p in range(PAIRS):
                    def given(name):
                        act.wait_ge(rw_pe, upto(RW_PE, name, p))

                    def done(name):
                        act.wait_ge(rw_dve, upto(RW_DVE, name, p))

                    def own(name):
                        act.wait_ge(rw_act, upto(RW_ACT, name, p))

                    given("w")
                    if p >= 1:
                        act.wait_ge(rw_dve, upto(RW_DVE, "o", p - 1))
                    rw("sw", act.activation(tA[:], psum[:, 0, :], ACT.Sigmoid, bias=v("w0", p)))
                    given("a")
                    rw("a", act.activation(tB[:], psum[:, 1, :], ACT.Sigmoid, bias=v("a0", p)))
                    given("g")
                    rw("g", act.activation(keep[:], psum[:, 2, :], ACT.Copy))
                    done("kk0")
                    rw("kkq", act.activation(tD[:], tC[:], ACT.Square))
                    given("kss")
                    rw("kstd", act.activation(kst[:].rearrange("p t c -> p (t c)"), psum[:, 3, 0:8], ACT.Sqrt))
                    done("dsum")
                    rw("Ep", act.activation(AR[:, :, 1, :], Kt[:].rearrange("p (t n) -> p t n", t=TT), ACT.Exp, scale=-DECAY))
                    own("Ep")
                    rw("En", act.activation(Kt[:], Kt[:], ACT.Exp, scale=DECAY))
                    rw("Em", act.activation(tD[:], tD[:], ACT.Exp, scale=-DECAY))
                    rw("D", act.activation(Dc[:, 0:NCH - 1], Dc[:, 0:NCH - 1], ACT.Exp, scale=-DECAY))
                    for n, name in enumerate(("tokA", "tokB", "tokK", "tokV")):
                        given(name)
                        rw(name, act.activation(tok[:, n], psum[:, (6 + n) % 8, :].rearrange("p (t n) -> p t n", t=TT), ACT.Copy))
                    for n in range(2):
                        given("X0" + "ab"[n])
                        rw("X0" + "ab"[n], act.activation(heads(X[:, 4 * n:4 * n + 4]), psum[:, 6 + n, :], ACT.Copy))
                    for lev in range(1, 6):
                        for n in range(2):
                            given(f"A{lev}" + "ab"[n])
                            rw(f"A{lev}" + "ab"[n], act.activation(heads(Ap[:, 4 * n:4 * n + 4]), psum[:, 2 + n, :], ACT.Copy))
                        if lev < 5:
                            for n in range(2):
                                given(f"X{lev}" + "ab"[n])
                                rw(f"X{lev}" + "ab"[n], act.activation(heads(X[:, 4 * n:4 * n + 4]), psum[:, 6 + n, :], ACT.Copy))
                    given("MV")
                    rw("MV", act.activation(heads(X[:, 0:4]), psum[:, 0, :], ACT.Copy))
                    given("U0")
                    rw("U0", act.activation(heads(X[:, 4:8]), psum[:, 1, :], ACT.Copy))
                    given("y")
                    rw("y", act.activation(tA[:], psum[:, 7, :], ACT.Copy))
                    done("yc")
                    rw("ysq", act.activation(tB[:], tC[:], ACT.Square))
                    given("vss")
                    rw("vstd", act.activation(kst[:].rearrange("p t c -> p (t c)"), psum[:, 1, 0:8], ACT.Sqrt,
                                              bias=eps[:, 1:2], scale=1.0 / HD))

                act.wait_ge(rw_dve, upto(RW_DVE, "o", PAIRS - 1))
                for k in range(KD):
                    act.activation(o_hi[:, k], o_nsa[:, k] if k < 4 else zm[:, k - 4], ACT.Copy).then_inc(osplit_hi, 1)
                s = seg["merge"]
                for n in range(KD):
                    for j in range(4):
                        act.wait_ge(unit_done, s.first + 4 * n + j + 1)
                        if j < 2:
                            if n >= 1:
                                act.wait_ge(y_step, 3 * n - (1 if j == 0 else 0))
                            act.activation(sg[:, j], bank(s.tile + 4 * n + j), ACT.Sigmoid).then_inc(sig_done, 1)
                        hi(s.first + 4 * n + j + 2)
                    act.wait_ge(y_step, 3 * n + 3)
                    act.activation(y_hi[:, n], y_t, ACT.Copy).then_inc(yhi_done, 1)
                mixed_out("mix_out", 1)
                root(1)
                round_h(1, zero_shift)
                up(0)
                down(0, 2 if second_block else 8)

            if second_block:
                def shift(layer, which):
                    return lambda k: modv[:, layer, 24 * which + k:24 * which + k + 1]

                root(2)
                act.wait_ge(mod_vec, 1)
                round_h(2, shift(0, 0))
                up(1)
                down(1, 3)
                root(3)
                act.wait_ge(padded, 4)
                for k in range(KD):
                    act.wait_ge(t_done, KD * NORM[3] + k + 1)
                    if k >= 2:
                        act.wait_ge(diff_done, k - 1)
                    act.activation(hp[:, k % 2, 8:8 + S], norm_t[:, k % 2], ACT.Identity,
                                   bias=shift(0, 1)(k)).then_inc(hhi_done, 1)
                    if k >= 1:
                        act.wait_ge(diff_done, k)
                        act.activation(h_hi[:, k - 1], diff[:, (k - 1) % 2], ACT.Copy).then_inc(diff_hi, 1)
                act.wait_ge(diff_done, KD)
                act.activation(h_hi[:, KD - 1], diff[:, (KD - 1) % 2], ACT.Copy).then_inc(diff_hi, 1)
                mixed_out("pool", 4)
                root(4)
                round_h(4, shift(0, 2))
                up(2)
                down(2, 5)
                root(5)
                act.wait_ge(mod_vec, 2)
                round_h(5, shift(1, 0))
                up(3)
                down(3, 6)
                root(6)
                round_h(6, shift(1, 1))

                s = seg["qkv"]
                for n in range(24):
                    hi(s.first + n + 2)
                    if 1 <= n <= 8:
                        act.wait_ge(post_done, n)
                        act.activation(v_tok[:, :, (n - 1) * P:n * P],
                                       psum[:, 4 + (n - 1) % 2, :].rearrange("p (t n) -> p t n", t=TT),
                                       ACT.Copy).then_inc(vtok_done, 1)

                for m in range(4 * DIFF_HEADS + 2):
                    if m < 4 * DIFF_HEADS:
                        act.wait_ge(max_done, m + 1)
                        if m >= 2:
                            act.wait_ge(a_turned, m - 1)
                        for c in range(2):
                            act.activation(E[:, m % 2, c], psum[:, 2 * (m % 2) + c, :], ACT.Exp,
                                           bias=nmax[:, m % 2, c:c + 1],
                                           accum_out=esum[:, m % 2, c:c + 1]).then_inc(exp_done, 1)
                    if m >= 2:
                        g = m - 2
                        h, j = g // 4, g % 4
                        act.wait_ge(a_turned, g + 1)
                        if h >= 2 and j == 0:
                            act.wait_ge(pv_done, h - 1)
                        act.activation(PT[:, h % 2, :, j * P:(j + 1) * P],
                                       psum[:, 4 + g % 2, :].rearrange("p (t n) -> p t n", t=TT),
                                       ACT.Copy).then_inc(pt_done, 1)
                for h in range(DIFF_HEADS):
                    act.wait_ge(o_done, h + 1)
                    if h >= 2:
                        act.wait_ge(ossq_done, h - 1)
                    act.activation(sq[:, h % 2], o_raw[:, h], ACT.Square).then_inc(osq_done, 1)
                act.wait_ge(ossq_done, DIFF_HEADS)
                act.activation(ostd[:], psum[:, 4, 0:DIFF_HEADS * TT], ACT.Sqrt, bias=eps[:, 0:1],
                               scale=1.0 / P).then_inc(ostd_done, 1)
                for h in range(DIFF_HEADS):
                    act.wait_ge(ot_done, h + 1)
                    act.activation(h_hi[:, h], norm_t[:, h % 2], ACT.Copy).then_inc(ohi_done, 1)
                mixed_out("attn_out", 7)
                root(7)
                round_h(7, shift(1, 2))
                up(4)
                down(4, 8)

            root(last_norm)
            for k in range(KD):
                act.wait_ge(xt_done, k + 1)
                act.activation(out_tok[:, :, k * P:(k + 1) * P],
                               psum[:, k % 4, :].rearrange("p (t n) -> p t n", t=TT), ACT.Copy).then_inc(out_copied, 1)

        @block.vector
        def _(dve):
            def lo(c, i=0):
                c, i = fixed(c, i)
                if c >= NU:
                    return
                kt, cols = shape_of(c)
                dve.wait_ge(hi_done, c + 4 * i + 1)
                dve.tensor_tensor(w_lo[:, c % 2, 0:kt * cols], stage[:, c % NSTAGE, 0:kt * cols],
                                  w_hi[:, c % 2, 0:kt * cols].bitcast(F32), ALU.subtract).then_inc(lo_done, 1)

            def norm(n_norm, scale, shift, hi_of=None, after=None):
                base = KD * NORM[n_norm]
                dve.wait_ge(std_done, NORM[n_norm] + 1)
                dve.reciprocal(rstd[:], std[:]).then_inc(rstd_done, 1)
                dve.wait_ge(rstd_done, NORM[n_norm] + 1)
                for tt in range(TT):
                    i = dve.tensor_scalar(rdiag[:, 0, tt], ident, rstd[:, tt:tt + 1], None, ALU.mult)
                i.then_inc(rdiag_done, 1)
                dve.wait_ge(rbc_done, NORM[n_norm] + 1)
                for k in range(KD + 1):
                    if k < KD:
                        if k >= 2:
                            dve.wait_ge(hlo_done, base + k - 1)
                        dve.scalar_tensor_tensor(out=norm_t[:, k % 2], in0=xT[:, k], scalar=scale(k),
                                                 in1=psum[:, 5, :], op0=ALU.mult, op1=ALU.mult).then_inc(t_done, 1)
                    if k >= 1:
                        dve.wait_ge(hhi_done, base + k)
                        dve.scalar_tensor_tensor(out=h_lo[:, k - 1], in0=norm_t[:, (k - 1) % 2], scalar=shift(k - 1),
                                                 in1=h_hi[:, k - 1].bitcast(F32), op0=ALU.add,
                                                 op1=ALU.subtract).then_inc(hlo_done, 1)

            def mod_finish(g):
                dve.wait_ge(mod_sum, g + 1)
                layer_cols = modv[:].rearrange("p a b -> p (a b)")
                dve.tensor_tensor(layer_cols[:, bass.ds(4 * g, 4)], psum[:, 7, 0:4],
                                  vec[:, bass.ds(VEC["mod_b"][0] + 4 * g, 4)], ALU.add).then_inc(mod_out, 1)

            def mod_group(g):
                if not (isinstance(g, int) and (g in FRESH if first_block else g % MOD_GROUPS_LAYER == 0)):
                    mod_finish(g - 1)
                for kk in range(KD):
                    w = mod_w[:, (kk // 2) % 2, kk % 2]
                    if kk % 2 == 0:
                        dve.wait_ge(mod_in[(kk // 2) % 2], 32 * g + 16 * (kk // 4 + 1))
                    if kk == 0:
                        dve.tensor_scalar(mod_acc[:], w, c_act[:, 0:1], None, ALU.mult).then_inc(mod_mul, 1)
                    else:
                        dve.wait_ge(mod_mul, 8 * g + kk)
                        dve.scalar_tensor_tensor(out=mod_acc[:], in0=w, scalar=c_act[:, kk:kk + 1], in1=mod_acc[:],
                                                 op0=ALU.mult, op1=ALU.add).then_inc(mod_mul, 1)

            def mod_vectors(layer):
                mod_finish(MOD_GROUPS_LAYER * (layer + 1) - 1)
                dve.wait_ge(mod_out, MOD_GROUPS_LAYER * (layer + 1))
                for which in range(3):
                    cols = modv[:, layer, 24 * which:24 * which + 24]
                    dve.scalar_tensor_tensor(out=scales[:, layer, which], in0=cols[:, 8:16], scalar=1.0,
                                             in1=v("norm_g", 8 * (3 * layer + which), 8), op0=ALU.add, op1=ALU.mult)
                    if which == 1 and layer == 0:
                        i = dve.tensor_tensor(gates[:, layer, which], cols[:, 16:24], v("pool_scale", 0, 8), ALU.mult)
                    else:
                        i = dve.tensor_scalar(gates[:, layer, which], cols[:, 16:24], 1.0 if which == 1 else 0.5,
                                              None, ALU.mult)
                i.then_inc(mod_vec, 1)

            def up(f):
                s, pairs = seg[f"up{f}"], PAIR[f]

                def tap(half, c, i):
                    u = c - s.first
                    col = vec[:, bass.ds(VEC["conv"][0] + 3 * (u + 4 * i), 3)]
                    base = 3 * (u + 4 * i)
                    dve.wait_ge(unit_done, c + 4 * i + 1)
                    src = bank(s.tile + u)
                    dve.tensor_scalar(taps[:, half], src, col[:, 2:3], None, ALU.mult).then_inc(tap_done, 1)
                    dve.wait_ge(tap_done, base + 1)
                    dve.scalar_tensor_tensor(out=taps[:, half, 1:S], in0=src[:, 0:S - 1], scalar=col[:, 1:2],
                                             in1=taps[:, half, 1:S], op0=ALU.mult, op1=ALU.add).then_inc(tap_done, 1)
                    dve.wait_ge(tap_done, base + 2)
                    dve.scalar_tensor_tensor(out=taps[:, half, 2:S], in0=src[:, 0:S - 2], scalar=col[:, 0:1],
                                             in1=taps[:, half, 2:S], op0=ALU.mult, op1=ALU.add).then_inc(tap_done, 1)

                def body(i, mod):
                    for q in range(2):
                        p, c = pairs + 2 * i + q, s.first + 2 * q
                        lo(c + 2, i)
                        if f == 0:
                            tap(0, c, i)
                            tap(1, c + 1, i)
                            dve.wait_ge(tap_done, 6 * (2 * i + q) + 6)
                        dve.wait_ge(silu_done, p + 1)
                        dve.wait_ge(unit_done, c + 4 * i + 2)
                        dve.tensor_tensor(hid[:, q], s_buf[:, q], taps[:, 1] if f == 0 else bank(s.tile + 2 * q + 1),
                                          ALU.mult).then_inc(hid_done, 1)
                        lo(c + 3, i)
                        dve.wait_ge(hidhi_done, p + 1)
                        tile = bass.ds(2 * i + q, 1)
                        dve.tensor_tensor(hid_lo[:, tile, :].rearrange("p a n -> p (a n)"), hid[:, q],
                                          hid_hi[:, tile, :].rearrange("p a n -> p (a n)").bitcast(F32),
                                          ALU.subtract).then_inc(hidlo_done, 1)
                        if q == 0 and mod:
                            mod_group(MOD_FIRST[f] + i)

                for start, count, mod in UP_RUNS[f]:
                    repeat(dve, start, count, lambda i: body(i, mod and second_block))

            def add_to_x(s, n, last_unit, gate):
                dve.wait_ge(unit_done, last_unit + 1)
                dve.scalar_tensor_tensor(out=xT[:, n], in0=bank(s.tile + n), scalar=gate(n), in1=xT[:, n],
                                         op0=ALU.mult, op1=ALU.add).then_inc(x_ready, 1)

            def down(f, gate):
                s = seg[f"down{f}"]
                for n in range(KD):
                    for j in range(3):
                        lo(s.first + 3 * n + j + 2)
                    add_to_x(s, n, s.first + 3 * n + 2, gate)

            def mixed_out(name, gate):
                s = seg[name]
                for n in range(KD):
                    lo(s.first + n + 2)
                    add_to_x(s, n, s.first + n, gate)

            one = lambda n: ones[:, 0:1]

            def plain(name):
                return lambda k: v(name, k)

            dve.wait_ge(tables, 48 if second_block else 32)
            if second_block:
                for n in range(2):
                    a = lam_in[:, 2 * n * HD:(2 * n + 1) * HD]
                    dve.tensor_tensor_reduce(out=raw[:, n, 0:HD], in0=a, in1=lam_in[:, (2 * n + 1) * HD:(2 * n + 2) * HD],
                                             scale=1.0, scalar=0.0, op0=ALU.mult, op1=ALU.add,
                                             accum_out=lam_sum[:, n:n + 1]).then_inc(lam_done, 1)
                dve.tensor_scalar(sub_gain[:], v("subln"), 1.0 - LAM_INIT, None, ALU.mult)
                dve.wait_ge(c_done, 2)
                dve.scalar_tensor_tensor(out=neg_lam[:], in0=lam_exp[:, 1:2], scalar=-LAM_INIT, in1=lam_exp[:, 0:1],
                                         op0=ALU.add, op1=ALU.subtract).then_inc(lam_done, 1)
            lo(0)
            lo(1)
            for k in range(KD):
                dve.wait_ge(turned, k + 1)
                dve.tensor_copy(xT[:, k], psum[:, k % 4, :]).then_inc(x_ready, 1)
            dve.wait_ge(filled, 2)

            if first_block:
                zero_shift = lambda k: zero[:, 0:1]
                norm(0, plain("norm_mix"), zero_shift)
                s = seg["mix_in"]
                ns_count = [0]

                def ns(name, ins):
                    assert NS_DVE[ns_count[0]] == name, (name, NS_DVE[ns_count[0]])
                    ns_count[0] += 1
                    ins.then_inc(ns_dve, 1)

                def given(name):
                    dve.wait_ge(ns_pe, upto(NS_PE, name))

                def done(name):
                    dve.wait_ge(ns_act, upto(NS_ACT, name))

                def own(name):
                    dve.wait_ge(ns_dve, upto(NS_DVE, name))

                def mods(n):
                    if second_block and n in MIX_AT:
                        mod_group(MIX_AT[n])
                    if second_block and n in MIX_FINISH:
                        mod_finish(MIX_FINISH[n])

                dve.wait_ge(ns_in, 96)
                ns("pe", dve.tensor_copy(kx[:, :, :, NC], cpe[:]))
                for n in range(11):
                    dve.wait_ge(unit_done, s.first + n + 1)
                    src = bank(s.tile + n)
                    if n < 4:
                        ns(f"q{n}", dve.tensor_copy(q_n[:, n], src))
                    elif n < 6:
                        cut = src.rearrange("p (b l) -> p l b", l=CMP_STRIDE)
                        dve.tensor_copy(kx[:, n - 4, 0:CMP_STRIDE, 0:NC], cut[:, :, 0:NC])
                        ns("kv"[n - 4] + "x", dve.tensor_copy(kx[:, n - 4, CMP_STRIDE:CMP_BLOCK, 0:NC], cut[:, :, 1:NC + 1]))
                    elif n < 10:
                        name = ("ks", "vs", "kw", "vw")[n - 6]
                        ns(name, dve.tensor_copy(k_n[:, n // 2 - 3] if name[0] == "k" else raw_n[:, n // 2 - 3], src))
                    lo(s.first + n + 2)
                    mods(n)
                done("gl")
                ns("gl", dve.tensor_copy(gl[:], gl[:]))
                ns("gq", dve.tensor_scalar(gq[:], v("qk_gain", 0), HD ** -0.5, None, ALU.mult))
                done("std")
                ns("rec", dve.reciprocal(rec_n[:, 0:6].rearrange("p a t c -> p (a t c)"),
                                         stat_n[:, 0:6].rearrange("p a t c -> p (a t c)")))
                own("rec")
                for n in range(6):
                    if n >= 2:
                        given(f"rs{n - 2}")
                    ns(f"rexp{n}", dve.tensor_copy(rexp_n[:, n % 2].rearrange("p t (c d) -> p t c d", c=2),
                                                   rec_n[:, n].unsqueeze(3).to_broadcast([P, TT, 2, HD])))
                    given(f"rs{n}")
                    x = q_n[:, n] if n < 4 else k_n[:, n - 4]
                    gain = gq[:, 0:1] if n < 4 else v("qk_gain", 2 + n - 4)
                    ns(f"n{n}", dve.scalar_tensor_tensor(out=x, in0=x, scalar=gain, in1=psum[:, 4 + n % 2, :],
                                                         op0=ALU.mult, op1=ALU.mult))
                given("kc")
                ns("kc", dve.tensor_copy(kc_n[:, 0:NC], psum[:, 6, 0:NC]))
                given("vc")
                ns("vc", dve.tensor_copy(vc_t[:], psum[0:NC, 7, 0:P]))
                done("kcstd")
                ns("kcrec", dve.reciprocal(rec_n[0:NC, 6, 0], stat_n[0:NC, 6, 0]))
                own("kcrec")
                ns("kcrexp", dve.tensor_copy(rexp_n[0:NC, 0, 0].rearrange("p (c d) -> p c d", c=2),
                                             rec_n[0:NC, 6, 0].unsqueeze(2).to_broadcast([NC, 2, HD])))
                given("kcrs")
                ns("kcn", dve.scalar_tensor_tensor(out=kc_n[:, 0:NC], in0=kc_n[:, 0:NC], scalar=v("qk_gain", 1),
                                                   in1=psum[:, 5, 0:NC], op0=ALU.mult, op1=ALU.mult))
                for j in range(TT):
                    given(f"cs{j}")
                    pc = Pc[:, j, :, 0:NC]
                    over = lambda x: x.unsqueeze(1).to_broadcast([P, NSA_HEADS, NC])
                    along = lambda x: x.unsqueeze(2).to_broadcast([P, NSA_HEADS, NC])
                    ns(f"add{j}", dve.tensor_tensor(
                        Pc[:, j].rearrange("p (a b) n -> p a b n", b=2)[:, :, :, 0:NC],
                        psum[:, 2 * j:2 * j + 2, 0:P].rearrange("p b (a n) -> p a b n", n=32)[:, :, :, 0:NC],
                        cadd[:, j].unsqueeze(1).unsqueeze(1).to_broadcast([P, 4, 2, NC]), ALU.add))
                    own(f"add{j}")
                    ns(f"max{j}", dve.tensor_reduce(cmx[:], pc, AX.X, ALU.max))
                    own(f"max{j}")
                    ns(f"sub{j}", dve.tensor_tensor(pc, pc, along(cmx[:]), ALU.subtract))
                    done(f"ce{j}")
                    ns(f"sum{j}", dve.tensor_reduce(csum[:], pc, AX.X, ALU.add))
                    own(f"sum{j}")
                    ns(f"rec{j}", dve.reciprocal(csum[:], csum[:]))
                    own(f"rec{j}")
                    ns(f"coef{j}", dve.tensor_tensor(csum[:], csum[:], gate_t[:, j, 0:24:3], ALU.mult))
                    ns(f"mask{j}", dve.tensor_tensor(pc, pc, over(cmul[:, j]), ALU.mult))
                    own(f"mask{j}")
                    ns(f"p{j}", dve.tensor_tensor(pc, pc, along(csum[:]), ALU.mult))

                M = 4 * NSA_HEADS
                steps = 0
                for m in range(M + 3):
                    if m < M:
                        h, j = m // 4, m % 4
                        dve.wait_ge(nscore_done, m + 1)
                        if m >= 2:
                            dve.wait_ge(nexp_done, 2 * (m - 1))
                        two = psum[:, 2 * (m % 2):2 * (m % 2) + 2, :]
                        dve.tensor_tensor(two[:, :, j * P:(j + 1) * P], two[:, :, j * P:(j + 1) * P],
                                          tri[:].unsqueeze(1).to_broadcast([P, 2, P]), ALU.add).then_inc(nmask_done, 1)
                        dve.wait_ge(nmask_done, m + 1)
                        dve.tensor_reduce(nmax_n[:, m % 2], two[:, :, 0:(j + 1) * P], AX.X, ALU.max,
                                          negate=True).then_inc(nmax_done, 1)
                    if 1 <= m <= M:
                        g = m - 1
                        b, h, j = g % 2, g // 4, g % 4
                        dve.wait_ge(nexp_done, 2 * g + 2)
                        dve.reciprocal(coef_n[:, b], esum_n[:, b]).then_inc(nscale_step, 1)
                        dve.wait_ge(nscale_step, steps + 1)
                        dve.tensor_tensor(coef_n[:, b], coef_n[:, b], gate_t[:, j, 3 * h + 1:3 * h + 3],
                                          ALU.mult).then_inc(nscale_step, 1)
                        dve.wait_ge(nscale_step, steps + 2)
                        for c in range(2):
                            x = Pn[:, b, c, 0:(j + 1) * P]
                            dve.tensor_scalar(x, x, coef_n[:, b, c:c + 1], None, ALU.mult).then_inc(nscale_step, 1)
                        steps += 4
                    if m >= 6 and (m - 6) % 4 == 0 or m == M + 2:
                        h = (m - 6) // 4
                        rows = slice(HD * (h % 2), HD * (h % 2) + HD)
                        dve.wait_ge(npv_done, h + 1)
                        dve.tensor_copy(o_nsa[rows, h // 2], psum[rows, 6, :]).then_inc(no_done, 1)

                dve.memset(zraw[:, 0, 0:1], 0.0).then_inc(zset, 1)
                dve.memset(zraw[:, 1, 0:1], 0.0).then_inc(zset, 1)
                dve.memset(TR[:], 0.0).then_inc(zset, 1)
                dve.memset(MR[:], 0.0).then_inc(zset, 1)
                dve.memset(Sh[:, 0], 0.0).then_inc(zset, 1)
                for n in range(14):
                    dve.wait_ge(zraw_done, n + 1)
                    z = zraw[:, n % 2]
                    dve.tensor_tensor(zm[:, n], z[:, 0:S], z[:, 1:S + 1], ALU.subtract).then_inc(zdiff_done, 1)
                    lo(s.first + 11 + n + 2)
                    dve.wait_ge(zdiff_done, n + 1)
                    dve.scalar_tensor_tensor(out=zm[:, n], in0=zm[:, n], scalar=v("mu", n), in1=z[:, 1:S + 1],
                                             op0=ALU.mult, op1=ALU.add).then_inc(zm_done, 1)
                    mods(11 + n)
                dve.wait_ge(zset, 5)
                dve.wait_ge(rw_in, 64)
                dve.tensor_copy(mask8[:], AR[:].rearrange("p t a n -> p (t a n)")).then_inc(zset, 1)
                dve.wait_ge(zset, 6)

                rw_count = [0]

                def rw(name, ins):
                    assert RW_DVE[rw_count[0] % len(RW_DVE)] == name, (name, RW_DVE[rw_count[0] % len(RW_DVE)])
                    rw_count[0] += 1
                    ins.then_inc(rw_dve, 1)

                def tiles(x):
                    return x.rearrange("p (t n) -> p t n", t=TT)

                def chunks(x):
                    return x.rearrange("p (c n) -> p c n", c=NCH)

                for p in range(PAIRS):
                    def given(name):
                        dve.wait_ge(rw_pe, upto(RW_PE, name, p))

                    def done(name):
                        dve.wait_ge(rw_act, upto(RW_ACT, name, p))

                    def own(name):
                        dve.wait_ge(rw_dve, upto(RW_DVE, name, p))

                    def step(name, ins, wait=True):
                        rw(name, ins)
                        if wait:
                            own(name)

                    r, k, val = zm[:, p], zm[:, 4 + p], zm[:, 8 + p]
                    if p >= 1:
                        dve.wait_ge(rw_dve, upto(RW_DVE, "o", p - 1))
                    step("kk0", dve.tensor_scalar(tC[:], k, v("k_k", p), None, ALU.mult))
                    done("sw")
                    step("cs", dve.tensor_tensor_scan(Bt[:], rmask[:], tA[:], 0.0, ALU.mult, ALU.add))
                    step("rel", dve.tensor_tensor(chunks(Kt[:]), chunks(Bt[:]),
                                                  chunks(Bt[:])[:, :, CHUNK // 2 - 1:CHUNK // 2].to_broadcast([P, NCH, CHUNK]),
                                                  ALU.subtract))
                    given("kss")
                    step("relm", dve.tensor_tensor(tD[:], Kt[:], tA[:], ALU.subtract))
                    step("dsum", dve.tensor_tensor(Dc[:, 0:NCH - 1], chunks(Kt[:])[:, 0:NCH - 1, CHUNK - 1],
                                                   chunks(Bt[:])[:, 1:NCH, CHUNK // 2 - 1], ALU.add))
                    done("kstd")
                    step("kmax", dve.tensor_scalar(kst[:], kst[:], 1e-12, None, ALU.max))
                    step("krec", dve.reciprocal(krec[:], kst[:]))
                    step("krexp", dve.tensor_copy(X[:, 0:4].rearrange("p t (c d) -> p t c d", c=2),
                                                  krec[:].unsqueeze(3).to_broadcast([P, TT, 2, HD])))
                    given("krs")
                    step("kkn", dve.tensor_tensor(tC[:], tC[:], psum[:, 4, :], ALU.mult))
                    done("a")
                    step("a1", dve.tensor_scalar(tA[:], tB[:], -1.0, v("k_a", p), ALU.add, ALU.mult))
                    step("kh", dve.scalar_tensor_tensor(out=tA[:], in0=tA[:], scalar=1.0, in1=k, op0=ALU.add, op1=ALU.mult))
                    done("Em")
                    step("A", dve.scalar_tensor_tensor(out=AR[:, :, 0, :], in0=tiles(tC[:]), scalar=-1.0, in1=tiles(tD[:]),
                                                       op0=ALU.mult, op1=ALU.mult))
                    step("kka", dve.tensor_tensor(Bt[:], tC[:], tB[:], ALU.mult))
                    step("B", dve.tensor_tensor(Bt[:], Bt[:], Kt[:], ALU.mult))
                    step("K", dve.tensor_tensor(Kt[:], Kt[:], tA[:], ALU.mult))
                    step("R", dve.tensor_tensor(AR[:, :, 1, :], AR[:, :, 1, :], tiles(r), ALU.mult))
                    step("rk", dve.scalar_tensor_tensor(out=tB[:], in0=r, scalar=v("r_k", p), in1=tA[:], op0=ALU.mult, op1=ALU.mult))
                    given("bonus")
                    step("bonus", dve.tensor_tensor(tD[:], val, psum[:, 5, :], ALU.mult))
                    lower = stri.unsqueeze(1).to_broadcast([P, 2, 2 * P])

                    def keep_lower(name, dst, n, b):
                        given(name)
                        step(name, dve.copy_predicated(dst[:, 2 * n:2 * n + 2], lower,
                                                       psum[:, b, :].rearrange("p (m n) -> p m n", m=2)), wait=False)

                    for n in range(4):
                        keep_lower(f"P1{n}", TR, n, 2 + n)
                    own("P13")
                    step("eye", dve.tensor_copy(XT[:], ident.unsqueeze(1).to_broadcast([P, 8, P])))
                    step("XT0", dve.copy_predicated(XT[:], lmask[:, 0].unsqueeze(1).to_broadcast([P, 8, P]), TR[:, :, 0:P]),
                         wait=False)
                    for n in range(4):
                        keep_lower(f"P2{n}", MR, n, (6 + n) % 8)
                    for lev in range(1, 6):
                        mask = lmask[:, lev].unsqueeze(1).to_broadcast([P, 4, P])
                        for n in range(2):
                            name = f"Y{lev}" + "ab"[n]
                            given(name)
                            step(name, dve.copy_predicated(XT[:, 4 * n:4 * n + 4], mask,
                                                           psum[:, 4 + n, :].rearrange("p (m n) -> p m n", m=4)), wait=False)
                    given("WT")
                    WT = Ap[:, 0:4].rearrange("p m n -> p (m n)")
                    Ut = Ap[:, 4:8].rearrange("p m n -> p (m n)").rearrange("p (h t d) -> p h t d", h=2, t=TT)
                    U0 = X[:, 4:8].rearrange("p m n -> p (m n)").rearrange("p (h t d) -> p h t d", h=2, t=TT)
                    step("WT", dve.tensor_copy(WT, psum[:, 2, :]), wait=False)
                    done("U0")
                    for c in range(NCH):
                        t, q = c // 2, slice(CHUNK * (c % 2), CHUNK * (c % 2) + CHUNK)
                        if c < NCH - 1:
                            if c >= 1:
                                own(f"S{c - 1}")
                            step(f"SD{c}", dve.tensor_scalar(SD[:], Sh[:, c], Dc[:, c:c + 1], None, ALU.mult), wait=False)
                        given(f"u{c}")
                        step(f"U{c}", dve.tensor_tensor(Ut[q, :, t], U0[q, :, t],
                                                        psum[q, 3:5, 0:HD],
                                                        ALU.add), wait=False)
                        if c < NCH - 1:
                            own(f"SD{c}")
                            given(f"s{c}")
                            step(f"S{c}", dve.scalar_tensor_tensor(out=Sh[:, c + 1], in0=psum[:, 5 + c % 2, 0:HD],
                                                                   scalar=Dc[:, c:c + 1], in1=SD[:], op0=ALU.mult,
                                                                   op1=ALU.add), wait=False)
                    given("mean")
                    step("yc", dve.scalar_tensor_tensor(out=tC[:], in0=psum[:, 0, :], scalar=-1.0 / HD, in1=tA[:],
                                                        op0=ALU.mult, op1=ALU.add))
                    done("vstd")
                    step("vrec", dve.reciprocal(krec[:], kst[:]))
                    step("vrexp", dve.tensor_copy(X[:, 0:4].rearrange("p t (c d) -> p t c d", c=2),
                                                  krec[:].unsqueeze(3).to_broadcast([P, TT, 2, HD])))
                    given("vrs")
                    step("yn", dve.scalar_tensor_tensor(out=tC[:], in0=tC[:], scalar=v("ln_w", p), in1=psum[:, 2, :],
                                                        op0=ALU.mult, op1=ALU.mult))
                    step("yb", dve.scalar_tensor_tensor(out=tC[:], in0=tC[:], scalar=v("ln_b", p), in1=tD[:], op0=ALU.add,
                                                        op1=ALU.add))
                    step("o", dve.tensor_tensor(zm[:, p], tC[:], keep[:], ALU.mult), wait=False)

                dve.wait_ge(rw_dve, upto(RW_DVE, "o", PAIRS - 1))
                for k in range(KD):
                    dve.wait_ge(osplit_hi, k + 1)
                    dve.tensor_tensor(o_lo[:, k], o_nsa[:, k] if k < 4 else zm[:, k - 4], o_hi[:, k].bitcast(F32),
                                      ALU.subtract).then_inc(osplit_lo, 1)
                s = seg["merge"]
                for n in range(KD):
                    for j in range(4):
                        u = s.first + 4 * n + j
                        dve.wait_ge(unit_done, u + 1)
                        if j == 2:
                            dve.wait_ge(sig_done, 2 * n + 1)
                            if n >= 1:
                                dve.wait_ge(ylo_done, n)
                            dve.tensor_tensor(y_t, sg[:, 0], bank(s.tile + 4 * n + 2), ALU.mult).then_inc(y_step, 1)
                        if j == 3:
                            dve.wait_ge(sig_done, 2 * n + 2)
                            dve.tensor_tensor(sg[:, 1], sg[:, 1], bank(s.tile + 4 * n + 3), ALU.mult).then_inc(y_step, 1)
                            dve.wait_ge(y_step, 3 * n + 2)
                            dve.tensor_tensor(y_t, y_t, sg[:, 1], ALU.add).then_inc(y_step, 1)
                        lo(u + 2)
                    dve.wait_ge(yhi_done, n + 1)
                    dve.tensor_tensor(y_lo[:, n], y_t, y_hi[:, n].bitcast(F32), ALU.subtract).then_inc(ylo_done, 1)
                mixed_out("mix_out", one)
                norm(1, plain("norm_ffn"), zero_shift)
                up(0)
                down(0, one)

            if second_block:
                if not first_block:
                    for g in range(N_MOD_GROUPS):
                        mod_group(g)
                        if g == 17:
                            mod_vectors(0)
                    mod_vectors(1)
                else:
                    mod_vectors(0)

                def scale(layer, which):
                    return lambda k: scales[:, layer, which, k:k + 1]

                def shift(layer, which):
                    return lambda k: modv[:, layer, 24 * which + k:24 * which + k + 1]

                def gate(layer, which):
                    return lambda k: gates[:, layer, which, k:k + 1]

                dve.wait_ge(mod_vec, 1)
                norm(2, scale(0, 0), shift(0, 0))
                up(1)
                down(1, gate(0, 0))

                for b in range(2):
                    dve.memset(hp[:, b, 0:8], 0.0).then_inc(padded, 1)
                    dve.memset(hp[:, b, 8 + S:16 + S], 0.0).then_inc(padded, 1)
                dve.wait_ge(std_done, NORM[3] + 1)
                dve.reciprocal(rstd[:], std[:]).then_inc(rstd_done, 1)
                dve.wait_ge(rstd_done, NORM[3] + 1)
                for tt in range(TT):
                    i = dve.tensor_scalar(rdiag[:, 0, tt], ident, rstd[:, tt:tt + 1], None, ALU.mult)
                i.then_inc(rdiag_done, 1)
                dve.wait_ge(rbc_done, NORM[3] + 1)
                dve.wait_ge(tables, 64)
                steps = 0

                def normed(k):
                    if k >= 2:
                        dve.wait_ge(hhi_done, KD * NORM[3] + k - 1)
                    dve.scalar_tensor_tensor(out=norm_t[:, k % 2], in0=xT[:, k], scalar=scale(0, 1)(k),
                                             in1=psum[:, 5, :], op0=ALU.mult, op1=ALU.mult).then_inc(t_done, 1)

                def low(k):
                    dve.wait_ge(diff_hi, k + 1)
                    dve.tensor_tensor(h_lo[:, k], diff[:, k % 2], h_hi[:, k].bitcast(F32),
                                      ALU.subtract).then_inc(hlo_done, 1)

                normed(0)
                for k in range(KD):
                    if k + 1 < KD:
                        normed(k + 1)
                    dve.wait_ge(hhi_done, KD * NORM[3] + k + 1)
                    doublings = k // 2 + 1
                    src, at, end = hp[:, k % 2], 0, S + 16
                    for d in range(doublings):
                        left, right = (1, 0) if d == 0 else (2 ** (d - 1), 2 ** (d - 1))
                        a, b = at + left, end - right
                        dst = win[:, k % 2, d]
                        dve.tensor_tensor(dst[:, a:b], src[:, a - left:b - left], src[:, a + right:b + right],
                                          ALU.add).then_inc(win_done, 1)
                        steps += 1
                        dve.wait_ge(win_done, steps)
                        src, at, end = dst, a, b
                    dve.tensor_tensor(src[:, 8:8 + S], src[:, 8:8 + S], icnt[:, doublings - 1], ALU.mult)\
                        .then_inc(win_done, 1)
                    steps += 1
                    dve.wait_ge(win_done, steps)
                    dve.tensor_tensor(diff[:, k % 2], src[:, 8:8 + S], hp[:, k % 2, 8:8 + S],
                                      ALU.subtract).then_inc(diff_done, 1)
                    if k >= 1:
                        low(k - 1)
                low(KD - 1)
                mixed_out("pool", gate(0, 1))
                norm(4, scale(0, 2), shift(0, 2))
                up(2)
                down(2, gate(0, 2))
                if first_block:
                    mod_vectors(1)
                dve.wait_ge(mod_vec, 2)
                norm(5, scale(1, 0), shift(1, 0))
                up(3)
                down(3, gate(1, 0))
                norm(6, scale(1, 1), shift(1, 1))

                s = seg["qkv"]
                dve.wait_ge(tables, 80)
                rope_step = 0
                for n in range(25):
                    if n < 24:
                        dve.wait_ge(unit_done, s.first + n + 1)
                        if n >= 10:
                            dve.wait_ge(roped, 3 * (n - 9))
                        dve.tensor_copy(raw[:, n % 2], bank(s.tile + n)).then_inc(raw_done, 1)
                        lo(s.first + n + 2)
                    if n >= 9:
                        m = n - 1
                        dst = (k_t if m < 16 else q_t)[:, m % 8]
                        by = 1.0 if m < 16 else HD ** -0.5
                        dve.wait_ge(post_done, n)
                        dve.wait_ge(raw_done, n)
                        dve.scalar_tensor_tensor(out=dst, in0=psum[:, 4 + m % 2, :], scalar=by, in1=rope[:, 1],
                                                 op0=ALU.mult, op1=ALU.mult).then_inc(roped, 1)
                        dve.scalar_tensor_tensor(out=raw[:, m % 2], in0=raw[:, m % 2], scalar=by, in1=rope[:, 0],
                                                 op0=ALU.mult, op1=ALU.mult).then_inc(roped, 1)
                        rope_step += 2
                        dve.wait_ge(roped, rope_step)
                        dve.tensor_tensor(dst, dst, raw[:, m % 2], ALU.add).then_inc(roped, 1)
                        rope_step += 1

                steps = 0
                M = 4 * DIFF_HEADS
                for m in range(M + 3):
                    if m < M:
                        dve.wait_ge(score_done, m + 1)
                        if m >= 2:
                            dve.wait_ge(exp_done, 2 * (m - 1))
                        dve.tensor_reduce(nmax[:, m % 2], psum[:, 2 * (m % 2):2 * (m % 2) + 2, :], AX.X, ALU.max,
                                          negate=True).then_inc(max_done, 1)
                    if 1 <= m <= M:
                        g = m - 1
                        b = g % 2
                        dve.wait_ge(exp_done, 2 * g + 2)
                        dve.reciprocal(coef[:, b], esum[:, b]).then_inc(comb_step, 1)
                        dve.wait_ge(comb_step, steps + 1)
                        dve.tensor_scalar(E[:, b, 1], E[:, b, 1], coef[:, b, 1:2], neg_lam[:, 0:1], ALU.mult,
                                          ALU.mult).then_inc(comb_step, 1)
                        dve.wait_ge(comb_step, steps + 2)
                        dve.scalar_tensor_tensor(out=E[:, b, 0], in0=E[:, b, 0], scalar=coef[:, b, 0:1], in1=E[:, b, 1],
                                                 op0=ALU.mult, op1=ALU.add).then_inc(comb_step, 1)
                        steps += 3
                    if m >= 6 and (m - 6) % 4 == 0 or m == M + 2:
                        h = (m - 6) // 4
                        dve.wait_ge(pv_done, h + 1)
                        dve.tensor_copy(o_raw[:, h], psum[:, 6, :]).then_inc(o_done, 1)
                dve.wait_ge(ostd_done, 1)
                dve.reciprocal(orstd[:], ostd[:]).then_inc(orstd_done, 1)
                dve.wait_ge(orstd_done, 1)
                for h in range(DIFF_HEADS + 2):
                    if h < DIFF_HEADS:
                        if h >= 2:
                            dve.wait_ge(obc_done, h - 1)
                        for tt in range(TT):
                            i = dve.tensor_scalar(rdiag[:, h % 2, tt], ident, orstd[:, 4 * h + tt:4 * h + tt + 1],
                                                  None, ALU.mult)
                        i.then_inc(odiag_done, 1)
                    if 1 <= h <= DIFF_HEADS:
                        g = h - 1
                        dve.wait_ge(obc_done, g + 1)
                        if g >= 2:
                            dve.wait_ge(olo_done, g - 1)
                        dve.scalar_tensor_tensor(out=norm_t[:, g % 2], in0=o_raw[:, g], scalar=sub_gain[:, 0:1],
                                                 in1=psum[:, 5 + g % 2, :], op0=ALU.mult,
                                                 op1=ALU.mult).then_inc(ot_done, 1)
                    if h >= 2:
                        g = h - 2
                        dve.wait_ge(ohi_done, g + 1)
                        dve.tensor_tensor(h_lo[:, g], norm_t[:, g % 2], h_hi[:, g].bitcast(F32),
                                          ALU.subtract).then_inc(olo_done, 1)
                mixed_out("attn_out", gate(1, 1))
                norm(7, scale(1, 2), shift(1, 2))
                up(4)
                down(4, gate(1, 2))

            n_norm = last_norm
            dve.wait_ge(std_done, NORM[n_norm] + 1)
            dve.reciprocal(rstd[:], std[:]).then_inc(rstd_done, 1)
            dve.wait_ge(rstd_done, NORM[n_norm] + 1)
            for tt in range(TT):
                i = dve.tensor_scalar(rdiag[:, 0, tt], ident, rstd[:, tt:tt + 1], None, ALU.mult)
            i.then_inc(rdiag_done, 1)
            dve.wait_ge(rbc_done, NORM[n_norm] + 1)
            for k in range(KD):
                if k >= 2:
                    dve.wait_ge(xt_done, k - 1)
                dve.scalar_tensor_tensor(out=y_out[:, k % 2], in0=xT[:, k], scalar=v("final_g", k),
                                         in1=psum[:, 5, :], op0=ALU.mult, op1=ALU.mult).then_inc(t_done, 1)

        @block.tensor
        def _(pe):
            def product(c, i, k_tiles, acts, tile, start, stop):
                c, i = fixed(c, i)
                kt, cols = shape_of(c)
                pe.wait_ge(lo_done, c + 4 * i + 1)
                wh, wl = slot(w_hi, c, kt, cols, 2), slot(w_lo, c, kt, cols, 2)
                a_hi, a_lo = acts
                dst = bank(tile)[0:cols, :]
                for n, k in enumerate(k_tiles):
                    pe.matmul(dst, wh[:, n], a_hi[:, k], start=start and n == 0, stop=False)
                    pe.matmul(dst, wh[:, n], a_lo[:, k], start=False, stop=False)
                    m = pe.matmul(dst, wl[:, n], a_hi[:, k], start=False, stop=stop and n == kt - 1)
                m.then_inc(unit_done, 1)

            def sum_squares(n_norm, k):
                pe.wait_ge(sq_done, KD * NORM[n_norm] + k + 1)
                for tt in range(TT):
                    m = pe.matmul(psum[:, 4, tt:tt + 1], sq[:, k % 2, tt * P:(tt + 1) * P], ones[:, 0:1],
                                  start=(k == 0 and tt == 0), stop=(k == KD - 1), skip_group_check=True)
                m.then_inc(ssq_done, 1)

            def spread_rstd(n_norm):
                pe.wait_ge(rdiag_done, NORM[n_norm] + 1)
                for tt in range(TT):
                    m = pe.matmul(psum[:, 5, tt * P:(tt + 1) * P], ones, rdiag[:, 0, tt], start=True, stop=True)
                m.then_inc(rbc_done, 1)

            def mod_product(g):
                pe.wait_ge(mod_mul, 8 * (g + 1))
                for j in range(4):
                    m = pe.matmul(psum[:, 7, j:j + 1], mod_acc[:, j * P:(j + 1) * P], ones[:, 0:1],
                                  start=True, stop=True)
                m.then_inc(mod_sum, 1)

            def up(f, n_norm):
                s, pairs = seg[f"up{f}"], PAIR[f]

                def body(i, mod):
                    if mod and not (isinstance(i, int) and MOD_FIRST[f] + i in FRESH):
                        mod_product(MOD_FIRST[f] + i - 1)
                    for j in range(4):
                        if isinstance(i, int) and i == 0 and j == 0:
                            pass
                        elif isinstance(i, int) and i == 0:
                            pe.wait_ge(hlo_done, KD * (NORM[n_norm] + 1))
                        if not (isinstance(i, int) and i == 0):
                            pe.wait_ge(hid_done, pairs + 2 * i - 1 + j // 2)
                        if isinstance(i, int) and i == 0 and j == 0:
                            first_unit(s, n_norm)
                        else:
                            product(s.first + j, i, range(KD), (h_hi, h_lo), s.tile + j, True, True)

                for start, count, mod in UP_RUNS[f]:
                    repeat(pe, start, count, lambda i: body(i, mod and second_block))

            def first_unit(s, n_norm):
                c = s.first
                kt, cols = shape_of(c)
                pe.wait_ge(lo_done, c + 1)
                wh, wl = slot(w_hi, c, kt, cols, 2), slot(w_lo, c, kt, cols, 2)
                for k in range(KD):
                    pe.wait_ge(hlo_done, KD * NORM[n_norm] + k + 1)
                    pe.matmul(bank(s.tile), wh[:, k], h_hi[:, k], start=k == 0, stop=False)
                    pe.matmul(bank(s.tile), wh[:, k], h_lo[:, k], start=False, stop=False)
                    m = pe.matmul(bank(s.tile), wl[:, k], h_hi[:, k], start=False, stop=k == KD - 1)
                m.then_inc(unit_done, 1)

            def down(f, n_norm):
                s, pairs = seg[f"down{f}"], PAIR[f]
                for n in range(KD):
                    if n < 4:
                        pe.wait_ge(hid_done, pairs + KF)
                    else:
                        pe.wait_ge(x_ready, KD * NORM[n_norm] + n - 3)
                    for j, (k0, kt) in enumerate(DOWN):
                        pe.wait_ge(hidlo_done, pairs + k0 + kt)
                        product(s.first + 3 * n + j, 0, range(k0, k0 + kt), (hid_hi, hid_lo), s.tile + n, j == 0, j == 2)
                    if n >= 1:
                        sum_squares(n_norm, n - 1)
                sum_squares(n_norm, KD - 1)

            def mixed_out(name, n_norm, operands):
                s = seg[name]
                for n in range(KD):
                    if n >= 4:
                        pe.wait_ge(x_ready, KD * NORM[n_norm] + n - 3)
                    operands(n)
                    if n >= 1:
                        sum_squares(n_norm, n - 1)
                sum_squares(n_norm, KD - 1)

            pe.wait_ge(tables, 48 if second_block else 32)
            pe.wait_ge(x_in, 16)
            for k in range(KD):
                if k >= 4:
                    pe.wait_ge(x_ready, k - 3)
                for tt in range(TT):
                    m = pe.transpose(psum[:, k % 4, tt * P:(tt + 1) * P], x_tok[:, tt, k * P:(k + 1) * P], ident)
                m.then_inc(turned, 1)
            for k in range(KD):
                sum_squares(0 if first_block else 2, k)

            if first_block:
                spread_rstd(0)
                s = seg["mix_in"]
                ns_count = [0]

                def ns(name, last):
                    assert NS_PE[ns_count[0]] == name, (name, NS_PE[ns_count[0]])
                    ns_count[0] += 1
                    last.then_inc(ns_pe, 1)

                def took(name):
                    pe.wait_ge(ns_act, upto(NS_ACT, name))

                def made(name):
                    pe.wait_ge(ns_dve, upto(NS_DVE, name))

                def turn(dst, src, rows=P):
                    for t in range(TT):
                        last = pe.transpose(dst[:, t], src[:, t * P:(t + 1) * P], ident[0:rows, 0:rows])
                    return last

                def cols_of(b, n=P):
                    return psum[:, b, 0:TT * n].rearrange("p (t n) -> p t n", t=TT)

                evac = ["q0", "q1", "q2", "q3", "kx", "vx", "ks", "vs", "kw", "vw"]
                for n in range(11):
                    if n >= 4:
                        made(evac[n - 4])
                    if n == 0:
                        first_unit(s, 0)
                    else:
                        product(s.first + n, 0, range(KD), (h_hi, h_lo), s.tile + n, True, True)
                    if second_block and n in MIX_SUM:
                        mod_product(MIX_SUM[n])
                made("vs")
                ns("vs", turn(cols_of(4), raw_n[:, 0]))
                made("vw")
                ns("vw", turn(cols_of(5), raw_n[:, 1]))
                made("gl")
                ns("gt", turn(cols_of(6, 24), gl, 24))
                head_of = pair_ones[:, 0:P:HD]
                for n in range(6):
                    took(f"sq{n}")
                    for t in range(TT):
                        c = 8 + 8 * n + 2 * t
                        last = pe.matmul(psum[:, 7, c:c + 2], raw_n[:, n % 2, t * P:(t + 1) * P], head_of,
                                         start=True, stop=True)
                    ns(f"ss{n}", last)
                for n in range(6):
                    made(f"rexp{n}")
                    if n >= 2:
                        made(f"n{n - 2}")
                    for t in range(TT):
                        last = pe.transpose(psum[:, 4 + n % 2, t * P:(t + 1) * P], rexp_n[:, n % 2, t], ident)
                    ns(f"rs{n}", last)
                made("n5")
                for c in range(2):
                    for place in range(CMP_BLOCK):
                        last = pe.matmul(psum[:, 4 + c, 0:32], w1_c[:, c, place], kx[:, c, place], start=place == 0,
                                         stop=place == CMP_BLOCK - 1)
                    ns(f"c{c}", last)
                took("h0")
                ns("kc", pe.matmul(psum[:, 6, 0:NC], w2_c[:, 0], hid_c[:, 0, 0:NC], start=True, stop=True))
                took("h1")
                ns("vc", pe.matmul(psum[0:NC, 7, 0:P], hid_c[:, 1, 0:NC], w2_c[:, 1], start=True, stop=True))
                took("kcsq")
                ns("kcss", pe.matmul(psum[0:NC, 4, 0:2], raw_n[:, 0, 0:NC], head_of, start=True, stop=True))
                made("kcrexp")
                ns("kcrs", pe.transpose(psum[:, 5, 0:NC], rexp_n[0:NC, 0, 0], ident[0:NC, 0:NC]))
                took("kcd3")
                for j in range(TT):
                    for h in range(NSA_HEADS):
                        rows = slice(HD * (h % 2), HD * (h % 2) + HD)
                        c = 32 * (h // 2)
                        last = pe.matmul(psum[:, 2 * j + h % 2, c:c + NC], q_n[rows, h // 2, j * P:(j + 1) * P],
                                         kcd[rows, h // 4, 0:NC], start=True, stop=True)
                    ns(f"cs{j}", last)

                took(f"ce{TT - 1}")
                made(f"p{TT - 1}")
                M = 4 * NSA_HEADS

                def weigh_n(h):
                    rows = slice(HD * (h % 2), HD * (h % 2) + HD)
                    g = slice(HD * (h // 4), HD * (h // 4) + HD)
                    pe.wait_ge(npt_done, 12 * (h + 1))
                    if h >= 1:
                        pe.wait_ge(no_done, h)
                    pe.matmul(psum[rows, 6, :], vc_t[:, g], PTc[:, h % 2], start=True, stop=False)
                    for c in range(2):
                        for kt in range(TT):
                            last = pe.matmul(psum[rows, 6, kt * P:S], v_nt[:, c, kt, g], PTn[:, h % 2, c, kt, kt * P:S],
                                             start=False, stop=c == 1 and kt == TT - 1)
                    last.then_inc(npv_done, 1)

                for m in range(M + 2):
                    if m < M:
                        h, j = m // 4, m % 4
                        rows = slice(HD * (h % 2), HD * (h % 2) + HD)
                        if m >= 2:
                            pe.wait_ge(nexp_done, 2 * (m - 1))
                        for c in range(2):
                            last = pe.matmul(psum[:, 2 * (m % 2) + c, 0:(j + 1) * P], q_n[rows, h // 2, j * P:(j + 1) * P],
                                             kd[rows, c, h // 4, 0:(j + 1) * P], start=True, stop=True)
                        last.then_inc(nscore_done, 1)
                    if m >= 2:
                        g = m - 2
                        h, j = g // 4, g % 4
                        pe.wait_ge(nscale_step, 4 * (g + 1))
                        if g >= 1:
                            pe.wait_ge(npt_done, 3 * g)
                        pe.transpose(psum[0:NC, 7, 0:P], Pc[:, j, h, 0:NC], ident)
                        for c in range(2):
                            for kt in range(j + 1):
                                last = pe.transpose(psum[:, 4 + c, kt * P:(kt + 1) * P],
                                                    Pn[:, g % 2, c, kt * P:(kt + 1) * P], ident)
                        last.then_inc(nturned, 1)
                    if m >= 6 and (m - 6) % 4 == 0:
                        weigh_n((m - 6) // 4)
                weigh_n(NSA_HEADS - 1)

                for n in range(14):
                    if n >= 4:
                        pe.wait_ge(zraw_done, n - 3)
                    product(s.first + 11 + n, 0, range(KD), (h_hi, h_lo), s.tile + 11 + n, True, True)
                    if second_block and 11 + n in MIX_SUM:
                        mod_product(MIX_SUM[11 + n])
                pe.wait_ge(zact_done, 2)
                pe.wait_ge(rw_in, 64)
                if second_block:
                    pe.wait_ge(mod_out, MIX_GROUPS)

                rw_count = [0]

                def rw(name, last):
                    assert RW_PE[rw_count[0] % len(RW_PE)] == name, (name, RW_PE[rw_count[0] % len(RW_PE)])
                    rw_count[0] += 1
                    last.then_inc(rw_pe, 1)

                for p in range(PAIRS):
                    def took(name):
                        pe.wait_ge(rw_act, upto(RW_ACT, name, p))

                    def made(name):
                        pe.wait_ge(rw_dve, upto(RW_DVE, name, p))

                    cols = slice(p * P, (p + 1) * P)
                    if p >= 1:
                        pe.wait_ge(rw_dve, upto(RW_DVE, "o", p - 1))
                    rw("w", pe.matmul(psum[:, 0, :], low_up[0:HD, cols], zm[0:HD, 12], start=True, stop=True))
                    rw("a", pe.matmul(psum[:, 1, :], low_up[HD:P, cols], zm[HD:P, 12], start=True, stop=True))
                    rw("g", pe.matmul(psum[:, 2, :], g_up[:, cols], zm[:, 13], start=True, stop=True))
                    took("kkq")
                    for t in range(TT):
                        last = pe.matmul(psum[:, 3, 2 * t:2 * t + 2], tD[:, t * P:(t + 1) * P], head_of, start=True, stop=True)
                    rw("kss", last)
                    made("krexp")
                    for t in range(TT):
                        last = pe.transpose(psum[:, 4, t * P:(t + 1) * P], X[:, t], ident)
                    rw("krs", last)
                    made("rk")
                    rw("bonus", pe.matmul(psum[:, 5, :], pair_ones, tB[:], start=True, stop=True))
                    srcs = [lambda t: AR[:, t, 0, :], lambda t: Bt[:, t * P:(t + 1) * P], lambda t: Kt[:, t * P:(t + 1) * P],
                            lambda t: zm[:, 8 + p, t * P:(t + 1) * P]]
                    for n, name in enumerate(("tokA", "tokB", "tokK", "tokV")):
                        if n >= 2:
                            took(("sw", "a")[n - 2])
                        for t in range(TT):
                            last = pe.transpose(psum[:, (6 + n) % 8, t * P:(t + 1) * P], srcs[n](t), ident)
                        rw(name, last)
                    made("bonus")
                    took("g")
                    for which, src in enumerate((Bt, Kt)):
                        for n in range(4):
                            b = 2 + n if which == 0 else (6 + n) % 8
                            if which == 1:
                                took(("tokA", "tokB", "tokK", "tokV")[n])
                            for m in (2 * n, 2 * n + 1):
                                rows, t = slice(HD * (m // 4), HD * (m // 4) + HD), m % 4
                                last = pe.matmul(psum[:, b, (m % 2) * 2 * P:(m % 2 + 1) * 2 * P], src[rows, t * P:(t + 1) * P],
                                                 AR[rows, t].rearrange("p a n -> p (a n)"), start=True, stop=True)
                            rw(f"P{which + 1}{n}", last)

                    def each(n, b, f):
                        for m in range(4 * n, 4 * n + 4):
                            last = f(psum[:, b, (m % 4) * P:(m % 4 + 1) * P], m)
                        return last

                    made("P21")
                    made("XT0")
                    for n in range(2):
                        rw("X0" + "ab"[n], each(n, 6 + n, lambda dst, m: pe.transpose(dst, XT[:, m], ident)))
                    for lev in range(1, 6):
                        for n in range(2):
                            took(f"X{lev - 1}" + "ab"[n])
                            rw(f"A{lev}" + "ab"[n], each(n, 2 + n, lambda dst, m: pe.matmul(
                                dst, TR[:, m, 0:P], X[:, m], start=True, stop=True)))
                        for n in range(2):
                            took(f"A{lev}" + "ab"[n])
                            rw(f"Y{lev}" + "ab"[n], each(n, 4 + n, lambda dst, m: pe.matmul(
                                dst, Ap[:, m], XT[:, m], start=True, stop=True)))
                        if lev < 5:
                            for n in range(2):
                                made(f"Y{lev}" + "ab"[n])
                                rw(f"X{lev}" + "ab"[n], each(n, 6 + n, lambda dst, m: pe.transpose(dst, XT[:, m], ident)))
                    MV = X[:, 0:4].rearrange("p m n -> p (m n)")
                    made("Y5b")
                    for m in range(8):
                        t, hd = m % 4, slice(HD * (m // 4), HD * (m // 4) + HD)
                        last = pe.matmul(psum[:, 0, HD * m:HD * m + HD], MR[:, m, 0:P], tok[:, 3, t, hd], start=True, stop=True)
                    rw("MV", last)
                    took("MV")
                    for m in range(8):
                        last = pe.matmul(psum[:, 1, HD * m:HD * m + HD], XT[:, m], MV[:, HD * m:HD * m + HD], start=True, stop=True)
                    rw("U0", last)
                    for m in range(8):
                        t, hd = m % 4, slice(HD * (m // 4), HD * (m // 4) + HD)
                        last = pe.matmul(psum[hd, 2, t * P:(t + 1) * P], tok[:, 0, t, hd], XT[:, m], start=True, stop=True)
                    rw("WT", last)
                    made("WT")
                    WT = Ap[:, 0:4].rearrange("p m n -> p (m n)")
                    Ut = Ap[:, 4:8].rearrange("p m n -> p (m n)").rearrange("p (h t d) -> p h t d", h=2, t=TT)
                    for c in range(NCH):
                        t, q = c // 2, slice(CHUNK * (c % 2), CHUNK * (c % 2) + CHUNK)
                        if c >= 1:
                            made(f"S{c - 1}")
                        for hb in range(2):
                            hd = slice(HD * hb, HD * hb + HD)
                            last = pe.matmul(psum[q, 3 + hb, 0:HD], WT[hd, CHUNK * c:CHUNK * c + CHUNK], Sh[hd, c],
                                             start=True, stop=True)
                        rw(f"u{c}", last)
                        if c < NCH - 1:
                            made(f"U{c}")
                            for hb in range(2):
                                hd = slice(HD * hb, HD * hb + HD)
                                pe.matmul(psum[hd, 5 + c % 2, 0:HD], tok[q, 2, t, hd], tok[q, 3, t, hd], start=True, stop=False)
                                last = pe.matmul(psum[hd, 5 + c % 2, 0:HD], tok[q, 1, t, hd], Ut[q, hb, t], start=False, stop=True)
                            rw(f"s{c}", last)
                    made(f"U{NCH - 1}")
                    for hb in range(2):
                        hd = slice(HD * hb, HD * hb + HD)
                        for t in range(TT):
                            m = 4 * hb + t
                            dst = psum[hd, 7, t * P:(t + 1) * P]
                            pe.matmul(dst, Ut[:, hb, t], TR[:, m, P:2 * P], start=True, stop=False)
                            pe.matmul(dst, tok[:, 3, t, hd], MR[:, m, P:2 * P], start=False, stop=False)
                            for q in range(2):
                                part = psum[hd, 7, t * P + CHUNK * q:t * P + CHUNK * q + CHUNK]
                                last = pe.matmul(part, Sh[hd, 2 * t + q], AR[hd, t, 1, CHUNK * q:CHUNK * q + CHUNK],
                                                 start=False, stop=q == 1)
                    rw("y", last)
                    took("y")
                    rw("mean", pe.matmul(psum[:, 0, :], pair_ones, tA[:], start=True, stop=True))
                    took("ysq")
                    for t in range(TT):
                        last = pe.matmul(psum[:, 1, 2 * t:2 * t + 2], tB[:, t * P:(t + 1) * P], head_of, start=True, stop=True)
                    rw("vss", last)
                    made("vrexp")
                    for t in range(TT):
                        last = pe.transpose(psum[:, 2, t * P:(t + 1) * P], X[:, t], ident)
                    rw("vrs", last)
                pe.wait_ge(rw_dve, upto(RW_DVE, "o", PAIRS - 1))

                s = seg["merge"]
                for n in range(KD):
                    for j in range(4):
                        tile = s.tile + 4 * n + j
                        if n >= 1:
                            pe.wait_ge(y_step, 3 * n if j >= 2 else 3 * n - 2)
                        if j < 2:
                            product(s.first + 4 * n + j, 0, range(KD), (h_hi, h_lo), tile, True, True)
                        else:
                            pe.wait_ge(osplit_lo, 4 * (j - 1))
                            product(s.first + 4 * n + j, 0, range(4 * (j - 2), 4 * (j - 1)), (o_hi, o_lo), tile, True, True)

                def y_unit(n):
                    if n == 0:
                        pe.wait_ge(ylo_done, KD)
                    product(seg["mix_out"].first + n, 0, range(KD), (y_hi, y_lo), seg["mix_out"].tile + n, True, True)

                mixed_out("mix_out", 1, y_unit)
                spread_rstd(1)
                up(0, 1)
                if second_block:
                    mod_product(MOD_GROUPS_LAYER - 1)
                down(0, 2 if second_block else 8)

            if second_block:
                if not first_block:
                    for g in range(N_MOD_GROUPS):
                        mod_product(g)
                spread_rstd(2)
                up(1, 2)
                down(1, 3)
                spread_rstd(3)

                def pool_units(n):
                    if n == 0:
                        pe.wait_ge(hlo_done, KD * NORM[3] + 2)
                    if n % 2 == 0:
                        pe.wait_ge(hlo_done, KD * NORM[3] + 2 * (n // 2) + 2)
                    product(seg["pool"].first + n, 0, [2 * (n // 2), 2 * (n // 2) + 1], (h_hi, h_lo),
                            seg["pool"].tile + n, True, True)

                mixed_out("pool", 4, pool_units)
                spread_rstd(4)
                up(2, 4)
                if first_block:
                    mod_product(N_MOD_GROUPS - 1)
                down(2, 5)
                spread_rstd(5)
                up(3, 5)
                down(3, 6)
                spread_rstd(6)

                s = seg["qkv"]
                for n in range(25):
                    if n < 24:
                        if n >= 4:
                            pe.wait_ge(raw_done, n - 3)
                        if n == 0:
                            first_unit(s, 6)
                        else:
                            product(s.first + n, 0, range(KD), (h_hi, h_lo), s.tile + n, True, True)
                    if n >= 1:
                        m = n - 1
                        pe.wait_ge(raw_done, m + 1)
                        if m >= 10:
                            pe.wait_ge(roped, 3 * (m - 9))
                        elif m >= 2:
                            pe.wait_ge(vtok_done, min(m - 1, 8))
                        if m < 8:
                            for tt in range(TT):
                                last = pe.transpose(psum[:, 4 + m % 2, tt * P:(tt + 1) * P],
                                                    raw[:, m % 2, tt * P:(tt + 1) * P], ident)
                        else:
                            last = pe.matmul(psum[:, 4 + m % 2, :], perm, raw[:, m % 2], start=True, stop=True)
                        last.then_inc(post_done, 1)

                pe.wait_ge(roped, 48)
                pe.wait_ge(vtok_done, 8)
                M = 4 * DIFF_HEADS

                def weigh(h):
                    pe.wait_ge(pt_done, 4 * h + 4)
                    if h >= 1:
                        pe.wait_ge(o_done, h)
                    for kt in range(TT):
                        m = pe.matmul(psum[:, 6, :], v_tok[:, kt, h * P:(h + 1) * P], PT[:, h % 2, kt],
                                      start=kt == 0, stop=kt == TT - 1)
                    m.then_inc(pv_done, 1)

                for m in range(M + 2):
                    if m < M:
                        h, j = m // 4, m % 4
                        if m >= 2:
                            pe.wait_ge(exp_done, 2 * (m - 1))
                        for c in range(2):
                            rows = slice(HD * c, HD * c + HD)
                            last = pe.matmul(psum[:, 2 * (m % 2) + c, :], q_t[rows, h, j * P:(j + 1) * P],
                                             k_t[rows, h, :], start=True, stop=True)
                        last.then_inc(score_done, 1)
                    if m >= 2:
                        g = m - 2
                        pe.wait_ge(comb_step, 3 * (g + 1))
                        if g >= 2:
                            pe.wait_ge(pt_done, g - 1)
                        for kt in range(TT):
                            last = pe.transpose(psum[:, 4 + g % 2, kt * P:(kt + 1) * P],
                                                E[:, g % 2, 0, kt * P:(kt + 1) * P], ident)
                        last.then_inc(a_turned, 1)
                    if m >= 6 and (m - 6) % 4 == 0:
                        weigh((m - 6) // 4)
                weigh(DIFF_HEADS - 1)
                for h in range(DIFF_HEADS):
                    pe.wait_ge(osq_done, h + 1)
                    for tt in range(TT):
                        last = pe.matmul(psum[:, 4, 4 * h + tt:4 * h + tt + 1], sq[:, h % 2, tt * P:(tt + 1) * P],
                                         ones[:, 0:1], start=True, stop=True)
                    last.then_inc(ossq_done, 1)
                for h in range(DIFF_HEADS):
                    pe.wait_ge(odiag_done, h + 1)
                    if h >= 2:
                        pe.wait_ge(ot_done, h - 1)
                    for tt in range(TT):
                        last = pe.matmul(psum[:, 5 + h % 2, tt * P:(tt + 1) * P], ones, rdiag[:, h % 2, tt],
                                         start=True, stop=True)
                    last.then_inc(obc_done, 1)
                pe.wait_ge(olo_done, DIFF_HEADS)
                mixed_out("attn_out", 7, lambda n: product(seg["attn_out"].first + n, 0, range(KD), (h_hi, h_lo),
                                                          seg["attn_out"].tile + n, True, True))
                spread_rstd(7)
                up(4, 7)
                down(4, 8)

            spread_rstd(last_norm)
            base = KD * NORM[last_norm]
            for k in range(KD):
                pe.wait_ge(t_done, base + k + 1)
                if k >= 4:
                    pe.wait_ge(out_copied, k - 3)
                for tt in range(TT):
                    m = pe.transpose(psum[:, k % 4, tt * P:(tt + 1) * P], y_out[:, k % 2, tt * P:(tt + 1) * P], ident)
                m.then_inc(xt_done, 1)


def units_of(w, kt):
    k, n = w.shape
    return np.ascontiguousarray(w.reshape(kt, P, n // P, P).transpose(2, 1, 0, 3)).reshape(n // P, P, kt * P)


def columns(x):
    return np.ascontiguousarray(np.asarray(x).reshape(-1, P).T)


def constants():
    eye = np.eye(P, dtype=np.float32)
    pair = np.kron(np.eye(2, dtype=np.float32), np.ones((HD, HD), np.float32))
    perm = np.zeros((P, P), np.float32)
    rot = HD // 4
    half = rot // 2
    for h in range(2):
        for r in range(half):
            perm[HD * h + half + r, HD * h + r] = -1.0
            perm[HD * h + r, HD * h + half + r] = 1.0
    cst = np.concatenate([eye, np.ones((P, P), np.float32), pair, perm], axis=1)
    inv = (1.0 / (np.float32(500000.0) ** (np.arange(0, rot, 2, dtype=np.float32) / np.float32(rot)))).astype(np.float32)
    ang = (np.arange(S, dtype=np.float32)[:, None] * inv[None, :]).astype(np.float32)
    rope = np.zeros((P, 2, S), np.float32)
    rope[:, 0] = 1.0
    for h in range(2):
        for s in range(2):
            rows = slice(HD * h + half * s, HD * h + half * (s + 1))
            rope[rows, 0] = np.cos(ang).T
            rope[rows, 1] = np.sin(ang).T
    t = np.arange(S)
    icnt = np.stack([1.0 / (np.minimum(t + w // 2, S) - np.maximum(t - w // 2, 0)) for w in (2, 4, 8, 16)])
    return cst, rope, icnt.astype(np.float32)[None]


def arrays_of(inputs):
    x = {k: np.asarray(a) for k, a in inputs.items()}
    a = {"x": x["x"][0]}
    gain = np.concatenate([x["qk_gain"][0], x["qk_gain"][0]], axis=1)
    parts = {"norm_mix": columns(x["norm_mix"][0]), "norm_ffn": columns(x["norm_ffn"][0]), "c": columns(x["c_2"][0]),
             "final_g": columns(x["final_g_2"]), "pool_scale": columns(x["pool_scale_2"]),
             "subln": columns(x["diff_subln_g_2"]), "norm_g": columns(x["norm_g_2"]),
             "conv": x["ffn_conv"][0].reshape(3, 2, KF, P).transpose(3, 2, 1, 0).reshape(P, 132),
             "mod_b": columns(x["mod_b_2"]), "mu": columns(x["rwkv_mu"][0]), "w0": columns(x["rwkv_w0"][0]),
             "a0": columns(x["rwkv_a0"][0]), "k_k": columns(x["rwkv_k_k"][0]), "k_a": columns(x["rwkv_k_a"][0]),
             "r_k": columns(x["rwkv_r_k"][0]), "ln_w": columns(x["rwkv_ln_w"][0]), "ln_b": columns(x["rwkv_ln_b"][0]),
             "qk_gain": gain.T}
    a["vec"] = np.ascontiguousarray(np.concatenate([parts[n] for n in VEC], axis=1))
    a["cst"], a["rope"], a["icnt"] = constants()
    a["lam"] = x["diff_lambda_2"].reshape(1, 4 * HD)
    ups = [x["ffn_up"][0], x["ffn_w_gu_2"][0, 0], x["ffn_w_gu_2"][0, 1], x["ffn_w_gu_2"][1, 0], x["ffn_w_gu_2"][1, 1]]
    downs = [x["ffn_down"][0], x["ffn_w_down_2"][0, 0], x["ffn_w_down_2"][0, 1], x["ffn_w_down_2"][1, 0],
             x["ffn_w_down_2"][1, 1]]
    for f in range(5):
        w = ups[f].reshape(KD, P, 2, KF, P).transpose(3, 2, 1, 0, 4)
        a[f"up{f}"] = np.ascontiguousarray(w).reshape(2 * KF, P, KD * P)
        a[f"down{f}"] = units_of(downs[f], KF)
    a["pool_w"] = np.concatenate([units_of(x["pool_w_2"][g], 2) for g in range(4)])
    qkv = units_of(x["diff_w_qkv_2"], KD)
    a["w_qkv"] = np.concatenate([qkv[16:24], qkv[8:16], qkv[0:8]])
    a["w_o"] = units_of(x["diff_w_o_2"], KD)
    m = x["mod_w_2"].reshape(2, 4, 2, P, MOD_GROUPS_LAYER, S)
    a["mod_w"] = np.ascontiguousarray(m.transpose(0, 4, 1, 3, 2, 5)).reshape(4 * N_MOD_GROUPS, P, 2 * S)
    w = x["w_in"][0]
    a["w_in"] = units_of(np.concatenate([w[:, 0:1280], w[:, 1304:3096]], axis=1), KD)
    a["w_in24"] = w[:, 1280:1304].reshape(KD, P, 24).transpose(1, 0, 2).reshape(P, KD * 24)
    a["w_merge"] = units_of(w[:, 3096:], KD)
    a["proj_nsa"], a["proj_rwkv"] = units_of(x["proj_nsa"][0], 4), units_of(x["proj_rwkv"][0], 4)
    a["w_out"] = units_of(x["w_out"][0], KD)
    w1, w2 = np.zeros((P, 2, CMP_BLOCK, P), np.float32), np.zeros((P, 2, P), np.float32)
    pe = np.zeros((P, 2, CMP_BLOCK), np.float32)
    for g in range(2):
        rows = slice(HD * g, HD * g + HD)
        w1[rows, :, :, rows] = x["cmp_w1"][0].transpose(2, 0, 1, 3)
        w2[rows, :, rows] = x["cmp_w2"][0].transpose(1, 0, 2)
        pe[rows] = x["cmp_pe"][0].transpose(2, 0, 1)
    a["cmp_w1"], a["cmp_w2"], a["cmp_pe"] = w1, w2, pe
    a["low_up"] = np.concatenate([x["rwkv_w_up"][0], x["rwkv_a_up"][0]], axis=0)
    a["g_up"] = x["rwkv_g_up"][0]
    a.update(masks())
    return {k: np.ascontiguousarray(b) for k, b in a.items()}


def masks():
    i = np.arange(P)
    tri = np.where(i[None, :] > i[:, None], np.float32(NEG), np.float32(0))
    t = np.arange(S).reshape(TT, P).T[:, :, None]
    seen = (np.arange(NC) * CMP_STRIDE + CMP_BLOCK - 1)[None, None, :] <= t
    rmask = np.broadcast_to((np.arange(S) % CHUNK != 0).astype(np.float32), (P, S))
    s, t = i[:, None], i[None, :]
    same = s // CHUNK == t // CHUNK
    stri = np.concatenate([same & (s < t), same & (s <= t)], axis=1)
    lmask = np.stack([(s // (2 * b) == t // (2 * b)) & (s // b < t // b) for b in (1, 2, 4, 8, 16, 32)], axis=1)
    return {"tri": tri, "cadd": np.where(seen, 0, NEG).astype(np.float32), "cmul": seen.astype(np.float32),
            "rmask": rmask, "masks": np.concatenate([stri, lmask.reshape(P, 6 * P)], axis=1).astype(np.float32)}


def kernel(**inputs):
    import concourse.bacc as bacc
    from concourse.bass_utils import run_bass_kernel_spmd

    nc = bacc.Bacc("TRN2", target_bir_lowering=False, num_devices=1)
    arrays = arrays_of(inputs)
    A = {n: nc.dram_tensor(f"in_{n}", a.shape, mybir.dt.from_np(a.dtype), kind="ExternalInput").ap()
         for n, a in arrays.items()}
    out = nc.dram_tensor("out", (S, D), F32, kind="ExternalOutput").ap()
    build(nc, A, out)
    r = run_bass_kernel_spmd(nc, [{f"in_{n}": a for n, a in arrays.items()}], core_ids=[0])
    return r.results[0]["out"].reshape(1, S, D)
```

```python
from contextlib import ExitStack

import numpy as np

import concourse.bass as bass
from concourse import mybir

F32 = mybir.dt.float32
F32R = mybir.dt.float32r
I32 = mybir.dt.int32
ALU = mybir.AluOpType
ACT = mybir.ActivationFunctionType
AX = mybir.AxisListType

P = 128
S = 512
TT = S // P
D = 1024
KD = D // P
FF = 2816
KF = FF // P
DOWN = [(0, 8), (8, 7), (15, 7)]
SLOT = KD * P
LAG = 3
NSTAGE = 4
EPS = 1e-6
MOD_TILES = 72
HD = 64
DIFF_HEADS = 8
NEG = -1e30
DECAY = float(np.exp(-0.5))
NSA_HEADS, NSA_GROUPS = 8, 2
CMP_BLOCK, CMP_STRIDE = 32, 16
NC = (S - CMP_BLOCK) // CMP_STRIDE + 1
CHUNK = 64
NCH = S // CHUNK
RW_TILES = [12, 13] + list(range(12))
PAIRS = 4
LNX_EPS = 1e-5 * HD
LAM_INIT = 0.8 - 0.6 * float(np.exp(-0.3))

VEC = {}
_at = 0
for _name, _n in [("norm_mix", 8), ("norm_ffn", 8), ("final_g", 8), ("pool_scale", 8), ("subln", 1),
                  ("norm_g", 48), ("conv", 132), ("mod_b", 144), ("mu", 14), ("w0", 4), ("a0", 4), ("k_k", 4),
                  ("k_a", 4), ("r_k", 4), ("ln_w", 4), ("ln_b", 4), ("qk_gain", 4)]:
    VEC[_name] = (_at, _n)
    _at += _n
NVEC = _at

CST = {}
_at = 0
for _name, _n in [("ident", 128), ("ones", 128), ("pair", 128), ("perm", 128)]:
    CST[_name] = (_at, _at + _n)
    _at += _n
NCST = _at


def level_halves():
    return [("a", 0), ("b", 4)]


RW_PE_HEAD = ["w", "a", "kss", "krs", "g", "bonus", "tokA", "tokB", "tokV", "P10", "P11", "P12", "tokK", "P13"]
RW_PE_REST = (["P20", "+w", "+a", "P23", "P21", "P22", "X0a", "X0b", "A1a", "A1b", "+kss", "Y1a", "Y1b", "X1a", "X1b",
               "A2a", "A2b", "+krs", "Y2a", "Y2b", "X2a", "X2b", "A3a", "A3b", "Y3a", "Y3b", "X3a", "X3b",
               "A4a", "A4b", "+g", "Y4a", "Y4b", "X4a", "X4b", "A5a", "A5b", "+bonus", "Y5a", "Y5b", "MV", "U0", "WT"]
              + [x for c in range(NCH) for x in ((f"u{c}", f"s{c}") if c < NCH - 1 else (f"u{c}",))]
              + ["y", "+tokA", "mean", "+tokB", "+tokV", "+P10", "+P11", "+P12", "vss", "+tokK", "+P13", "vrs"])
RW_ACT_HEAD = ["sw", "a", "kkq", "kstd", "Ep", "En", "Em", "D", "g", "tokA", "tokB", "tokV", "tokK"]
RW_ACT_REST = ["+sw", "+a", "+kkq", "X0a", "X0b", "A1a", "A1b", "+kstd", "X1a", "X1b", "A2a", "A2b", "+Ep", "+En",
               "X2a", "X2b", "A3a", "A3b", "+Em", "+D", "X3a", "X3b", "A4a", "A4b", "+g", "X4a", "X4b", "A5a", "A5b",
               "MV", "U0", "y", "+tokA", "+tokB", "+tokV", "ysq", "vstd", "+tokK"]
RW_DVE_HEAD = ["kk0", "cs", "rel", "dsum", "relm", "kmax", "krec", "krexp", "kkn", "a1", "kh", "A", "kka", "B", "K", "R",
               "rk", "bonus", "eye", "P10", "P11", "P12", "P13"]
RW_DVE_REST = (["XT0", "+kk0", "P20", "P23", "P21", "P22", "+cs", "+rel", "+dsum", "Y1a", "Y1b",
                "+relm", "+kmax", "+krec", "+krexp", "Y2a", "Y2b", "+kkn", "+a1", "+kh", "Y3a", "Y3b",
                "+A", "+kka", "+B", "+K", "Y4a", "Y4b", "+R", "+rk", "Y5a", "Y5b", "+bonus", "WT"]
               + [x for c in range(NCH) for x in ((f"SD{c}", f"U{c}", f"S{c}") if c < NCH - 1 else (f"U{c}",))]
               + ["+eye", "yc", "+P10", "+P11", "+P12", "vrec", "vrexp", "+P13", "yn", "yb", "o"])


def pair_steps(head, rest):
    steps = [(x, 0) for x in head]
    for p in range(PAIRS):
        steps += [(x[1:], p + 1) if x[0] == "+" else (x, p) for x in rest if x[0] != "+" or p + 1 < PAIRS]
    return steps


RW_PE, RW_ACT, RW_DVE = (pair_steps(RW_PE_HEAD, RW_PE_REST), pair_steps(RW_ACT_HEAD, RW_ACT_REST),
                         pair_steps(RW_DVE_HEAD, RW_DVE_REST))

NS_PE = (["vs", "vw", "gt"] + [f"ss{n}" for n in range(6)] + [f"rs{n}" for n in range(4)]
         + ["c0", "rs4", "rs5", "c1", "kc", "vc", "kcss", "kcrs"] + [f"cs{j}" for j in range(TT)])
NS_ACT = (["gl", "vs", "vw", "gt"] + [f"sq{n}" for n in range(6)] + ["std", "cb0", "h0"] + [f"kd{n}" for n in range(8)]
          + ["cb1", "h1", "kcsq", "kcstd"] + [f"kcd{n}" for n in range(4)] + [f"ce{j}" for j in range(TT)])
NS_DVE = (["pe", "q0", "q1", "q2", "q3", "kx", "vx", "ks", "vs", "kw", "vw", "gl", "gq", "rec"]
          + [f"{x}{n}" for n in range(6) for x in ("rexp", "n")] + ["kc", "vc", "kcrec", "kcrexp", "kcn"]
          + [f"{x}{j}" for j in range(TT) for x in ("add", "max", "sub", "sum", "rec", "coef", "mask", "p")])


def upto(steps, name):
    return steps.index(name) + 1


class Segment:

    def __init__(self, name, first, tile, shapes, tiles):
        self.name, self.first, self.tile, self.shapes, self.tiles = name, first, tile, shapes, tiles


def plan_stream(first_block, second_block):
    up, down = [(KD, P)] * (2 * KF), [(n, P) for _, n in DOWN] * KD
    order = []
    if first_block:
        order += [("mix_in", [(KD, P)] * 10 + [(KD, 24)] + [(KD, P)] * 14, 25),
                  ("merge", [(KD, P), (KD, P), (4, P), (4, P)] * 8, 32),
                  ("mix_out", [(KD, P)] * 8, 8), ("up0", up, 44), ("down0", down, 8)]
    if second_block:
        order += [("up1", up, 44), ("down1", down, 8), ("pool", [(2, P)] * 8, 8),
                  ("up2", up, 44), ("down2", down, 8), ("up3", up, 44), ("down3", down, 8),
                  ("qkv", [(KD, P)] * 24, 24), ("attn_out", [(KD, P)] * 8, 8),
                  ("up4", up, 44), ("down4", down, 8)]
    segments, unit, tile = {}, 0, 0
    for name, shapes, tiles in order:
        segments[name] = Segment(name, unit, tile, shapes, tiles)
        unit, tile = unit + len(shapes), tile + tiles
    return segments


def build(nc, A, out, first_block=True, second_block=True):
    seg = plan_stream(first_block, second_block)
    units = [(s, n) for s in seg.values() for n in range(len(s.shapes))]

    with ExitStack() as ctx:
        def sb(name, shape, dt=F32, on=ctx):
            return on.enter_context(nc.sbuf_tensor(name, shape, dt))

        def sem(name):
            return ctx.enter_context(nc.semaphore(name))

        cst = sb("cst", [P, NCST])
        vec = sb("vec", [P, NVEC])
        eps = sb("eps", [P, 2])
        zero = sb("zero", [P, 1])
        xT = sb("xT", [P, KD, S])
        h_hi = sb("h_hi", [P, KD, S], F32R)
        h_lo = sb("h_lo", [P, KD, S], F32R)
        stage = sb("stage", [P, NSTAGE, SLOT])
        w_hi = sb("w_hi", [P, 2, SLOT], F32R)
        w_lo = sb("w_lo", [P, 2, SLOT], F32R)
        norm_t = sb("norm_t", [P, 2, S])
        std = sb("std", [P, TT])
        warm_out = sb("warm_out", [P, 1])
        rstd = sb("rstd", [P, TT])
        rexp = sb("rexp", [P, 2, TT, P])
        if second_block:
            modv = sb("modv", [P, 2, 72])
            c_act = sb("c_act", [P, D])
            mod_w = sb("mod_w", [P, 2, D])
            mod_four = sb("mod_four", [P, 4])
            scales = sb("scales", [P, 2, 3, KD])
            gates = sb("gates", [P, 2, 3, KD])
            lam_in = sb("lam_in", [P, 4 * HD])
            lam_sum = sb("lam_sum", [P, 2])
            lam_exp = sb("lam_exp", [P, 2])
            neg_lam = sb("neg_lam", [P, 1])
            sub_gain = sb("sub_gain", [P, 1])
            nmax = sb("nmax", [P, 2, 2])
            esum = sb("esum", [P, 2, 2])
            coef = sb("coef", [P, 2, 2])
            ostd = sb("ostd", [P, DIFF_HEADS * TT])
            orstd = sb("orstd", [P, DIFF_HEADS * TT])

        ident, ones = cst[:, 0:128], cst[:, 128:256]
        pair_ones, perm = cst[:, 256:384], cst[:, 384:512]

        def v(name, n=0, count=1):
            return vec[:, VEC[name][0] + n:VEC[name][0] + n + count]

        psum = ctx.enter_context(nc.psum_tensor("psum", [P, 8, S], F32))

        tables = sem("tables")
        cst_in = sem("cst_in")
        cond_in = sem("cond_in")
        x_in = [sem(f"x_in{n}") for n in range(4)]
        filled = sem("filled")
        loaded = [sem(f"loaded{n}") for n in range(NSTAGE)]
        hi_done = sem("hi_done")
        lo_done = sem("lo_done")
        unit_done = sem("unit_done")
        x_ready = sem("x_ready")
        sq_done = sem("sq_done")
        ssq_done = sem("ssq_done")
        std_done = sem("std_done")
        warmed = sem("warmed")
        rstd_done = sem("rstd_done")
        rexp_done = sem("rexp_done")
        rbc_done = sem("rbc_done")
        t_done = sem("t_done")
        hhi_done = sem("hhi_done")
        hlo_done = sem("hlo_done")
        silu_done = sem("silu_done")
        hid_done = sem("hid_done")
        hidhi_done = sem("hidhi_done")
        hidlo_done = sem("hidlo_done")
        tap_done = sem("tap_done")
        mod_in = [sem("mod_in0"), sem("mod_in1")]
        mod_done = sem("mod_done")
        mod_put = sem("mod_put")
        mod_out = sem("mod_out")
        mod_vec = sem("mod_vec")
        c_done = sem("c_done")
        lam_done = sem("lam_done")
        padded = sem("padded")
        win_done = sem("win_done")
        diff_done = sem("diff_done")
        diff_hi = sem("diff_hi")
        raw_done = sem("raw_done")
        post_done = sem("post_done")
        roped = sem("roped")
        vtok_done = sem("vtok_done")
        score_done = sem("score_done")
        max_done = sem("max_done")
        exp_done = sem("exp_done")
        comb_step = sem("comb_step")
        a_turned = sem("a_turned")
        pt_done = sem("pt_done")
        pv_done = sem("pv_done")
        o_done = sem("o_done")
        osq_done = sem("osq_done")
        ossq_done = sem("ossq_done")
        ostd_done = sem("ostd_done")
        orstd_done = sem("orstd_done")
        orexp_done = sem("orexp_done")
        obc_done = sem("obc_done")
        ot_done = sem("ot_done")
        ohi_done = sem("ohi_done")
        olo_done = sem("olo_done")
        xt_done = sem("xt_done")
        if first_block:
            ns_in, ns2_in, rw_in = sem("ns_in"), sem("ns2_in"), sem("rw_in")
            ns_pe, ns_act, ns_dve = sem("ns_pe"), sem("ns_act"), sem("ns_dve")
            rw_pe, rw_act, rw_dve = sem("rw_pe"), sem("rw_act"), sem("rw_dve")
            nscore_done, nmask_done, nmax_done, nexp_done = sem("nscore_done"), sem("nmask_done"), sem("nmax_done"), sem("nexp_done")
            nscale_step, nturned, npt_done, npv_done, no_done = (sem("nscale_step"), sem("nturned"), sem("npt_done"),
                                                                 sem("npv_done"), sem("no_done"))
            zraw_done, zdiff_done, zm_done, zact_done, zset = (sem("zraw_done"), sem("zdiff_done"), sem("zm_done"),
                                                              sem("zact_done"), sem("zset"))
            osplit_hi, osplit_lo = sem("osplit_hi"), sem("osplit_lo")
            sig_done, y_step, yhi_done, ylo_done = sem("sig_done"), sem("y_step"), sem("yhi_done"), sem("ylo_done")
        turned = sem("turned")
        out_copied = sem("out_copied")
        stored = sem("stored")

        def phase(*tensors):
            with ExitStack() as own:
                return [sb(n, shape, dt, own) for n, shape, dt in tensors]

        if first_block:
            mixer = ExitStack()
            o_nsa = sb("o_nsa", [P, 4, S], F32, mixer)

            def mixer_phase(*tensors):
                with ExitStack() as own:
                    return [sb(n, shape, dt, own) for n, shape, dt in tensors]

            (q_n, k_n, kd, kx, v_nt, gl, gate_t, Pn, PTn, PTc, Pc, kcd, cb, hid_c, kc_n, vc_t, raw_n, tri, cadd, cmul, w2_c,
             stat_n, rec_n, nmax_n, esum_n, coef_n, cmx, csum, gq, cpe) = mixer_phase(
                ("q_n", [P, 4, S], F32), ("k_n", [P, 2, S], F32), ("kd", [P, 2, 2, S], F32),
                ("kx", [P, 2, CMP_BLOCK, 32], F32), ("v_nt", [P, 2, TT, P], F32), ("gl", [24, S], F32),
                ("gate_t", [P, TT, 24], F32), ("Pn", [P, 2, 2, S], F32), ("PTn", [P, 2, 2, TT, S], F32),
                ("PTc", [NC, 2, S], F32), ("Pc", [P, TT, NSA_HEADS, 32], F32), ("kcd", [P, 2, 32], F32),
                ("cb", [P, 2], F32), ("hid_c", [P, 2, 32], F32), ("kc_n", [P, 32], F32), ("vc_t", [NC, P], F32),
                ("raw_n", [P, 2, S], F32), ("tri", [P, P], F32), ("cadd", [P, TT, NC], F32), ("cmul", [P, TT, NC], F32),
                ("w2_c", [P, 2, P], F32), ("stat_n", [P, 7, TT, 2], F32), ("rec_n", [P, 7, TT, 2], F32),
                ("nmax_n", [P, 2, 2], F32), ("esum_n", [P, 2, 2], F32),
                ("coef_n", [P, 2, 2], F32), ("cmx", [P, NSA_HEADS], F32), ("csum", [P, NSA_HEADS], F32),
                ("gq", [P, 1], F32), ("cpe", [P, 2, CMP_BLOCK], F32))
            rexp_n = Pn[:, 0].rearrange("p a (t n) -> p a t n", t=TT)
            w1_c = PTn[:].rearrange("p a b t s -> p (a b t s)").rearrange("p (k l n) -> p k l n", k=2, l=CMP_BLOCK)

            zm = sb("zm", [P, 14, S], F32, mixer)
            (low_up, g_up, keep, zraw, tA, tB, tC, tD, AR, Bt, Kt, tok, TR, MR, XT, X, Ap, Sh, SD, Dc, kst, krec,
             mask8) = mixer_phase(
                ("low_up", [P, S], F32), ("g_up", [P, S], F32), ("keep", [P, S], F32), ("zraw", [P, 2, S + 4], F32),
                ("tA", [P, S], F32), ("tB", [P, S], F32), ("tC", [P, S], F32), ("tD", [P, S], F32),
                ("AR", [P, TT, 2, P], F32), ("Bt", [P, S], F32), ("Kt", [P, S], F32), ("tok", [P, 4, TT, P], F32),
                ("TR", [P, 8, 2 * P], F32), ("MR", [P, 8, 2 * P], F32), ("XT", [P, 8, P], F32), ("X", [P, 8, P], F32),
                ("Ap", [P, 8, P], F32), ("Sh", [P, NCH, HD], F32), ("SD", [P, HD], F32), ("Dc", [P, 2, NCH], F32),
                ("kst", [P, TT, 2], F32), ("krec", [P, TT, 2], F32),
                ("mask8", [P, 8 * P], mybir.dt.uint8))
            odd_ar, odd_td = [stage[:, (seg["merge"].first + n) % NSTAGE] for n in (2, 3)]
            ARs = [AR[:], odd_ar.rearrange("p (t a n) -> p t a n", t=TT, a=2)]
            tDs, keeps = [tD[:], odd_td[:, 0:S]], [keep[:], odd_td[:, S:2 * S]]
            rexp_k = norm_t[:, 0].rearrange("p (t n) -> p t n", t=TT)
            rmask = norm_t[:, 1]
            stri = mask8[:, 0:2 * P]
            lmask = mask8[:, 2 * P:].rearrange("p (l n) -> p l n", l=6)
            o_hi, o_lo, y_hi, y_lo = mixer_phase(
                ("o_hi", [P, KD, S], F32R), ("o_lo", [P, KD, S], F32R), ("y_hi", [P, KD, S], F32R),
                ("y_lo", [P, KD, S], F32R))
            sg = rexp[:].rearrange("p a t n -> p a (t n)")
            y_t = norm_t[:, 0]
            mixer.close()

        x_tok, = phase(("x_tok", [P, TT, D], F32))
        hid_hi, hid_lo, s_buf, hid, taps = phase(
            ("hid_hi", [P, KF, S], F32R), ("hid_lo", [P, KF, S], F32R),
            ("s_buf", [P, 2, S], F32), ("hid", [P, 2, S], F32), ("taps", [P, 2, S], F32))
        hp, win, icnt, diff, psq = phase(
            ("hp", [P, 2, 2, S + 16], F32), ("win", [P, 2, 2, S + 16], F32), ("icnt", [P, 4 * 16], F32),
            ("diff", [P, 2, 2, S], F32), ("psq", [P, 2, S], F32))
        q_t, k_t, v_tok, rope, raw, E, PT, o_raw = phase(
            ("q_t", [P, KD, S], F32), ("k_t", [P, KD, S], F32), ("v_tok", [P, TT, D], F32), ("rope", [P, 2, S], F32),
            ("raw", [P, 2, S], F32), ("E", [P, 2, 2, S], F32), ("PT", [P, 2, TT, S], F32), ("o_raw", [P, DIFF_HEADS, S], F32))
        y_out, out_tok = phase(("y_out", [P, 2, S], F32), ("out_tok", [P, TT, D], F32))

        def repeat(eng, start, count, body):
            if count == 1:
                body(start)
            elif count > 1:
                with eng.Fori(start, start + count) as i:
                    body(i)

        def fixed(c, i):
            return (c + 4 * i, 0) if isinstance(i, int) else (c, i)

        def shape_of(c):
            s, n = units[c]
            return s.shapes[n]

        def slot(buf, c, kt, cols, ring):
            return buf[:, c % ring, 0:kt * cols].rearrange("p (k n) -> p k n", k=kt)

        def bank(c):
            return psum[:, c % 4, :]

        def sq(n_norm, k):
            return (psq if n_norm == 4 else norm_t)[:, k % 2]

        UP_RUNS = {
            f: [(0, 1), (1, 9), (10, 1)] for f in range(5)}
        MOD_AT = {"mix_in": 0, "merge": 25, "mix_out": 57, "down0": 64, "up1": 85, "down1": 129}
        PAIR = {f: KF * (f - (0 if first_block else 1)) for f in range(5)}
        NORM = {n: n - (0 if first_block else 2) for n in range(9)}
        ffns = ([0] if first_block else []) + ([1, 2, 3, 4] if second_block else [])
        last_norm = 8
        if not second_block:
            NORM[8] = 2

        def source(c, i=0):
            s, n = units[c]
            kt, cols = s.shapes[n]
            if s.name.startswith("up") or s.name.startswith("down"):
                w = A[s.name]
                if s.name.startswith("down"):
                    k0 = DOWN[n % 3][0] * P
                    return w[n // 3, :, k0:k0 + kt * P]
                return w[bass.ds(n + 4 * i, 1)].rearrange("a p n -> (a p) n")
            if s.name == "mix_in":
                return A["w_in24"] if cols == 24 else A["w_in"][n if n < 10 else 10 + RW_TILES[n - 11]]
            if s.name == "merge":
                w, at = [("w_merge", n // 4), ("w_merge", 8 + n // 4), ("proj_nsa", n // 4), ("proj_rwkv", n // 4)][n % 4]
                return A[w][at]
            return A[{"mix_out": "w_out", "pool": "pool_w", "qkv": "w_qkv", "attn_out": "w_o"}[s.name]][n]

        NU = len(units)

        block = ctx.enter_context(nc.Block())

        @block.sync
        def _(sp):
            sp.dma_start(cst[:], A["cst"]).then_inc(cst_in, 16)
            for n in range(4):
                cols = slice(n * D // 4, (n + 1) * D // 4)
                sp.dma_start(x_tok[:, :, cols], A["x"].rearrange("(t p) d -> p t d", p=P)[:, :, cols]).then_inc(x_in[n], 16)
                if n == 0 and second_block:
                    sp.dma_start(c_act[:], A["c"].to_broadcast([P, D])).then_inc(cond_in, 16)
                    sp.dma_start(lam_in[:], A["lam"].to_broadcast([P, 4 * HD])).then_inc(cond_in, 16)
            sp.dma_start(vec[:], A["vec"]).then_inc(tables, 16)

            def load(c, i=0):
                c, i = fixed(c, i)
                kt, cols = shape_of(c)
                if not (isinstance(i, int) and c < NSTAGE):
                    sp.wait_ge(lo_done, c + 4 * i - NSTAGE + 1)
                sp.dma_start(stage[:, c % NSTAGE, 0:kt * cols], source(c, i)).then_inc(loaded[c % NSTAGE], 16)

            for s in seg.values():
                if s.name == "mix_in":
                    for n in range(NSTAGE):
                        load(s.first + n)
                    for dst, src in ((w1_c, "cmp_w1"), (w2_c[:], "cmp_w2"), (cpe[:], "cmp_pe"), (tri[:], "tri"),
                                     (cadd[:], "cadd"), (cmul[:], "cmul")):
                        if dst is w1_c:
                            sp.wait_ge(turned, KD)
                        sp.dma_start(dst, A[src]).then_inc(ns_in, 16)
                    for n in range(NSTAGE, 14):
                        load(s.first + n)
                    sp.wait_ge(no_done, NSA_HEADS)
                    for dst, src in ((low_up[:], "low_up"), (g_up[:], "g_up"), (rmask, "rmask"),
                                     (AR[:].rearrange("p t a n -> p (t a n)"), "masks")):
                        sp.dma_start(dst, A[src]).then_inc(rw_in, 16)
                    for n in range(14, 25):
                        load(s.first + n)
                elif s.name.startswith("up"):
                    repeat(sp, 0, KF // 2, lambda i: [load(s.first + j, i) for j in range(4)])
                else:
                    for n in range(len(s.shapes)):
                        if n == NSTAGE and s.name == "pool":
                            sp.wait_ge(unit_done, s.first)
                            sp.dma_start(icnt[:], A["icnt"].to_broadcast([P, 4 * 16])).then_inc(tables, 16)
                        if n == NSTAGE and s.name == "qkv":
                            sp.wait_ge(unit_done, s.first)
                            sp.dma_start(rope[:], A["rope"]).then_inc(tables, 16)
                        if s.name == "merge" and n == 2:
                            sp.wait_ge(rw_dve, upto(RW_DVE, ("o", PAIRS - 1)))
                        load(s.first + n)
            for tt in range(2):
                sp.wait_ge(out_copied, 8)
                sp.dma_start(out.rearrange("(t p) d -> p t d", p=P)[:, 2 * tt:2 * tt + 2, :],
                             out_tok[:, 2 * tt:2 * tt + 2, :]).then_inc(stored, 16)
            sp.wait_ge(stored, 32)

        @block.gpsimd
        def _(pool):
            pool.memset(eps[:, 0:1], EPS)
            pool.memset(eps[:, 1:2], LNX_EPS).then_inc(filled, 1)
            pool.memset(zero[:], 0.0).then_inc(filled, 1)

            def mod_load(t):
                for e in range(2):
                    if not (isinstance(t, int) and t == 0):
                        pool.wait_ge(mod_done, t + e - 1)
                    pool.dma_start(mod_w[:, e], A["mod_w"][bass.ds(t + e, 1)].rearrange(
                        "a p n -> (a p) n")).then_inc(mod_in[e], 16)

            if second_block:
                mod_load(0)
                with pool.Fori(1, MOD_TILES) as i:
                    mod_load(2 * i)
                for k in range(KD):
                    pool.wait_ge(diff_hi, k + 1)
                    pool.tensor_tensor(h_lo[:, k], diff[:, k // 2 % 2, k % 2], h_hi[:, k].bitcast(F32),
                                       ALU.subtract).then_inc(hlo_done, 1)

        @block.scalar
        def _(act):
            def hi(c, i=0):
                c, i = fixed(c, i)
                if c >= NU:
                    return
                kt, cols = shape_of(c)
                act.wait_ge(loaded[c % NSTAGE], 16 * (c // NSTAGE + 1 + i))
                if not (isinstance(i, int) and c < 2):
                    act.wait_ge(unit_done, c + 4 * i - 1)
                act.activation(w_hi[:, c % 2, 0:kt * cols], stage[:, c % NSTAGE, 0:kt * cols],
                               ACT.Copy).then_inc(hi_done, 1)

            def square(n_norm, k):
                at = KD * NORM[n_norm] + k
                act.wait_ge(x_ready, at + 1)
                if at >= 2:
                    act.wait_ge(ssq_done, at - 1)
                act.activation(sq(n_norm, k), xT[:, k], ACT.Square).then_inc(sq_done, 1)

            def warm(func):
                if warm_count[0]:
                    act.wait_ge(warmed, warm_count[0])
                warm_count[0] += 1
                act.activation(warm_out[:], eps[:, 0:1], func).then_inc(warmed, 1)

            warm_count = [0]

            def root(n_norm):
                at = KD * NORM[n_norm]
                act.wait_ge(ssq_done, at + KD)
                act.activation(std[:], psum[:, 4, 0:TT], ACT.Sqrt, bias=eps[:, 0:1], scale=1.0 / D).then_inc(std_done, 1)
                if n_norm in (1, 2, 4, 5, 7):
                    warm(ACT.Silu)

            def round_h(n_norm, shift):
                for k in range(KD):
                    at = KD * NORM[n_norm] + k
                    act.wait_ge(t_done, at + 1)
                    act.activation(h_hi[:, k], norm_t[:, k % 2], ACT.Identity, bias=shift(k)).then_inc(hhi_done, 1)

            def up(f):
                s, pairs = seg[f"up{f}"], PAIR[f]

                def body(i):
                    for q in range(2):
                        p = pairs + 2 * i + q
                        hi(s.first + 2 * q + 2, i)
                        if f == 0:
                            act.wait_ge(tap_done, 6 * (2 * i + q) + 3)
                            act.activation(s_buf[:, q], taps[:, 0], ACT.Silu).then_inc(silu_done, 1)
                        else:
                            act.wait_ge(unit_done, s.first + 4 * i + 2 * q + 1)
                            act.activation(s_buf[:, q], bank(s.tile + 2 * q), ACT.Silu).then_inc(silu_done, 1)
                        hi(s.first + 2 * q + 3, i)
                        act.wait_ge(hid_done, p + 1)
                        act.activation(hid_hi[:, bass.ds(2 * i + q, 1), :].rearrange("p a n -> p (a n)"), hid[:, q],
                                       ACT.Copy).then_inc(hidhi_done, 1)

                for start, count in UP_RUNS[f]:
                    repeat(act, start, count, body)

            def down(f, n_norm):
                s = seg[f"down{f}"]
                for n in range(KD):
                    if n == 1:
                        warm(ACT.Sqrt)
                    for j in range(3):
                        hi(s.first + 3 * n + j + 2)
                    square(n_norm, n)

            def mixed_out(name, n_norm, tiles=range(KD)):
                s = seg[name]
                for n in tiles:
                    if n == 0:
                        warm(ACT.Sqrt)
                    hi(s.first + n + 2)
                    square(n_norm, n)

            act.wait_ge(filled, 2)
            if second_block:
                act.wait_ge(cond_in, 32)
                act.activation(c_act[:], c_act[:], ACT.Silu).then_inc(c_done, 1)
                act.wait_ge(lam_done, 2)
                act.activation(lam_exp[:], lam_sum[:], ACT.Exp).then_inc(c_done, 1)
            for k in range(KD):
                square(0 if first_block else 2, k)
            hi(0)
            act.wait_ge(tables, 16)

            def plain(name):
                return lambda k: v(name, k)

            if first_block:
                zero_shift = lambda k: zero[:, 0:1]
                root(0)
                hi(1)
                round_h(0, zero_shift)
                s = seg["mix_in"]

                def ns(name, ins):
                    assert NS_ACT[ns_count[0]] == name, (name, NS_ACT[ns_count[0]])
                    ns_count[0] += 1
                    ins.then_inc(ns_act, 1)

                def after_ns(sem_, steps, name):
                    act.wait_ge(sem_, upto(steps, name))

                ns_count = [0]
                for n in range(11):
                    hi(s.first + n + 2)
                act.wait_ge(unit_done, s.first + 11)
                ns("gl", act.activation(gl[:], bank(s.tile + 10)[0:24, :], ACT.Sigmoid))
                for n, name in enumerate(("vs", "vw")):
                    after_ns(ns_pe, NS_PE, name)
                    ns(name, act.activation(v_nt[:, n], psum[:, 4 + n, :].rearrange("p (t n) -> p t n", t=TT), ACT.Copy))
                after_ns(ns_pe, NS_PE, "gt")
                ns("gt", act.activation(gate_t[:], psum[:, 6, 0:TT * 24].rearrange("p (t n) -> p t n", t=TT), ACT.Copy))
                for n in range(6):
                    src = q_n[:, n] if n < 4 else k_n[:, n - 4]
                    after_ns(ns_dve, NS_DVE, f"q{n}" if n < 4 else ("ks", "kw")[n - 4])
                    if n >= 2:
                        after_ns(ns_pe, NS_PE, f"ss{n - 2}")
                    ns(f"sq{n}", act.activation(raw_n[:, n % 2], src, ACT.Square))
                after_ns(ns_pe, NS_PE, "ss5")
                ns("std", act.activation(stat_n[:, 0:6].rearrange("p a t c -> p (a t c)"), psum[:, 7, 8:56], ACT.Sqrt,
                                         bias=eps[:, 0:1], scale=1.0 / HD))
                def compressed(c):
                    after_ns(ns_pe, NS_PE, f"c{c}")
                    ns(f"cb{c}", act.activation(cb[:, c:c + 1], psum[:, c, NC:NC + 1], ACT.Copy))
                    act.wait_ge(ns_act, upto(NS_ACT, f"cb{c}"))
                    ns(f"h{c}", act.activation(hid_c[:, c, 0:NC], psum[:, c, 0:NC], ACT.Silu, bias=cb[:, c:c + 1]))

                compressed(0)
                after_ns(ns_dve, NS_DVE, "n5")
                for kind in range(2):
                    for g in range(NSA_GROUPS):
                        for half in range(2):
                            src = k_n[HD * g:HD * g + HD, kind]
                            ns(f"kd{4 * kind + 2 * g + half}",
                               act.activation(kd[HD * half:HD * half + HD, kind, g], src, ACT.Copy))
                compressed(1)
                after_ns(ns_dve, NS_DVE, "kc")
                ns("kcsq", act.activation(raw_n[:, 0, 0:NC], kc_n[:, 0:NC], ACT.Square))
                after_ns(ns_pe, NS_PE, "kcss")
                ns("kcstd", act.activation(stat_n[0:NC, 6, 0, :], psum[0:NC, 4, 0:2], ACT.Sqrt, bias=eps[0:NC, 0:1],
                                           scale=1.0 / HD))
                after_ns(ns_dve, NS_DVE, "kcn")
                for g in range(NSA_GROUPS):
                    for half in range(2):
                        ns(f"kcd{2 * g + half}", act.activation(kcd[HD * half:HD * half + HD, g, 0:NC],
                                                                kc_n[HD * g:HD * g + HD, 0:NC], ACT.Copy))
                for j in range(TT):
                    after_ns(ns_dve, NS_DVE, f"sub{j}")
                    ns(f"ce{j}", act.activation(Pc[:, j, :, 0:NC], Pc[:, j, :, 0:NC], ACT.Exp))

                M = 4 * NSA_HEADS
                for m in range(M + 2):
                    if m < M:
                        h, j = m // 4, m % 4
                        act.wait_ge(nmax_done, m + 1)
                        if m >= 2:
                            act.wait_ge(nturned, m - 1)
                        for c in range(2):
                            act.activation(Pn[:, m % 2, c, 0:(j + 1) * P], psum[:, 2 * (m % 2) + c, 0:(j + 1) * P], ACT.Exp,
                                           bias=nmax_n[:, m % 2, c:c + 1],
                                           accum_out=esum_n[:, m % 2, c:c + 1]).then_inc(nexp_done, 1)
                    if m >= 2:
                        h, j = (m - 2) // 4, (m - 2) % 4
                        act.wait_ge(nturned, m - 1)
                        if h >= 2 and j == 0:
                            act.wait_ge(npv_done, h - 1)
                        for c in range(2):
                            act.activation(PTn[:, h % 2, c, 0:j + 1, j * P:(j + 1) * P],
                                           psum[:, 4 + c, 0:(j + 1) * P].rearrange("p (t n) -> p t n", n=P),
                                           ACT.Copy).then_inc(npt_done, 1)
                        act.activation(PTc[:, h % 2, j * P:(j + 1) * P], psum[0:NC, 7, 0:P], ACT.Copy).then_inc(npt_done, 1)

                act.wait_ge(zset, 2)
                for n in range(14):
                    act.wait_ge(unit_done, s.first + 11 + n + 1)
                    if n >= 2:
                        act.wait_ge(zm_done, n - 1)
                    act.activation(zraw[:, n % 2, 1:S + 1], bank(s.tile + 11 + n), ACT.Copy).then_inc(zraw_done, 1)
                    hi(s.first + 11 + n + 2)
                    if n == 4:
                        act.wait_ge(zm_done, 2)
                        act.activation(zm[0:HD, 12], zm[0:HD, 12], ACT.Tanh).then_inc(zact_done, 1)
                        act.activation(zm[:, 13], zm[:, 13], ACT.Sigmoid).then_inc(zact_done, 1)

                rw_count = [0]

                def heads(x):
                    return x.rearrange("p t n -> p (t n)")

                def rw(p, name, ins):
                    assert RW_ACT[rw_count[0]] == (name, p), (name, p, RW_ACT[rw_count[0]])
                    rw_count[0] += 1
                    ins.then_inc(rw_act, 1)

                def given(p, name):
                    act.wait_ge(rw_pe, upto(RW_PE, (name, p)))

                def done(p, name):
                    act.wait_ge(rw_dve, upto(RW_DVE, (name, p)))

                def head(p, *names):
                    if p >= PAIRS:
                        return
                    odd = p % 2
                    for name in names:
                        if name == "sw":
                            given(p, "w")
                            rw(p, "sw", act.activation(tA[:], psum[:, 0, :], ACT.Sigmoid, bias=v("w0", p)))
                        if name == "a":
                            given(p, "a")
                            rw(p, "a", act.activation(tB[:], psum[:, 1, :], ACT.Sigmoid, bias=v("a0", p)))
                        if name == "g":
                            given(p, "g")
                            rw(p, "g", act.activation(keeps[odd], psum[:, 0, :], ACT.Copy))
                        if name == "kkq":
                            done(p, "kk0")
                            rw(p, "kkq", act.activation(tDs[odd], tC[:], ACT.Square))
                        if name == "kstd":
                            given(p, "kss")
                            rw(p, "kstd", act.activation(kst[:].rearrange("p t c -> p (t c)"), psum[:, 1, 0:8], ACT.Sqrt))
                        if name == "Ep":
                            done(p, "relm")
                            rw(p, "Ep", act.activation(ARs[odd][:, :, 1, :], Kt[:].rearrange("p (t n) -> p t n", t=TT),
                                                       ACT.Exp, scale=-DECAY))
                        if name == "En":
                            act.wait_ge(rw_act, upto(RW_ACT, ("Ep", p)))
                            rw(p, "En", act.activation(Kt[:], Kt[:], ACT.Exp, scale=DECAY))
                        if name == "Em":
                            rw(p, "Em", act.activation(tDs[odd], tDs[odd], ACT.Exp, scale=-DECAY))
                        if name == "D":
                            rw(p, "D", act.activation(Dc[:, odd, 0:NCH - 1], Dc[:, odd, 0:NCH - 1], ACT.Exp, scale=-DECAY))
                        if name[0:3] == "tok":
                            given(p, name)
                            n, b = {"A": (0, 6), "B": (1, 7), "K": (2, 0), "V": (3, 2)}[name[3]]
                            rw(p, name, act.activation(tok[:, n], psum[:, b, :].rearrange("p (t n) -> p t n", t=TT), ACT.Copy))

                head(0, *RW_ACT_HEAD)
                AHEAD = {1: ("kstd",), 2: ("Ep", "En"), 3: ("Em", "D"), 4: ("g",), 5: ()}
                for p in range(PAIRS):
                    head(p + 1, "sw", "a", "kkq")
                    for n in range(2):
                        given(p, "X0" + "ab"[n])
                        rw(p, "X0" + "ab"[n], act.activation(heads(X[:, 4 * n:4 * n + 4]), psum[:, 6 + n, :], ACT.Copy))
                    for lev in range(1, 6):
                        for n in range(2):
                            given(p, f"A{lev}" + "ab"[n])
                            rw(p, f"A{lev}" + "ab"[n], act.activation(heads(Ap[:, 4 * n:4 * n + 4]), psum[:, 2 + n, :],
                                                                      ACT.Copy))
                        head(p + 1, *AHEAD[lev])
                        if lev < 5:
                            for n in range(2):
                                given(p, f"X{lev}" + "ab"[n])
                                rw(p, f"X{lev}" + "ab"[n], act.activation(heads(X[:, 4 * n:4 * n + 4]), psum[:, 6 + n, :],
                                                                          ACT.Copy))
                    given(p, "MV")
                    rw(p, "MV", act.activation(heads(X[:, 0:4]), psum[:, 0, :], ACT.Copy))
                    given(p, "U0")
                    rw(p, "U0", act.activation(heads(X[:, 4:8]), psum[:, 1, :], ACT.Copy))
                    given(p, "y")
                    rw(p, "y", act.activation(tA[:], psum[:, 7, :], ACT.Copy))
                    head(p + 1, "tokA", "tokB", "tokV")
                    done(p, "yc")
                    rw(p, "ysq", act.activation(tB[:], tC[:], ACT.Square))
                    given(p, "vss")
                    rw(p, "vstd", act.activation(kst[:].rearrange("p t c -> p (t c)"), psum[:, 1, 0:8], ACT.Sqrt,
                                                 bias=eps[:, 1:2], scale=1.0 / HD))
                    head(p + 1, "tokK")

                act.wait_ge(rw_dve, upto(RW_DVE, ("o", PAIRS - 1)))
                for k in range(KD):
                    act.activation(o_hi[:, k], o_nsa[:, k] if k < 4 else zm[:, k - 4], ACT.Copy).then_inc(osplit_hi, 1)
                s = seg["merge"]
                for n in range(KD):
                    for j in range(4):
                        act.wait_ge(unit_done, s.first + 4 * n + j + 1)
                        if j < 2:
                            if n >= 1:
                                act.wait_ge(y_step, 3 * n - (1 if j == 0 else 0))
                            act.activation(sg[:, j], bank(s.tile + 4 * n + j), ACT.Sigmoid).then_inc(sig_done, 1)
                        hi(s.first + 4 * n + j + 2)
                    act.wait_ge(y_step, 3 * n + 3)
                    act.activation(y_hi[:, n], y_t, ACT.Copy).then_inc(yhi_done, 1)
                mixed_out("mix_out", 1)
                root(1)
                round_h(1, zero_shift)
                up(0)
                down(0, 2 if second_block else 8)

            if second_block:
                def shift(layer, which):
                    return lambda k: modv[:, layer, 24 * which + k:24 * which + k + 1]

                root(2)
                if not first_block:
                    hi(1)
                act.wait_ge(mod_vec, 1)
                round_h(2, shift(0, 0))
                up(1)
                down(1, 3)
                root(3)
                def padded_h(g):
                    for k in (2 * g, 2 * g + 1):
                        act.wait_ge(t_done, KD * NORM[3] + k + 1)
                        if g >= 2:
                            act.wait_ge(diff_done, g - 1)
                        act.activation(hp[:, g % 2, k % 2, 8:8 + S], norm_t[:, k % 2], ACT.Identity,
                                       bias=shift(0, 1)(k)).then_inc(hhi_done, 1)

                act.wait_ge(padded, 4)
                padded_h(0)
                for g in range(4):
                    if g + 1 < 4:
                        padded_h(g + 1)
                    act.wait_ge(diff_done, g + 1)
                    for k in (2 * g, 2 * g + 1):
                        act.activation(h_hi[:, k], diff[:, g % 2, k % 2], ACT.Copy).then_inc(diff_hi, 1)
                    if g >= 1:
                        mixed_out("pool", 4, (2 * g - 2, 2 * g - 1))
                mixed_out("pool", 4, (KD - 2, KD - 1))
                root(4)
                round_h(4, shift(0, 2))
                up(2)
                down(2, 5)
                root(5)
                act.wait_ge(mod_vec, 2)
                round_h(5, shift(1, 0))
                up(3)
                down(3, 6)
                root(6)
                round_h(6, shift(1, 1))

                s = seg["qkv"]
                for n in range(24):
                    hi(s.first + n + 2)
                    if 1 <= n <= 8:
                        act.wait_ge(post_done, n)
                        act.activation(v_tok[:, :, (n - 1) * P:n * P],
                                       psum[:, 4 + (n - 1) % 2, :].rearrange("p (t n) -> p t n", t=TT),
                                       ACT.Copy).then_inc(vtok_done, 1)

                for m in range(4 * DIFF_HEADS + 2):
                    if m < 4 * DIFF_HEADS:
                        act.wait_ge(max_done, m + 1)
                        if m >= 2:
                            act.wait_ge(a_turned, m - 1)
                        for c in range(2):
                            act.activation(E[:, m % 2, c], psum[:, 2 * (m % 2) + c, :], ACT.Exp,
                                           bias=nmax[:, m % 2, c:c + 1],
                                           accum_out=esum[:, m % 2, c:c + 1]).then_inc(exp_done, 1)
                    if m >= 2:
                        g = m - 2
                        h, j = g // 4, g % 4
                        act.wait_ge(a_turned, g + 1)
                        if h >= 2 and j == 0:
                            act.wait_ge(pv_done, h - 1)
                        act.activation(PT[:, h % 2, :, j * P:(j + 1) * P],
                                       psum[:, 4 + g % 2, :].rearrange("p (t n) -> p t n", t=TT),
                                       ACT.Copy).then_inc(pt_done, 1)
                for h in range(DIFF_HEADS):
                    act.wait_ge(o_done, h + 1)
                    if h >= 2:
                        act.wait_ge(ossq_done, h - 1)
                    act.activation(norm_t[:, h % 2], o_raw[:, h], ACT.Square).then_inc(osq_done, 1)
                act.wait_ge(ossq_done, DIFF_HEADS)
                act.activation(ostd[:], psum[:, 4, 0:DIFF_HEADS * TT], ACT.Sqrt, bias=eps[:, 0:1],
                               scale=1.0 / P).then_inc(ostd_done, 1)
                for h in range(DIFF_HEADS):
                    act.wait_ge(ot_done, h + 1)
                    act.activation(h_hi[:, h], norm_t[:, h % 2], ACT.Copy).then_inc(ohi_done, 1)
                mixed_out("attn_out", 7)
                root(7)
                round_h(7, shift(1, 2))
                up(4)
                down(4, 8)

            root(last_norm)
            for k in range(KD):
                act.wait_ge(xt_done, k + 1)
                act.activation(out_tok[:, :, k * P:(k + 1) * P],
                               psum[:, k % 4, :].rearrange("p (t n) -> p t n", t=TT), ACT.Copy).then_inc(out_copied, 1)

        @block.vector
        def _(dve):
            def lo(c, i=0):
                c, i = fixed(c, i)
                if c >= NU:
                    return
                kt, cols = shape_of(c)
                dve.wait_ge(hi_done, c + 4 * i + 1)
                dve.tensor_tensor(w_lo[:, c % 2, 0:kt * cols], stage[:, c % NSTAGE, 0:kt * cols],
                                  w_hi[:, c % 2, 0:kt * cols].bitcast(F32), ALU.subtract).then_inc(lo_done, 1)

            def spread(n_norm):
                dve.wait_ge(std_done, NORM[n_norm] + 1)
                dve.reciprocal(rstd[:], std[:]).then_inc(rstd_done, 1)
                dve.wait_ge(rstd_done, NORM[n_norm] + 1)
                dve.tensor_copy(rexp[:, 0], rstd[:].unsqueeze(2).to_broadcast([P, TT, P])).then_inc(rexp_done, 1)
                dve.wait_ge(rbc_done, NORM[n_norm] + 1)

            def norm(n_norm, scale, shift):
                base = KD * NORM[n_norm]
                spread(n_norm)
                if NORM[n_norm] == 0:
                    lo(1)
                for k in range(KD + 1):
                    if k < KD:
                        if k >= 2:
                            dve.wait_ge(hlo_done, base + k - 1)
                        dve.scalar_tensor_tensor(out=norm_t[:, k % 2], in0=xT[:, k], scalar=scale(k),
                                                 in1=psum[:, 5, :], op0=ALU.mult, op1=ALU.mult).then_inc(t_done, 1)
                    if k >= 1:
                        dve.wait_ge(hhi_done, base + k)
                        dve.scalar_tensor_tensor(out=h_lo[:, k - 1], in0=norm_t[:, (k - 1) % 2], scalar=shift(k - 1),
                                                 in1=h_hi[:, k - 1].bitcast(F32), op0=ALU.add,
                                                 op1=ALU.subtract).then_inc(hlo_done, 1)

            def mod(t, i=0):
                if not second_block or isinstance(i, int) and t + 4 * i >= 2 * MOD_TILES:
                    return
                dve.wait_ge(mod_in[t % 2], 16 * (t // 2 + 1) + 32 * i)
                if isinstance(i, int):
                    dst = modv[:].rearrange("p a b -> p (a b)")[:, t + 4 * i:t + 4 * i + 1]
                else:
                    dst = mod_four[:, (t - MOD_AT["up1"]) % 4:(t - MOD_AT["up1"]) % 4 + 1]
                dve.tensor_tensor_reduce(out=mod_w[:, t % 2], in0=mod_w[:, t % 2], in1=c_act[:], scale=1.0, scalar=0.0,
                                         op0=ALU.mult, op1=ALU.add,
                                         accum_out=dst).then_inc(mod_done, 1)

            def mod_vectors(layer):
                dve.wait_ge(mod_done, MOD_TILES * (layer + 1))
                dve.tensor_tensor(modv[:, layer], modv[:, layer], v("mod_b", MOD_TILES * layer, MOD_TILES),
                                  ALU.add).then_inc(mod_out, 1)
                dve.wait_ge(mod_out, layer + 1)
                for which in range(3):
                    cols = modv[:, layer, 24 * which:24 * which + 24]
                    dve.scalar_tensor_tensor(out=scales[:, layer, which], in0=cols[:, 8:16], scalar=1.0,
                                             in1=v("norm_g", 8 * (3 * layer + which), 8), op0=ALU.add, op1=ALU.mult)
                    if which == 1 and layer == 0:
                        i = dve.tensor_tensor(gates[:, layer, which], cols[:, 16:24], v("pool_scale", 0, 8), ALU.mult)
                    else:
                        i = dve.tensor_scalar(gates[:, layer, which], cols[:, 16:24], 1.0 if which == 1 else 0.5,
                                              None, ALU.mult)
                i.then_inc(mod_vec, 1)

            def up(f):
                s, pairs = seg[f"up{f}"], PAIR[f]

                def tap(half, c, i):
                    u = c - s.first
                    col = vec[:, bass.ds(VEC["conv"][0] + 3 * (u + 4 * i), 3)]
                    base = 3 * (u + 4 * i)
                    dve.wait_ge(unit_done, c + 4 * i + 1)
                    src = bank(s.tile + u)
                    dve.tensor_scalar(taps[:, half], src, col[:, 2:3], None, ALU.mult).then_inc(tap_done, 1)
                    dve.wait_ge(tap_done, base + 1)
                    dve.scalar_tensor_tensor(out=taps[:, half, 1:S], in0=src[:, 0:S - 1], scalar=col[:, 1:2],
                                             in1=taps[:, half, 1:S], op0=ALU.mult, op1=ALU.add).then_inc(tap_done, 1)
                    dve.wait_ge(tap_done, base + 2)
                    dve.scalar_tensor_tensor(out=taps[:, half, 2:S], in0=src[:, 0:S - 2], scalar=col[:, 0:1],
                                             in1=taps[:, half, 2:S], op0=ALU.mult, op1=ALU.add).then_inc(tap_done, 1)

                def body(i):
                    for q in range(2):
                        p, c = pairs + 2 * i + q, s.first + 2 * q
                        lo(c + 2, i)
                        if f == 0:
                            tap(0, c, i)
                            tap(1, c + 1, i)
                            dve.wait_ge(tap_done, 6 * (2 * i + q) + 6)
                        dve.wait_ge(silu_done, p + 1)
                        dve.wait_ge(unit_done, c + 4 * i + 2)
                        dve.tensor_tensor(hid[:, q], s_buf[:, q], taps[:, 1] if f == 0 else bank(s.tile + 2 * q + 1),
                                          ALU.mult).then_inc(hid_done, 1)
                        if f == 1:
                            mod(MOD_AT["up1"] + 2 * q, i)
                        lo(c + 3, i)
                        dve.wait_ge(hidhi_done, p + 1)
                        tile = bass.ds(2 * i + q, 1)
                        dve.tensor_tensor(hid_lo[:, tile, :].rearrange("p a n -> p (a n)"), hid[:, q],
                                          hid_hi[:, tile, :].rearrange("p a n -> p (a n)").bitcast(F32),
                                          ALU.subtract).then_inc(hidlo_done, 1)
                        if f == 1:
                            mod(MOD_AT["up1"] + 2 * q + 1, i)
                    if f == 1 and second_block and not isinstance(i, int):
                        dve.wait_ge(mod_done, MOD_AT["up1"] + 4 * i + 4)
                        dve.tensor_copy(modv[:].rearrange("p a b -> p (a b)")[:, bass.ds(MOD_AT["up1"] + 4 * i, 4)],
                                        mod_four[:]).then_inc(mod_put, 1)
                        dve.wait_ge(mod_put, i)

                for start, count in UP_RUNS[f]:
                    repeat(dve, start, count, body)

            def add_to_x(s, n, last_unit, gate):
                dve.wait_ge(unit_done, last_unit + 1)
                dve.scalar_tensor_tensor(out=xT[:, n], in0=bank(s.tile + n), scalar=gate(n), in1=xT[:, n],
                                         op0=ALU.mult, op1=ALU.add).then_inc(x_ready, 1)

            def down(f, gate):
                s = seg[f"down{f}"]
                for n in range(KD):
                    for j in range(3):
                        if n == KD - 1 and j == 2:
                            add_to_x(s, n, s.first + 3 * n + 2, gate)
                        lo(s.first + 3 * n + j + 2)
                        if s.name in MOD_AT and n < KD - 1:
                            mod(MOD_AT[s.name] + 3 * n + j)
                    if n < KD - 1:
                        add_to_x(s, n, s.first + 3 * n + 2, gate)

            def mixed_out(name, gate, tiles=range(KD)):
                s = seg[name]
                for n in tiles:
                    if n < KD - 1:
                        lo(s.first + n + 2)
                        if s.name in MOD_AT:
                            mod(MOD_AT[s.name] + n)
                    add_to_x(s, n, s.first + n, gate)
                    if n == KD - 1:
                        lo(s.first + n + 2)

            one = lambda n: ones[:, 0:1]

            def plain(name):
                return lambda k: v(name, k)

            if second_block:
                dve.wait_ge(cond_in, 32)
                for n in range(2):
                    a = lam_in[:, 2 * n * HD:(2 * n + 1) * HD]
                    dve.tensor_tensor_reduce(out=raw[:, n, 0:HD], in0=a, in1=lam_in[:, (2 * n + 1) * HD:(2 * n + 2) * HD],
                                             scale=1.0, scalar=0.0, op0=ALU.mult, op1=ALU.add,
                                             accum_out=lam_sum[:, n:n + 1]).then_inc(lam_done, 1)
                dve.wait_ge(c_done, 2)
                dve.scalar_tensor_tensor(out=neg_lam[:], in0=lam_exp[:, 1:2], scalar=-LAM_INIT, in1=lam_exp[:, 0:1],
                                         op0=ALU.add, op1=ALU.subtract).then_inc(lam_done, 1)
            for k in range(KD):
                dve.wait_ge(turned, k + 1)
                dve.tensor_copy(xT[:, k], psum[:, k % 4, :]).then_inc(x_ready, 1)
            lo(0)
            dve.wait_ge(tables, 16)
            if second_block:
                dve.tensor_scalar(sub_gain[:], v("subln"), 1.0 - LAM_INIT, None, ALU.mult)
            dve.wait_ge(filled, 2)

            if first_block:
                zero_shift = lambda k: zero[:, 0:1]
                norm(0, plain("norm_mix"), zero_shift)
                s = seg["mix_in"]
                ns_count = [0]

                def ns(name, ins):
                    assert NS_DVE[ns_count[0]] == name, (name, NS_DVE[ns_count[0]])
                    ns_count[0] += 1
                    ins.then_inc(ns_dve, 1)

                def given(name):
                    dve.wait_ge(ns_pe, upto(NS_PE, name))

                def done(name):
                    dve.wait_ge(ns_act, upto(NS_ACT, name))

                def own(name):
                    dve.wait_ge(ns_dve, upto(NS_DVE, name))

                dve.wait_ge(ns_in, 96)
                ns("pe", dve.tensor_copy(kx[:, :, :, NC], cpe[:]))
                for n in range(11):
                    dve.wait_ge(unit_done, s.first + n + 1)
                    src = bank(s.tile + n)
                    if n < 4:
                        ns(f"q{n}", dve.tensor_copy(q_n[:, n], src))
                    elif n < 6:
                        cut = src.rearrange("p (b l) -> p l b", l=CMP_STRIDE)
                        dve.tensor_copy(kx[:, n - 4, 0:CMP_STRIDE, 0:NC], cut[:, :, 0:NC])
                        ns("kv"[n - 4] + "x", dve.tensor_copy(kx[:, n - 4, CMP_STRIDE:CMP_BLOCK, 0:NC], cut[:, :, 1:NC + 1]))
                    elif n < 10:
                        name = ("ks", "vs", "kw", "vw")[n - 6]
                        ns(name, dve.tensor_copy(k_n[:, n // 2 - 3] if name[0] == "k" else raw_n[:, n // 2 - 3], src))
                    lo(s.first + n + 2)
                    mod(n)
                done("gl")
                ns("gl", dve.tensor_copy(gl[:], gl[:]))
                ns("gq", dve.tensor_scalar(gq[:], v("qk_gain", 0), HD ** -0.5, None, ALU.mult))
                done("std")
                ns("rec", dve.reciprocal(rec_n[:, 0:6].rearrange("p a t c -> p (a t c)"),
                                         stat_n[:, 0:6].rearrange("p a t c -> p (a t c)")))
                own("rec")
                for n in range(6):
                    if n >= 2:
                        given(f"rs{n - 2}")
                    ns(f"rexp{n}", dve.tensor_copy(rexp_n[:, n % 2].rearrange("p t (c d) -> p t c d", c=2),
                                                   rec_n[:, n].unsqueeze(3).to_broadcast([P, TT, 2, HD])))
                    given(f"rs{n}")
                    x = q_n[:, n] if n < 4 else k_n[:, n - 4]
                    gain = gq[:, 0:1] if n < 4 else v("qk_gain", 2 + n - 4)
                    ns(f"n{n}", dve.scalar_tensor_tensor(out=x, in0=x, scalar=gain, in1=psum[:, 4 + n % 2, :],
                                                         op0=ALU.mult, op1=ALU.mult))
                given("kc")
                ns("kc", dve.tensor_copy(kc_n[:, 0:NC], psum[:, 6, 0:NC]))
                given("vc")
                ns("vc", dve.tensor_copy(vc_t[:], psum[0:NC, 7, 0:P]))
                done("kcstd")
                ns("kcrec", dve.reciprocal(rec_n[0:NC, 6, 0], stat_n[0:NC, 6, 0]))
                own("kcrec")
                ns("kcrexp", dve.tensor_copy(rexp_n[0:NC, 0, 0].rearrange("p (c d) -> p c d", c=2),
                                             rec_n[0:NC, 6, 0].unsqueeze(2).to_broadcast([NC, 2, HD])))
                given("kcrs")
                ns("kcn", dve.scalar_tensor_tensor(out=kc_n[:, 0:NC], in0=kc_n[:, 0:NC], scalar=v("qk_gain", 1),
                                                   in1=psum[:, 5, 0:NC], op0=ALU.mult, op1=ALU.mult))
                for j in range(TT):
                    given(f"cs{j}")
                    pc = Pc[:, j, :, 0:NC]
                    over = lambda x: x.unsqueeze(1).to_broadcast([P, NSA_HEADS, NC])
                    along = lambda x: x.unsqueeze(2).to_broadcast([P, NSA_HEADS, NC])
                    ns(f"add{j}", dve.tensor_tensor(
                        Pc[:, j].rearrange("p (a b) n -> p a b n", b=2)[:, :, :, 0:NC],
                        psum[:, 2 * j:2 * j + 2, 0:P].rearrange("p b (a n) -> p a b n", n=32)[:, :, :, 0:NC],
                        cadd[:, j].unsqueeze(1).unsqueeze(1).to_broadcast([P, 4, 2, NC]), ALU.add))
                    own(f"add{j}")
                    ns(f"max{j}", dve.tensor_reduce(cmx[:], pc, AX.X, ALU.max))
                    own(f"max{j}")
                    ns(f"sub{j}", dve.tensor_tensor(pc, pc, along(cmx[:]), ALU.subtract))
                    done(f"ce{j}")
                    ns(f"sum{j}", dve.tensor_reduce(csum[:], pc, AX.X, ALU.add))
                    own(f"sum{j}")
                    ns(f"rec{j}", dve.reciprocal(csum[:], csum[:]))
                    own(f"rec{j}")
                    ns(f"coef{j}", dve.tensor_tensor(csum[:], csum[:], gate_t[:, j, 0:24:3], ALU.mult))
                    ns(f"mask{j}", dve.tensor_tensor(pc, pc, over(cmul[:, j]), ALU.mult))
                    own(f"mask{j}")
                    ns(f"p{j}", dve.tensor_tensor(pc, pc, along(csum[:]), ALU.mult))

                M = 4 * NSA_HEADS
                steps = 0

                def take_o_nsa(h):
                    rows = slice(HD * (h % 2), HD * (h % 2) + HD)
                    dve.wait_ge(npv_done, h + 1)
                    dve.tensor_copy(o_nsa[rows, h // 2], psum[rows, 6, :]).then_inc(no_done, 1)

                for m in range(M + 1):
                    if m < M:
                        h, j = m // 4, m % 4
                        dve.wait_ge(nscore_done, m + 1)
                        if m >= 2:
                            dve.wait_ge(nexp_done, 2 * (m - 1))
                        two = psum[:, 2 * (m % 2):2 * (m % 2) + 2, :]
                        dve.tensor_tensor(two[:, :, j * P:(j + 1) * P], two[:, :, j * P:(j + 1) * P],
                                          tri[:].unsqueeze(1).to_broadcast([P, 2, P]), ALU.add).then_inc(nmask_done, 1)
                        dve.wait_ge(nmask_done, m + 1)
                        dve.tensor_reduce(nmax_n[:, m % 2], two[:, :, 0:(j + 1) * P], AX.X, ALU.max,
                                          negate=True).then_inc(nmax_done, 1)
                    if 1 <= m <= M:
                        g = m - 1
                        b, h, j = g % 2, g // 4, g % 4
                        dve.wait_ge(nexp_done, 2 * g + 2)
                        dve.reciprocal(coef_n[:, b], esum_n[:, b]).then_inc(nscale_step, 1)
                        dve.wait_ge(nscale_step, steps + 1)
                        dve.tensor_tensor(coef_n[:, b], coef_n[:, b], gate_t[:, j, 3 * h + 1:3 * h + 3],
                                          ALU.mult).then_inc(nscale_step, 1)
                        dve.wait_ge(nscale_step, steps + 2)
                        for c in range(2):
                            x = Pn[:, b, c, 0:(j + 1) * P]
                            dve.tensor_scalar(x, x, coef_n[:, b, c:c + 1], None, ALU.mult).then_inc(nscale_step, 1)
                        steps += 4
                    if 1 <= m <= M:
                        if m >= 9 and (m - 9) % 4 == 0:
                            take_o_nsa((m - 9) // 4)
                take_o_nsa(NSA_HEADS - 2)
                take_o_nsa(NSA_HEADS - 1)

                dve.memset(zraw[:, 0, 0:1], 0.0).then_inc(zset, 1)
                dve.memset(zraw[:, 1, 0:1], 0.0).then_inc(zset, 1)
                dve.memset(TR[:], 0.0).then_inc(zset, 1)
                dve.memset(MR[:], 0.0).then_inc(zset, 1)
                dve.memset(Sh[:, 0], 0.0).then_inc(zset, 1)
                for n in range(14):
                    dve.wait_ge(zraw_done, n + 1)
                    z = zraw[:, n % 2]
                    tile = RW_TILES[n]
                    dve.tensor_tensor(zm[:, tile], z[:, 0:S], z[:, 1:S + 1], ALU.subtract).then_inc(zdiff_done, 1)
                    lo(s.first + 11 + n + 2)
                    dve.wait_ge(zdiff_done, n + 1)
                    dve.scalar_tensor_tensor(out=zm[:, tile], in0=zm[:, tile], scalar=v("mu", tile), in1=z[:, 1:S + 1],
                                             op0=ALU.mult, op1=ALU.add).then_inc(zm_done, 1)
                    mod(11 + n)
                dve.wait_ge(zset, 5)
                dve.wait_ge(rw_in, 64)
                dve.tensor_copy(mask8[:], AR[:].rearrange("p t a n -> p (t a n)")).then_inc(zset, 1)
                dve.wait_ge(zset, 6)

                rw_count = [0]

                def rw(p, name, ins):
                    assert RW_DVE[rw_count[0]] == (name, p), (name, p, RW_DVE[rw_count[0]])
                    rw_count[0] += 1
                    ins.then_inc(rw_dve, 1)

                def tiles(x):
                    return x.rearrange("p (t n) -> p t n", t=TT)

                def chunks(x):
                    return x.rearrange("p (c n) -> p c n", c=NCH)

                def given(p, name):
                    dve.wait_ge(rw_pe, upto(RW_PE, (name, p)))

                def done(p, name):
                    dve.wait_ge(rw_act, upto(RW_ACT, (name, p)))

                def own(p, name):
                    dve.wait_ge(rw_dve, upto(RW_DVE, (name, p)))

                lower = stri.unsqueeze(1).to_broadcast([P, 2, 2 * P])

                def keep_lower(p, name, dst, b):
                    n = int(name[2])
                    given(p, name)
                    rw(p, name, dve.copy_predicated(dst[:, 2 * n:2 * n + 2], lower,
                                                    psum[:, b, :].rearrange("p (m n) -> p m n", m=2)))

                def head(p, *names):
                    if p >= PAIRS:
                        return
                    odd = p % 2
                    r, k, val = zm[:, p], zm[:, 4 + p], zm[:, 8 + p]
                    AR, tD = ARs[odd], tDs[odd]

                    def step(name, ins):
                        rw(p, name, ins)
                        own(p, name)

                    for name in names:
                        if name == "kk0":
                            if p >= 2:
                                own(p - 2, "o")
                            step("kk0", dve.tensor_scalar(tC[:], k, v("k_k", p), None, ALU.mult))
                        if name == "cs":
                            done(p, "sw")
                            step("cs", dve.tensor_tensor_scan(Bt[:], rmask, tA[:], 0.0, ALU.mult, ALU.add))
                        if name == "rel":
                            step("rel", dve.tensor_tensor(
                                chunks(Kt[:]), chunks(Bt[:]),
                                chunks(Bt[:])[:, :, CHUNK // 2 - 1:CHUNK // 2].to_broadcast([P, NCH, CHUNK]), ALU.subtract))
                        if name == "dsum":
                            step("dsum", dve.tensor_tensor(Dc[:, odd, 0:NCH - 1], chunks(Kt[:])[:, 0:NCH - 1, CHUNK - 1],
                                                           chunks(Bt[:])[:, 1:NCH, CHUNK // 2 - 1], ALU.add))
                        if name == "relm":
                            given(p, "kss")
                            step("relm", dve.tensor_tensor(tD, Kt[:], tA[:], ALU.subtract))
                        if name == "kmax":
                            done(p, "kstd")
                            step("kmax", dve.tensor_scalar(kst[:], kst[:], 1e-12, None, ALU.max))
                        if name == "krec":
                            step("krec", dve.reciprocal(krec[:], kst[:]))
                        if name == "krexp":
                            step("krexp", dve.tensor_copy(rexp_k.rearrange("p t (c d) -> p t c d", c=2),
                                                          krec[:].unsqueeze(3).to_broadcast([P, TT, 2, HD])))
                        if name == "kkn":
                            given(p, "krs")
                            step("kkn", dve.tensor_tensor(tC[:], tC[:], psum[:, 0, :], ALU.mult))
                        if name == "a1":
                            done(p, "a")
                            step("a1", dve.tensor_scalar(tA[:], tB[:], -1.0, v("k_a", p), ALU.add, ALU.mult))
                        if name == "kh":
                            step("kh", dve.scalar_tensor_tensor(out=tA[:], in0=tA[:], scalar=1.0, in1=k, op0=ALU.add,
                                                                op1=ALU.mult))
                        if name == "A":
                            done(p, "Em")
                            step("A", dve.scalar_tensor_tensor(out=AR[:, :, 0, :], in0=tiles(tC[:]), scalar=-1.0,
                                                               in1=tiles(tD), op0=ALU.mult, op1=ALU.mult))
                        if name == "kka":
                            step("kka", dve.tensor_tensor(Bt[:], tC[:], tB[:], ALU.mult))
                        if name == "B":
                            done(p, "En")
                            step("B", dve.tensor_tensor(Bt[:], Bt[:], Kt[:], ALU.mult))
                        if name == "K":
                            step("K", dve.tensor_tensor(Kt[:], Kt[:], tA[:], ALU.mult))
                        if name == "R":
                            step("R", dve.tensor_tensor(AR[:, :, 1, :], AR[:, :, 1, :], tiles(r), ALU.mult))
                        if name == "rk":
                            step("rk", dve.scalar_tensor_tensor(out=tB[:], in0=r, scalar=v("r_k", p), in1=tA[:],
                                                                op0=ALU.mult, op1=ALU.mult))
                        if name == "bonus":
                            given(p, "bonus")
                            step("bonus", dve.tensor_tensor(tD, val, psum[:, 1, :], ALU.mult))
                        if name == "eye":
                            rw(p, "eye", dve.tensor_copy(XT[:], ident.unsqueeze(1).to_broadcast([P, 8, P])))
                        if name[0:2] == "P1":
                            keep_lower(p, name, TR, 3 + int(name[2]))

                head(0, *RW_DVE_HEAD)
                AHEAD = {1: ("relm", "kmax", "krec", "krexp"), 2: ("kkn", "a1", "kh"), 3: ("A", "kka", "B", "K"),
                         4: ("R", "rk"), 5: ("bonus",)}
                for p in range(PAIRS):
                    D_p = Dc[:, p % 2]

                    def step(name, ins, wait=True):
                        rw(p, name, ins)
                        if wait:
                            own(p, name)

                    own(p, "P13")
                    step("XT0", dve.copy_predicated(XT[:], lmask[:, 0].unsqueeze(1).to_broadcast([P, 8, P]), TR[:, :, 0:P]),
                         wait=False)
                    head(p + 1, "kk0")
                    for n in (0, 3, 1, 2):
                        keep_lower(p, f"P2{n}", MR, (7, 0, 1, 2)[n])
                    head(p + 1, "cs", "rel", "dsum")
                    for lev in range(1, 6):
                        mask = lmask[:, lev].unsqueeze(1).to_broadcast([P, 4, P])
                        for n in range(2):
                            name = f"Y{lev}" + "ab"[n]
                            given(p, name)
                            step(name, dve.copy_predicated(XT[:, 4 * n:4 * n + 4], mask,
                                                           psum[:, 4 + n, :].rearrange("p (m n) -> p m n", m=4)), wait=False)
                        head(p + 1, *AHEAD[lev])
                    given(p, "WT")
                    WT = Ap[:, 0:4].rearrange("p m n -> p (m n)")
                    Ut = Ap[:, 4:8].rearrange("p m n -> p (m n)").rearrange("p (h t d) -> p h t d", h=2, t=TT)
                    U0 = X[:, 4:8].rearrange("p m n -> p (m n)").rearrange("p (h t d) -> p h t d", h=2, t=TT)
                    step("WT", dve.tensor_copy(WT, psum[:, 2, :]), wait=False)
                    done(p, "U0")
                    for c in range(NCH):
                        t, q = c // 2, slice(CHUNK * (c % 2), CHUNK * (c % 2) + CHUNK)
                        if c < NCH - 1:
                            if c >= 1:
                                own(p, f"S{c - 1}")
                            step(f"SD{c}", dve.tensor_scalar(SD[:], Sh[:, c], D_p[:, c:c + 1], None, ALU.mult), wait=False)
                        given(p, f"u{c}")
                        step(f"U{c}", dve.tensor_tensor(Ut[q, :, t], U0[q, :, t],
                                                        psum[q, 3:5, 0:HD],
                                                        ALU.add), wait=False)
                        if c < NCH - 1:
                            own(p, f"SD{c}")
                            given(p, f"s{c}")
                            step(f"S{c}", dve.scalar_tensor_tensor(out=Sh[:, c + 1], in0=psum[:, 5 + c % 2, 0:HD],
                                                                   scalar=D_p[:, c:c + 1], in1=SD[:], op0=ALU.mult,
                                                                   op1=ALU.add), wait=False)
                    head(p + 1, "eye")
                    given(p, "mean")
                    done(p, "y")
                    step("yc", dve.scalar_tensor_tensor(out=tC[:], in0=psum[:, 0, :], scalar=-1.0 / HD, in1=tA[:],
                                                        op0=ALU.mult, op1=ALU.add))
                    head(p + 1, "P10", "P11", "P12")
                    done(p, "vstd")
                    step("vrec", dve.reciprocal(krec[:], kst[:]))
                    step("vrexp", dve.tensor_copy(X[:, 0:4].rearrange("p t (c d) -> p t c d", c=2),
                                                  krec[:].unsqueeze(3).to_broadcast([P, TT, 2, HD])))
                    head(p + 1, "P13")
                    given(p, "vrs")
                    step("yn", dve.scalar_tensor_tensor(out=tC[:], in0=tC[:], scalar=v("ln_w", p), in1=psum[:, 1, :],
                                                        op0=ALU.mult, op1=ALU.mult))
                    step("yb", dve.scalar_tensor_tensor(out=tC[:], in0=tC[:], scalar=v("ln_b", p), in1=tDs[p % 2],
                                                        op0=ALU.add, op1=ALU.add))
                    step("o", dve.tensor_tensor(zm[:, p], tC[:], keeps[p % 2], ALU.mult), wait=False)

                dve.wait_ge(rw_dve, upto(RW_DVE, ("o", PAIRS - 1)))
                for k in range(KD):
                    dve.wait_ge(osplit_hi, k + 1)
                    dve.tensor_tensor(o_lo[:, k], o_nsa[:, k] if k < 4 else zm[:, k - 4], o_hi[:, k].bitcast(F32),
                                      ALU.subtract).then_inc(osplit_lo, 1)
                s = seg["merge"]
                for n in range(KD):
                    for j in range(4):
                        u = s.first + 4 * n + j
                        dve.wait_ge(unit_done, u + 1)
                        if j == 2:
                            dve.wait_ge(sig_done, 2 * n + 1)
                            if n >= 1:
                                dve.wait_ge(ylo_done, n)
                            dve.tensor_tensor(y_t, sg[:, 0], bank(s.tile + 4 * n + 2), ALU.mult).then_inc(y_step, 1)
                        if j == 3:
                            dve.wait_ge(sig_done, 2 * n + 2)
                            dve.tensor_tensor(sg[:, 1], sg[:, 1], bank(s.tile + 4 * n + 3), ALU.mult).then_inc(y_step, 1)
                            dve.wait_ge(y_step, 3 * n + 2)
                            dve.tensor_tensor(y_t, y_t, sg[:, 1], ALU.add).then_inc(y_step, 1)
                        lo(u + 2)
                        mod(MOD_AT["merge"] + 4 * n + j)
                    dve.wait_ge(yhi_done, n + 1)
                    dve.tensor_tensor(y_lo[:, n], y_t, y_hi[:, n].bitcast(F32), ALU.subtract).then_inc(ylo_done, 1)
                mixed_out("mix_out", one)
                norm(1, plain("norm_ffn"), zero_shift)
                up(0)
                down(0, one)

            if second_block:
                if not first_block:
                    for t in range(2 * MOD_TILES):
                        mod(t)
                    mod_vectors(0)
                    mod_vectors(1)
                else:
                    mod_vectors(0)

                def scale(layer, which):
                    return lambda k: scales[:, layer, which, k:k + 1]

                def shift(layer, which):
                    return lambda k: modv[:, layer, 24 * which + k:24 * which + k + 1]

                def gate(layer, which):
                    return lambda k: gates[:, layer, which, k:k + 1]

                dve.wait_ge(mod_vec, 1)
                norm(2, scale(0, 0), shift(0, 0))
                up(1)
                down(1, gate(0, 0))

                for b in range(2):
                    dve.memset(hp[:, b, :, 0:8], 0.0).then_inc(padded, 1)
                    dve.memset(hp[:, b, :, 8 + S:16 + S], 0.0).then_inc(padded, 1)
                spread(3)
                steps = 0

                def normed(g):
                    for k in (2 * g, 2 * g + 1):
                        if k >= 2:
                            dve.wait_ge(hhi_done, KD * NORM[3] + k - 1)
                        dve.scalar_tensor_tensor(out=norm_t[:, k % 2], in0=xT[:, k], scalar=scale(0, 1)(k),
                                                 in1=psum[:, 5, :], op0=ALU.mult, op1=ALU.mult).then_inc(t_done, 1)

                normed(0)
                for g in range(4):
                    if g + 1 < 4:
                        normed(g + 1)
                    dve.wait_ge(hhi_done, KD * NORM[3] + 2 * g + 2)
                    if g >= 1:
                        dve.wait_ge(diff_done, g)
                    src, at, end = hp[:, g % 2], 0, S + 16
                    for d in range(g + 1):
                        left, right = (1, 0) if d == 0 else (2 ** (d - 1), 2 ** (d - 1))
                        a, b = at + left, end - right
                        dst = win[:, d % 2]
                        dve.tensor_tensor(dst[:, :, a:b], src[:, :, a - left:b - left], src[:, :, a + right:b + right],
                                          ALU.add).then_inc(win_done, 1)
                        steps += 1
                        dve.wait_ge(win_done, steps)
                        src, at, end = dst, a, b
                    if g == 0:
                        dve.wait_ge(tables, 32)
                    ends = src[:, :, 8:8 + S].rearrange("p e (a b) -> p e a b", b=8)[:, :, 0:S // 8:S // 8 - 1]
                    for e in range(2):
                        i = dve.tensor_tensor(ends[:, e], ends[:, e],
                                              icnt[:, 16 * g:16 * g + 16].rearrange("p (a b) -> p a b", b=8), ALU.mult)
                    i.then_inc(win_done, 1)
                    steps += 1
                    dve.wait_ge(win_done, steps)
                    if g >= 2:
                        dve.wait_ge(hlo_done, KD * NORM[3] + 2 * g - 2)
                    dve.scalar_tensor_tensor(out=diff[:, g % 2], in0=src[:, :, 8:8 + S], scalar=1.0 / (2 << g),
                                             in1=hp[:, g % 2, :, 8:8 + S], op0=ALU.mult,
                                             op1=ALU.subtract).then_inc(diff_done, 1)
                    if g >= 1:
                        mixed_out("pool", gate(0, 1), (2 * g - 2, 2 * g - 1))
                mixed_out("pool", gate(0, 1), (KD - 2, KD - 1))
                norm(4, scale(0, 2), shift(0, 2))
                up(2)
                down(2, gate(0, 2))
                if first_block:
                    mod_vectors(1)
                dve.wait_ge(mod_vec, 2)
                norm(5, scale(1, 0), shift(1, 0))
                up(3)
                down(3, gate(1, 0))
                norm(6, scale(1, 1), shift(1, 1))

                s = seg["qkv"]
                dve.wait_ge(tables, 48)
                rope_step = 0
                for n in range(25):
                    if n < 24:
                        dve.wait_ge(unit_done, s.first + n + 1)
                        if n >= 10:
                            dve.wait_ge(roped, 3 * (n - 9))
                        dve.tensor_copy(raw[:, n % 2], bank(s.tile + n)).then_inc(raw_done, 1)
                        lo(s.first + n + 2)
                    if n >= 9:
                        m = n - 1
                        dst = (k_t if m < 16 else q_t)[:, m % 8]
                        by = 1.0 if m < 16 else HD ** -0.5
                        dve.wait_ge(post_done, n)
                        dve.wait_ge(raw_done, n)
                        dve.scalar_tensor_tensor(out=dst, in0=psum[:, 4 + m % 2, :], scalar=by, in1=rope[:, 1],
                                                 op0=ALU.mult, op1=ALU.mult).then_inc(roped, 1)
                        dve.scalar_tensor_tensor(out=raw[:, m % 2], in0=raw[:, m % 2], scalar=by, in1=rope[:, 0],
                                                 op0=ALU.mult, op1=ALU.mult).then_inc(roped, 1)
                        rope_step += 2
                        dve.wait_ge(roped, rope_step)
                        dve.tensor_tensor(dst, dst, raw[:, m % 2], ALU.add).then_inc(roped, 1)
                        rope_step += 1

                steps = 0
                M = 4 * DIFF_HEADS
                def take_o(h):
                    dve.wait_ge(pv_done, h + 1)
                    dve.tensor_copy(o_raw[:, h], psum[:, 6 + h % 2, :]).then_inc(o_done, 1)

                for m in range(M + 3):
                    if m < M:
                        dve.wait_ge(score_done, m + 1)
                        if m >= 2:
                            dve.wait_ge(exp_done, 2 * (m - 1))
                        dve.tensor_reduce(nmax[:, m % 2], psum[:, 2 * (m % 2):2 * (m % 2) + 2, :], AX.X, ALU.max,
                                          negate=True).then_inc(max_done, 1)
                    if 1 <= m <= M:
                        g = m - 1
                        b = g % 2
                        dve.wait_ge(exp_done, 2 * g + 2)
                        dve.reciprocal(coef[:, b], esum[:, b]).then_inc(comb_step, 1)
                        dve.wait_ge(comb_step, steps + 1)
                        dve.tensor_scalar(E[:, b, 1], E[:, b, 1], coef[:, b, 1:2], neg_lam[:, 0:1], ALU.mult,
                                          ALU.mult).then_inc(comb_step, 1)
                        dve.wait_ge(comb_step, steps + 2)
                        dve.scalar_tensor_tensor(out=E[:, b, 0], in0=E[:, b, 0], scalar=coef[:, b, 0:1], in1=E[:, b, 1],
                                                 op0=ALU.mult, op1=ALU.add).then_inc(comb_step, 1)
                        steps += 3
                    if m >= 10 and (m - 10) % 4 == 0:
                        take_o((m - 10) // 4)
                take_o(DIFF_HEADS - 1)
                dve.wait_ge(ostd_done, 1)
                dve.reciprocal(orstd[:], ostd[:]).then_inc(orstd_done, 1)
                dve.wait_ge(orstd_done, 1)
                for h in range(DIFF_HEADS + 2):
                    if h < DIFF_HEADS:
                        if h >= 2:
                            dve.wait_ge(obc_done, h - 1)
                        dve.tensor_copy(rexp[:, h % 2], orstd[:, 4 * h:4 * h + 4].unsqueeze(2).to_broadcast(
                            [P, TT, P])).then_inc(orexp_done, 1)
                    if 1 <= h <= DIFF_HEADS:
                        g = h - 1
                        dve.wait_ge(obc_done, g + 1)
                        if g >= 2:
                            dve.wait_ge(olo_done, g - 1)
                        dve.scalar_tensor_tensor(out=norm_t[:, g % 2], in0=o_raw[:, g], scalar=sub_gain[:, 0:1],
                                                 in1=psum[:, 5 + g % 2, :], op0=ALU.mult,
                                                 op1=ALU.mult).then_inc(ot_done, 1)
                    if h >= 2:
                        g = h - 2
                        dve.wait_ge(ohi_done, g + 1)
                        dve.tensor_tensor(h_lo[:, g], norm_t[:, g % 2], h_hi[:, g].bitcast(F32),
                                          ALU.subtract).then_inc(olo_done, 1)
                mixed_out("attn_out", gate(1, 1))
                norm(7, scale(1, 2), shift(1, 2))
                up(4)
                down(4, gate(1, 2))

            n_norm = last_norm
            spread(n_norm)
            for k in range(KD):
                if k >= 2:
                    dve.wait_ge(xt_done, k - 1)
                dve.scalar_tensor_tensor(out=y_out[:, k % 2], in0=xT[:, k], scalar=v("final_g", k),
                                         in1=psum[:, 5, :], op0=ALU.mult, op1=ALU.mult).then_inc(t_done, 1)

        @block.tensor
        def _(pe):
            def product(c, i, k_tiles, acts, tile, start, stop):
                c, i = fixed(c, i)
                kt, cols = shape_of(c)
                pe.wait_ge(lo_done, c + 4 * i + 1)
                wh, wl = slot(w_hi, c, kt, cols, 2), slot(w_lo, c, kt, cols, 2)
                a_hi, a_lo = acts
                dst = bank(tile)[0:cols, :]
                for n, k in enumerate(k_tiles):
                    pe.matmul(dst, wh[:, n], a_hi[:, k], start=start and n == 0, stop=False)
                    pe.matmul(dst, wh[:, n], a_lo[:, k], start=False, stop=False)
                    m = pe.matmul(dst, wl[:, n], a_hi[:, k], start=False, stop=stop and n == kt - 1)
                m.then_inc(unit_done, 1)

            def sum_squares(n_norm, k):
                pe.wait_ge(sq_done, KD * NORM[n_norm] + k + 1)
                for tt in range(TT):
                    m = pe.matmul(psum[:, 4, tt:tt + 1], sq(n_norm, k)[:, tt * P:(tt + 1) * P], ones[:, 0:1],
                                  start=(k == 0 and tt == 0), stop=(k == KD - 1), skip_group_check=True)
                m.then_inc(ssq_done, 1)

            def spread_rstd(n_norm):
                pe.wait_ge(rexp_done, NORM[n_norm] + 1)
                for tt in range(TT):
                    m = pe.transpose(psum[:, 5, tt * P:(tt + 1) * P], rexp[:, 0, tt], ident)
                m.then_inc(rbc_done, 1)

            def up(f, n_norm):
                s, pairs = seg[f"up{f}"], PAIR[f]

                def body(i):
                    for j in range(4):
                        if not (isinstance(i, int) and i == 0):
                            pe.wait_ge(hid_done, pairs + 2 * i - 1 + j // 2)
                        if isinstance(i, int) and i == 0 and j < 2:
                            if j == 0:
                                first_units(s, n_norm)
                        else:
                            product(s.first + j, i, range(KD), (h_hi, h_lo), s.tile + j, True, True)

                for start, count in UP_RUNS[f]:
                    repeat(pe, start, count, body)

            def first_units(s, n_norm):
                kt, cols = shape_of(s.first)
                for k in range(KD + LAG):
                    for e, at in ((0, k), (1, k - LAG)):
                        if not 0 <= at < KD:
                            continue
                        c = s.first + e
                        if at == 0:
                            pe.wait_ge(lo_done, c + 1)
                        if e == 0:
                            pe.wait_ge(hhi_done, KD * NORM[n_norm] + k + 1)
                        wh, wl, dst = slot(w_hi, c, kt, cols, 2), slot(w_lo, c, kt, cols, 2), bank(s.tile + e)
                        pe.matmul(dst, wh[:, at], h_hi[:, at], start=at == 0, stop=False)
                        pe.matmul(dst, wl[:, at], h_hi[:, at], start=False, stop=False)
                        if e == 0:
                            pe.wait_ge(hlo_done, KD * NORM[n_norm] + k + 1)
                        m = pe.matmul(dst, wh[:, at], h_lo[:, at], start=False, stop=at == KD - 1)
                        if at == KD - 1:
                            m.then_inc(unit_done, 1)

            def down(f, n_norm):
                s, pairs = seg[f"down{f}"], PAIR[f]
                for n in range(KD):
                    if n < 4:
                        pe.wait_ge(hid_done, pairs + KF)
                    else:
                        pe.wait_ge(x_ready, KD * NORM[n_norm] + n - 3)
                    for j, (k0, kt) in enumerate(DOWN):
                        pe.wait_ge(hidlo_done, pairs + k0 + kt)
                        product(s.first + 3 * n + j, 0, range(k0, k0 + kt), (hid_hi, hid_lo), s.tile + n, j == 0, j == 2)
                    if n >= 1:
                        sum_squares(n_norm, n - 1)
                sum_squares(n_norm, KD - 1)

            def mixed_out(name, n_norm, operands):
                s = seg[name]
                for n in range(KD):
                    if n >= 4:
                        pe.wait_ge(x_ready, KD * NORM[n_norm] + n - 3)
                    operands(n)
                    if n >= 1:
                        sum_squares(n_norm, n - 1)
                sum_squares(n_norm, KD - 1)

            pe.wait_ge(cst_in, 16)
            for k in range(KD):
                pe.wait_ge(x_in[k // 2], 16)
                if k >= 4:
                    pe.wait_ge(x_ready, k - 3)
                for tt in range(TT):
                    m = pe.transpose(psum[:, k % 4, tt * P:(tt + 1) * P], x_tok[:, tt, k * P:(k + 1) * P], ident)
                m.then_inc(turned, 1)
            for k in range(KD):
                sum_squares(0 if first_block else 2, k)

            if first_block:
                spread_rstd(0)
                s = seg["mix_in"]
                ns_count = [0]

                def ns(name, last):
                    assert NS_PE[ns_count[0]] == name, (name, NS_PE[ns_count[0]])
                    ns_count[0] += 1
                    last.then_inc(ns_pe, 1)

                def took(name):
                    pe.wait_ge(ns_act, upto(NS_ACT, name))

                def made(name):
                    pe.wait_ge(ns_dve, upto(NS_DVE, name))

                def turn(dst, src, rows=P):
                    for t in range(TT):
                        last = pe.transpose(dst[:, t], src[:, t * P:(t + 1) * P], ident[0:rows, 0:rows])
                    return last

                def cols_of(b, n=P):
                    return psum[:, b, 0:TT * n].rearrange("p (t n) -> p t n", t=TT)

                evac = ["q0", "q1", "q2", "q3", "kx", "vx", "ks", "vs", "kw", "vw"]
                for n in range(11):
                    if n >= 4:
                        made(evac[n - 4])
                    if n == 0:
                        first_units(s, 0)
                    elif n >= 2:
                        product(s.first + n, 0, range(KD), (h_hi, h_lo), s.tile + n, True, True)
                made("vs")
                ns("vs", turn(cols_of(4), raw_n[:, 0]))
                made("vw")
                ns("vw", turn(cols_of(5), raw_n[:, 1]))
                made("gl")
                ns("gt", turn(cols_of(6, 24), gl, 24))
                head_of = pair_ones[:, 0:P:HD]
                for n in range(6):
                    took(f"sq{n}")
                    for t in range(TT):
                        c = 8 + 8 * n + 2 * t
                        last = pe.matmul(psum[:, 7, c:c + 2], raw_n[:, n % 2, t * P:(t + 1) * P], head_of,
                                         start=True, stop=True)
                    ns(f"ss{n}", last)
                def compress(first, count):
                    for c, place in [divmod(i, CMP_BLOCK) for i in range(first, first + count)]:
                        last = pe.matmul(psum[:, c, 0:32], w1_c[:, c, place], kx[:, c, place], start=place == 0,
                                         stop=place == CMP_BLOCK - 1)
                        if place == CMP_BLOCK - 1:
                            ns(f"c{c}", last)

                for n in range(6):
                    compress(6 * n + (2 if n else 0), 6 if n else 8)
                    made(f"rexp{n}")
                    if n >= 2:
                        made(f"n{n - 2}")
                    for t in range(TT):
                        last = pe.transpose(psum[:, 4 + n % 2, t * P:(t + 1) * P], rexp_n[:, n % 2, t], ident)
                    ns(f"rs{n}", last)
                compress(38, 2 * CMP_BLOCK - 38)
                took("h0")
                ns("kc", pe.matmul(psum[:, 6, 0:NC], w2_c[:, 0], hid_c[:, 0, 0:NC], start=True, stop=True))
                took("h1")
                ns("vc", pe.matmul(psum[0:NC, 7, 0:P], hid_c[:, 1, 0:NC], w2_c[:, 1], start=True, stop=True))
                took("kcsq")
                made("n5")
                ns("kcss", pe.matmul(psum[0:NC, 4, 0:2], raw_n[:, 0, 0:NC], head_of, start=True, stop=True))
                made("kcrexp")
                ns("kcrs", pe.transpose(psum[:, 5, 0:NC], rexp_n[0:NC, 0, 0], ident[0:NC, 0:NC]))
                took("kcd3")
                for j in range(TT):
                    for h in range(NSA_HEADS):
                        rows = slice(HD * (h % 2), HD * (h % 2) + HD)
                        c = 32 * (h // 2)
                        last = pe.matmul(psum[:, 2 * j + h % 2, c:c + NC], q_n[rows, h // 2, j * P:(j + 1) * P],
                                         kcd[rows, h // 4, 0:NC], start=True, stop=True)
                    ns(f"cs{j}", last)

                took(f"ce{TT - 1}")
                made(f"p{TT - 1}")
                M = 4 * NSA_HEADS

                def weigh_n(h, part):
                    rows = slice(HD * (h % 2), HD * (h % 2) + HD)
                    g = slice(HD * (h // 4), HD * (h // 4) + HD)
                    if part == 0:
                        pe.wait_ge(npt_done, 12 * (h + 1))
                        if h >= 1:
                            pe.wait_ge(no_done, h)
                        pe.matmul(psum[rows, 6, :], vc_t[:, g], PTc[:, h % 2], start=True, stop=False)
                    c = part // 2
                    for kt in range(1, TT) if part % 2 else range(1):
                        last = pe.matmul(psum[rows, 6, kt * P:S], v_nt[:, c, kt, g], PTn[:, h % 2, c, kt, kt * P:S],
                                         start=False, stop=c == 1 and kt == TT - 1)
                    if part == 3:
                        last.then_inc(npv_done, 1)

                for m in range(M + 2):
                    if m < M:
                        h, j = m // 4, m % 4
                        rows = slice(HD * (h % 2), HD * (h % 2) + HD)
                        if m >= 2:
                            pe.wait_ge(nexp_done, 2 * (m - 1))
                        for c in range(2):
                            last = pe.matmul(psum[:, 2 * (m % 2) + c, 0:(j + 1) * P], q_n[rows, h // 2, j * P:(j + 1) * P],
                                             kd[rows, c, h // 4, 0:(j + 1) * P], start=True, stop=True)
                        last.then_inc(nscore_done, 1)
                    if m >= 2:
                        g = m - 2
                        h, j = g // 4, g % 4
                        pe.wait_ge(nscale_step, 4 * (g + 1))
                        if g >= 1:
                            pe.wait_ge(npt_done, 3 * g)
                        pe.transpose(psum[0:NC, 7, 0:P], Pc[:, j, h, 0:NC], ident)
                        for c in range(2):
                            for kt in range(j + 1):
                                last = pe.transpose(psum[:, 4 + c, kt * P:(kt + 1) * P],
                                                    Pn[:, g % 2, c, kt * P:(kt + 1) * P], ident)
                        last.then_inc(nturned, 1)
                    if m >= 6:
                        weigh_n((m - 6) // 4, (m - 6) % 4)
                for part in range(4):
                    weigh_n(NSA_HEADS - 1, part)

                for n in range(14):
                    if n >= 4:
                        pe.wait_ge(zraw_done, n - 3)
                    product(s.first + 11 + n, 0, range(KD), (h_hi, h_lo), s.tile + 11 + n, True, True)
                pe.wait_ge(zraw_done, 14)
                pe.wait_ge(zact_done, 2)
                pe.wait_ge(rw_in, 64)

                rw_count = [0]

                def rw(p, name, last):
                    assert RW_PE[rw_count[0]] == (name, p), (name, p, RW_PE[rw_count[0]])
                    rw_count[0] += 1
                    last.then_inc(rw_pe, 1)

                def took(p, name):
                    pe.wait_ge(rw_act, upto(RW_ACT, (name, p)))

                def made(p, name):
                    pe.wait_ge(rw_dve, upto(RW_DVE, (name, p)))

                def scores(p, name, src, b):
                    for m in (2 * int(name[2]), 2 * int(name[2]) + 1):
                        rows, t = slice(HD * (m // 4), HD * (m // 4) + HD), m % 4
                        last = pe.matmul(psum[:, b, (m % 2) * 2 * P:(m % 2 + 1) * 2 * P], src[rows, t * P:(t + 1) * P],
                                         ARs[p % 2][rows, t].rearrange("p a n -> p (a n)"), start=True, stop=True)
                    rw(p, name, last)

                def head(p, *names):
                    if p >= PAIRS:
                        return
                    odd, cols = p % 2, slice(p * P, (p + 1) * P)
                    for name in names:
                        if name == "w":
                            if p >= 1:
                                took(p - 1, "tokK")
                            rw(p, "w", pe.matmul(psum[:, 0, :], low_up[0:HD, cols], zm[0:HD, 12], start=True, stop=True))
                        if name == "a":
                            if p >= 2:
                                made(p - 2, "yn")
                            rw(p, "a", pe.matmul(psum[:, 1, :], low_up[HD:P, cols], zm[HD:P, 12], start=True, stop=True))
                        if name == "g":
                            made(p, "kkn")
                            rw(p, "g", pe.matmul(psum[:, 0, :], g_up[:, cols], zm[:, 13], start=True, stop=True))
                        if name == "kss":
                            took(p, "kkq")
                            if p >= 1:
                                made(p - 1, "P22")
                            for t in range(TT):
                                last = pe.matmul(psum[:, 1, 2 * t:2 * t + 2], tDs[odd][:, t * P:(t + 1) * P], head_of,
                                                 start=True, stop=True)
                            rw(p, "kss", last)
                        if name == "krs":
                            made(p, "krexp")
                            took(p, "sw")
                            for t in range(TT):
                                last = pe.transpose(psum[:, 0, t * P:(t + 1) * P], rexp_k[:, t], ident)
                            rw(p, "krs", last)
                        if name == "bonus":
                            made(p, "rk")
                            rw(p, "bonus", pe.matmul(psum[:, 1, :], pair_ones, tB[:], start=True, stop=True))
                        if name[0:3] == "tok":
                            if p >= 1 and name == "tokB":
                                took(p - 1, "y")
                            if name == "tokK":
                                if p == 0:
                                    took(0, "g")
                                else:
                                    made(p - 1, "yc")
                            if p == 0:
                                made(0, "bonus")
                            elif name == "tokA":
                                made(p - 1, f"S{NCH - 2}")
                            src, b = {"A": (ARs[odd][:, :, 0, :], 6), "B": (Bt, 7), "K": (Kt, 0), "V": (zm[:, 8 + p], 2)}[name[3]]
                            for t in range(TT):
                                last = pe.transpose(psum[:, b, t * P:(t + 1) * P],
                                                    src[:, t] if name == "tokA" else src[:, t * P:(t + 1) * P], ident)
                            rw(p, name, last)
                        if name[0:2] == "P1":
                            if name == "P13":
                                took(p, "tokA")
                            scores(p, name, Bt, 3 + int(name[2]))

                def each(n, b, f):
                    for m in range(4 * n, 4 * n + 4):
                        last = f(psum[:, b, (m % 4) * P:(m % 4 + 1) * P], m)
                    return last

                head(0, *RW_PE_HEAD)
                for p in range(PAIRS):
                    more = p + 1 < PAIRS
                    took(p, "tokB")
                    scores(p, "P20", Kt, 7)
                    head(p + 1, "w", "a")
                    took(p, "tokV")
                    scores(p, "P23", Kt, 2)
                    if more:
                        took(p + 1, "sw")
                    else:
                        took(p, "tokK")
                    scores(p, "P21", Kt, 0)
                    if more:
                        took(p + 1, "a")
                    elif p >= 1:
                        made(p - 1, "yn")
                    scores(p, "P22", Kt, 1)
                    made(p, "P20")
                    made(p, "XT0")
                    for n in range(2):
                        rw(p, "X0" + "ab"[n], each(n, 6 + n, lambda dst, m: pe.transpose(dst, XT[:, m], ident)))
                    made(p, "P23")
                    for lev in range(1, 6):
                        for n in range(2):
                            took(p, f"X{lev - 1}" + "ab"[n])
                            rw(p, f"A{lev}" + "ab"[n], each(n, 2 + n, lambda dst, m: pe.matmul(
                                dst, TR[:, m, 0:P], X[:, m], start=True, stop=True)))
                        head(p + 1, *{1: ("kss",), 2: ("krs",), 3: (), 4: ("g",), 5: ("bonus",)}[lev])
                        for n in range(2):
                            took(p, f"A{lev}" + "ab"[n])
                            rw(p, f"Y{lev}" + "ab"[n], each(n, 4 + n, lambda dst, m: pe.matmul(
                                dst, Ap[:, m], XT[:, m], start=True, stop=True)))
                        if lev < 5:
                            for n in range(2):
                                made(p, f"Y{lev}" + "ab"[n])
                                rw(p, f"X{lev}" + "ab"[n], each(n, 6 + n, lambda dst, m: pe.transpose(dst, XT[:, m], ident)))
                    MV = X[:, 0:4].rearrange("p m n -> p (m n)")
                    made(p, "Y5b")
                    if more:
                        took(p + 1, "g")
                    else:
                        made(p, "P21")
                    for m in range(8):
                        t, hd = m % 4, slice(HD * (m // 4), HD * (m // 4) + HD)
                        last = pe.matmul(psum[:, 0, HD * m:HD * m + HD], MR[:, m, 0:P], tok[:, 3, t, hd], start=True, stop=True)
                    rw(p, "MV", last)
                    took(p, "MV")
                    made(*((p + 1, "bonus") if more else (p, "P22")))
                    for m in range(8):
                        last = pe.matmul(psum[:, 1, HD * m:HD * m + HD], XT[:, m], MV[:, HD * m:HD * m + HD], start=True, stop=True)
                    rw(p, "U0", last)
                    for m in range(8):
                        t, hd = m % 4, slice(HD * (m // 4), HD * (m // 4) + HD)
                        last = pe.matmul(psum[hd, 2, t * P:(t + 1) * P], tok[:, 0, t, hd], XT[:, m], start=True, stop=True)
                    rw(p, "WT", last)
                    made(p, "WT")
                    WT = Ap[:, 0:4].rearrange("p m n -> p (m n)")
                    Ut = Ap[:, 4:8].rearrange("p m n -> p (m n)").rearrange("p (h t d) -> p h t d", h=2, t=TT)
                    for c in range(NCH):
                        t, q = c // 2, slice(CHUNK * (c % 2), CHUNK * (c % 2) + CHUNK)
                        if c >= 1:
                            made(p, f"S{c - 1}")
                        for hb in range(2):
                            hd = slice(HD * hb, HD * hb + HD)
                            last = pe.matmul(psum[q, 3 + hb, 0:HD], WT[hd, CHUNK * c:CHUNK * c + CHUNK], Sh[hd, c],
                                             start=True, stop=True)
                        rw(p, f"u{c}", last)
                        if c < NCH - 1:
                            for hb in range(2):
                                hd = slice(HD * hb, HD * hb + HD)
                                pe.matmul(psum[hd, 5 + c % 2, 0:HD], tok[q, 2, t, hd], tok[q, 3, t, hd], start=True, stop=False)
                            made(p, f"U{c}")
                            for hb in range(2):
                                hd = slice(HD * hb, HD * hb + HD)
                                last = pe.matmul(psum[hd, 5 + c % 2, 0:HD], tok[q, 1, t, hd], Ut[q, hb, t], start=False, stop=True)
                            rw(p, f"s{c}", last)
                    made(p, f"U{NCH - 1}")
                    for hb in range(2):
                        hd = slice(HD * hb, HD * hb + HD)
                        for t in range(TT):
                            m = 4 * hb + t
                            dst = psum[hd, 7, t * P:(t + 1) * P]
                            pe.matmul(dst, Ut[:, hb, t], TR[:, m, P:2 * P], start=True, stop=False)
                            pe.matmul(dst, tok[:, 3, t, hd], MR[:, m, P:2 * P], start=False, stop=False)
                            for q in range(2):
                                part = psum[hd, 7, t * P + CHUNK * q:t * P + CHUNK * q + CHUNK]
                                last = pe.matmul(part, Sh[hd, 2 * t + q], ARs[p % 2][hd, t, 1, CHUNK * q:CHUNK * q + CHUNK],
                                                 start=False, stop=q == 1)
                    rw(p, "y", last)
                    head(p + 1, "tokA")
                    took(p, "y")
                    rw(p, "mean", pe.matmul(psum[:, 0, :], pair_ones, tA[:], start=True, stop=True))
                    head(p + 1, "tokB", "tokV", "P10", "P11", "P12")
                    took(p, "ysq")
                    for t in range(TT):
                        last = pe.matmul(psum[:, 1, 2 * t:2 * t + 2], tB[:, t * P:(t + 1) * P], head_of, start=True, stop=True)
                    rw(p, "vss", last)
                    head(p + 1, "tokK", "P13")
                    made(p, "vrexp")
                    for t in range(TT):
                        last = pe.transpose(psum[:, 1, t * P:(t + 1) * P], X[:, t], ident)
                    rw(p, "vrs", last)
                pe.wait_ge(rw_dve, upto(RW_DVE, ("yn", PAIRS - 1)))

                s = seg["merge"]
                for n in range(KD):
                    for j in range(4):
                        tile = s.tile + 4 * n + j
                        if n >= 1:
                            pe.wait_ge(y_step, 3 * n if j >= 2 else 3 * n - 2)
                        if j < 2:
                            product(s.first + 4 * n + j, 0, range(KD), (h_hi, h_lo), tile, True, True)
                        else:
                            pe.wait_ge(osplit_lo, 4 * (j - 1))
                            product(s.first + 4 * n + j, 0, range(4 * (j - 2), 4 * (j - 1)), (o_hi, o_lo), tile, True, True)

                def y_unit(n):
                    if n == 0:
                        c = seg["mix_out"].first
                        pe.wait_ge(lo_done, c + 1)
                        wh, wl, dst = slot(w_hi, c, KD, P, 2), slot(w_lo, c, KD, P, 2), bank(seg["mix_out"].tile)
                        for k in range(KD):
                            pe.wait_ge(ylo_done, k + 1)
                            pe.matmul(dst, wh[:, k], y_hi[:, k], start=k == 0, stop=False)
                            pe.matmul(dst, wh[:, k], y_lo[:, k], start=False, stop=False)
                            m = pe.matmul(dst, wl[:, k], y_hi[:, k], start=False, stop=k == KD - 1)
                        m.then_inc(unit_done, 1)
                        return
                    product(seg["mix_out"].first + n, 0, range(KD), (y_hi, y_lo), seg["mix_out"].tile + n, True, True)

                mixed_out("mix_out", 1, y_unit)
                spread_rstd(1)
                up(0, 1)
                down(0, 2 if second_block else 8)

            if second_block:
                spread_rstd(2)
                up(1, 2)
                down(1, 3)
                spread_rstd(3)

                def pool_units(n):
                    if n == 0:
                        pe.wait_ge(hlo_done, KD * NORM[3] + 2)
                    if n % 2 == 0:
                        pe.wait_ge(hlo_done, KD * NORM[3] + 2 * (n // 2) + 2)
                    product(seg["pool"].first + n, 0, [2 * (n // 2), 2 * (n // 2) + 1], (h_hi, h_lo),
                            seg["pool"].tile + n, True, True)

                mixed_out("pool", 4, pool_units)
                spread_rstd(4)
                up(2, 4)
                down(2, 5)
                spread_rstd(5)
                up(3, 5)
                down(3, 6)
                spread_rstd(6)

                s = seg["qkv"]
                for n in range(25):
                    if n < 24:
                        if n >= 4:
                            pe.wait_ge(raw_done, n - 3)
                        if n == 0:
                            first_units(s, 6)
                        elif n >= 2:
                            product(s.first + n, 0, range(KD), (h_hi, h_lo), s.tile + n, True, True)
                    if n >= 1:
                        m = n - 1
                        pe.wait_ge(raw_done, m + 1)
                        if m >= 10:
                            pe.wait_ge(roped, 3 * (m - 9))
                        elif m >= 2:
                            pe.wait_ge(vtok_done, min(m - 1, 8))
                        if m < 8:
                            for tt in range(TT):
                                last = pe.transpose(psum[:, 4 + m % 2, tt * P:(tt + 1) * P],
                                                    raw[:, m % 2, tt * P:(tt + 1) * P], ident)
                        else:
                            last = pe.matmul(psum[:, 4 + m % 2, :], perm, raw[:, m % 2], start=True, stop=True)
                        last.then_inc(post_done, 1)

                pe.wait_ge(roped, 48)
                pe.wait_ge(vtok_done, 8)
                M = 4 * DIFF_HEADS

                def weigh(h, kt):
                    if kt == 0:
                        pe.wait_ge(pt_done, 4 * h + 4)
                        if h >= 2:
                            pe.wait_ge(o_done, h - 1)
                    m = pe.matmul(psum[:, 6 + h % 2, :], v_tok[:, kt, h * P:(h + 1) * P], PT[:, h % 2, kt],
                                  start=kt == 0, stop=kt == TT - 1)
                    if kt == TT - 1:
                        m.then_inc(pv_done, 1)

                for m in range(M + 2):
                    if m < M:
                        h, j = m // 4, m % 4
                        if m >= 2:
                            pe.wait_ge(exp_done, 2 * (m - 1))
                        for c in range(2):
                            rows = slice(HD * c, HD * c + HD)
                            last = pe.matmul(psum[:, 2 * (m % 2) + c, :], q_t[rows, h, j * P:(j + 1) * P],
                                             k_t[rows, h, :], start=True, stop=True)
                        last.then_inc(score_done, 1)
                    if m >= 2:
                        g = m - 2
                        pe.wait_ge(comb_step, 3 * (g + 1))
                        if g >= 2:
                            pe.wait_ge(pt_done, g - 1)
                        for kt in range(TT):
                            last = pe.transpose(psum[:, 4 + g % 2, kt * P:(kt + 1) * P],
                                                E[:, g % 2, 0, kt * P:(kt + 1) * P], ident)
                        last.then_inc(a_turned, 1)
                    if m >= 6:
                        weigh((m - 6) // 4, (m - 6) % 4)
                for kt in range(TT):
                    weigh(DIFF_HEADS - 1, kt)
                for h in range(DIFF_HEADS):
                    pe.wait_ge(osq_done, h + 1)
                    for tt in range(TT):
                        last = pe.matmul(psum[:, 4, 4 * h + tt:4 * h + tt + 1], norm_t[:, h % 2, tt * P:(tt + 1) * P],
                                         ones[:, 0:1], start=True, stop=True)
                    last.then_inc(ossq_done, 1)
                for h in range(DIFF_HEADS):
                    pe.wait_ge(orexp_done, h + 1)
                    if h >= 2:
                        pe.wait_ge(ot_done, h - 1)
                    for tt in range(TT):
                        last = pe.transpose(psum[:, 5 + h % 2, tt * P:(tt + 1) * P], rexp[:, h % 2, tt], ident)
                    last.then_inc(obc_done, 1)
                pe.wait_ge(olo_done, DIFF_HEADS)
                mixed_out("attn_out", 7, lambda n: product(seg["attn_out"].first + n, 0, range(KD), (h_hi, h_lo),
                                                          seg["attn_out"].tile + n, True, True))
                spread_rstd(7)
                up(4, 7)
                down(4, 8)

            spread_rstd(last_norm)
            base = KD * NORM[last_norm]
            for k in range(KD):
                pe.wait_ge(t_done, base + k + 1)
                if k >= 4:
                    pe.wait_ge(out_copied, k - 3)
                for tt in range(TT):
                    m = pe.transpose(psum[:, k % 4, tt * P:(tt + 1) * P], y_out[:, k % 2, tt * P:(tt + 1) * P], ident)
                m.then_inc(xt_done, 1)


def units_of(w, kt):
    k, n = w.shape
    return np.ascontiguousarray(w.reshape(kt, P, n // P, P).transpose(2, 1, 0, 3)).reshape(n // P, P, kt * P)


def columns(x):
    return np.ascontiguousarray(np.asarray(x).reshape(-1, P).T)


def constants():
    eye = np.eye(P, dtype=np.float32)
    pair = np.kron(np.eye(2, dtype=np.float32), np.ones((HD, HD), np.float32))
    perm = np.zeros((P, P), np.float32)
    rot = HD // 4
    half = rot // 2
    for h in range(2):
        for r in range(half):
            perm[HD * h + half + r, HD * h + r] = -1.0
            perm[HD * h + r, HD * h + half + r] = 1.0
    cst = np.concatenate([eye, np.ones((P, P), np.float32), pair, perm], axis=1)
    inv = (1.0 / (np.float32(500000.0) ** (np.arange(0, rot, 2, dtype=np.float32) / np.float32(rot)))).astype(np.float32)
    ang = (np.arange(S, dtype=np.float32)[:, None] * inv[None, :]).astype(np.float32)
    rope = np.zeros((P, 2, S), np.float32)
    rope[:, 0] = 1.0
    for h in range(2):
        for s in range(2):
            rows = slice(HD * h + half * s, HD * h + half * (s + 1))
            rope[rows, 0] = np.cos(ang).T
            rope[rows, 1] = np.sin(ang).T
    t = np.arange(S)
    icnt = np.stack([w / (np.minimum(t + w // 2, S) - np.maximum(t - w // 2, 0)) for w in (2, 4, 8, 16)])
    icnt = np.concatenate([icnt[:, 0:8], icnt[:, S - 8:S]], axis=1)
    return cst, rope, icnt.astype(np.float32).reshape(1, 4 * 16)


def arrays_of(inputs):
    x = {k: np.asarray(a) for k, a in inputs.items()}
    a = {"x": x["x"][0]}
    gain = np.concatenate([x["qk_gain"][0], x["qk_gain"][0]], axis=1)
    parts = {"norm_mix": columns(x["norm_mix"][0]), "norm_ffn": columns(x["norm_ffn"][0]), 
             "final_g": columns(x["final_g_2"]), "pool_scale": columns(x["pool_scale_2"]),
             "subln": columns(x["diff_subln_g_2"]), "norm_g": columns(x["norm_g_2"]),
             "conv": x["ffn_conv"][0].reshape(3, 2, KF, P).transpose(3, 2, 1, 0).reshape(P, 132),
             "mod_b": columns(x["mod_b_2"]), "mu": columns(x["rwkv_mu"][0]), "w0": columns(x["rwkv_w0"][0]),
             "a0": columns(x["rwkv_a0"][0]), "k_k": columns(x["rwkv_k_k"][0]), "k_a": columns(x["rwkv_k_a"][0]),
             "r_k": columns(x["rwkv_r_k"][0]), "ln_w": columns(x["rwkv_ln_w"][0]), "ln_b": columns(x["rwkv_ln_b"][0]),
             "qk_gain": gain.T}
    a["vec"] = np.ascontiguousarray(np.concatenate([parts[n] for n in VEC], axis=1))
    a["cst"], a["rope"], a["icnt"] = constants()
    a["c"] = x["c_2"]
    a["lam"] = x["diff_lambda_2"].reshape(1, 4 * HD)
    ups = [x["ffn_up"][0], x["ffn_w_gu_2"][0, 0], x["ffn_w_gu_2"][0, 1], x["ffn_w_gu_2"][1, 0], x["ffn_w_gu_2"][1, 1]]
    downs = [x["ffn_down"][0], x["ffn_w_down_2"][0, 0], x["ffn_w_down_2"][0, 1], x["ffn_w_down_2"][1, 0],
             x["ffn_w_down_2"][1, 1]]
    for f in range(5):
        w = ups[f].reshape(KD, P, 2, KF, P).transpose(3, 2, 1, 0, 4)
        a[f"up{f}"] = np.ascontiguousarray(w).reshape(2 * KF, P, KD * P)
        a[f"down{f}"] = units_of(downs[f], KF)
    a["pool_w"] = np.concatenate([units_of(x["pool_w_2"][g], 2) for g in range(4)])
    qkv = units_of(x["diff_w_qkv_2"], KD)
    a["w_qkv"] = np.concatenate([qkv[16:24], qkv[8:16], qkv[0:8]])
    a["w_o"] = units_of(x["diff_w_o_2"], KD)
    a["mod_w"] = x["mod_w_2"].transpose(0, 2, 1).reshape(2 * MOD_TILES, P, D)
    w = x["w_in"][0]
    a["w_in"] = units_of(np.concatenate([w[:, 0:1280], w[:, 1304:3096]], axis=1), KD)
    a["w_in24"] = w[:, 1280:1304].reshape(KD, P, 24).transpose(1, 0, 2).reshape(P, KD * 24)
    a["w_merge"] = units_of(w[:, 3096:], KD)
    a["proj_nsa"], a["proj_rwkv"] = units_of(x["proj_nsa"][0], 4), units_of(x["proj_rwkv"][0], 4)
    a["w_out"] = units_of(x["w_out"][0], KD)
    w1, w2 = np.zeros((P, 2, CMP_BLOCK, P), np.float32), np.zeros((P, 2, P), np.float32)
    pe = np.zeros((P, 2, CMP_BLOCK), np.float32)
    for g in range(2):
        rows = slice(HD * g, HD * g + HD)
        w1[rows, :, :, rows] = x["cmp_w1"][0].transpose(2, 0, 1, 3)
        w2[rows, :, rows] = x["cmp_w2"][0].transpose(1, 0, 2)
        pe[rows] = x["cmp_pe"][0].transpose(2, 0, 1)
    a["cmp_w1"], a["cmp_w2"], a["cmp_pe"] = w1, w2, pe
    a["low_up"] = np.concatenate([x["rwkv_w_up"][0], x["rwkv_a_up"][0]], axis=0)
    a["g_up"] = x["rwkv_g_up"][0]
    a.update(masks())
    return {k: np.ascontiguousarray(b) for k, b in a.items()}


def masks():
    i = np.arange(P)
    tri = np.where(i[None, :] > i[:, None], np.float32(NEG), np.float32(0))
    t = np.arange(S).reshape(TT, P).T[:, :, None]
    seen = (np.arange(NC) * CMP_STRIDE + CMP_BLOCK - 1)[None, None, :] <= t
    rmask = np.broadcast_to((np.arange(S) % CHUNK != 0).astype(np.float32), (P, S))
    s, t = i[:, None], i[None, :]
    same = s // CHUNK == t // CHUNK
    stri = np.concatenate([same & (s < t), same & (s <= t)], axis=1)
    lmask = np.stack([(s // (2 * b) == t // (2 * b)) & (s // b < t // b) for b in (1, 2, 4, 8, 16, 32)], axis=1)
    return {"tri": tri, "cadd": np.where(seen, 0, NEG).astype(np.float32), "cmul": seen.astype(np.float32),
            "rmask": rmask, "masks": np.concatenate([stri, lmask.reshape(P, 6 * P)], axis=1).astype(np.float32)}


def kernel(**inputs):
    import concourse.bacc as bacc
    from concourse.bass_utils import run_bass_kernel_spmd

    nc = bacc.Bacc("TRN2", target_bir_lowering=False, num_devices=1)
    arrays = arrays_of(inputs)
    A = {n: nc.dram_tensor(f"in_{n}", a.shape, mybir.dt.from_np(a.dtype), kind="ExternalInput").ap()
         for n, a in arrays.items()}
    out = nc.dram_tensor("out", (S, D), F32, kind="ExternalOutput").ap()
    build(nc, A, out)
    r = run_bass_kernel_spmd(nc, [{f"in_{n}": a for n, a in arrays.items()}], core_ids=[0])
    return r.results[0]["out"].reshape(1, S, D)
```
